# Optimizing a Trainium2 kernel written in Bass

```python
import math
import jax, jax.numpy as jnp
from jax import lax
import numpy as np

D_MODEL = 2048
BATCH = 1
SEQ = 256
DEPTH = 2

N_MIXERS = 2
N_SSD_LAYERS = (DEPTH + 1) // 2
N_DSA_LAYERS = DEPTH // 2
DN_ALPHA = (2.0 * DEPTH) ** 0.25
DN_BETA = (8.0 * DEPTH) ** -0.25
LN_EPS = 1e-5
RMS_EPS = 1e-6

SSD_EXPAND = 2
SSD_D_INNER = SSD_EXPAND * D_MODEL
SSD_HEAD_DIM = 64
SSD_N_HEADS = SSD_D_INNER // SSD_HEAD_DIM
SSD_N_GROUPS = 8
SSD_HEADS_PER_GROUP = SSD_N_HEADS // SSD_N_GROUPS
SSD_D_STATE = 128
SSD_D_CONV = 4
SSD_CHUNK = 256
SSD_CONV_DIM = SSD_D_INNER + 2 * SSD_N_GROUPS * SSD_D_STATE
SSD_IN_DIM = SSD_D_INNER + SSD_CONV_DIM + SSD_N_HEADS
SSD_NORM_GROUP = SSD_D_INNER // SSD_N_GROUPS

DSA_N_HEADS = 32
DSA_HEAD_DIM = 128
DSA_WIDTH = DSA_N_HEADS * DSA_HEAD_DIM
DSA_Q_RANK = 512
DSA_KV_RANK = 256
IDX_N_HEADS = 16
IDX_HEAD_DIM = 64
IDX_TOPK = 256
Q_BLOCK = 128
DSA_IN_DIM = DSA_Q_RANK + DSA_KV_RANK + IDX_HEAD_DIM + IDX_N_HEADS + DSA_WIDTH


def layer_norm(x, g, b):
    xf = x.astype(jnp.float32)
    mu = jnp.mean(xf, -1, keepdims=True)
    var = jnp.mean(jnp.square(xf - mu), -1, keepdims=True)
    return ((xf - mu) * lax.rsqrt(var + LN_EPS) * g + b).astype(x.dtype)

def rms_norm(x, g):
    xf = x.astype(jnp.float32)
    y = xf * lax.rsqrt(jnp.mean(xf * xf, -1, keepdims=True) + RMS_EPS) * g
    return y.astype(x.dtype)

def causal_depthwise_conv(u, w, b):
    k, c = w.shape
    out = lax.conv_general_dilated(u, w[:, None, :], window_strides=(1,), padding=[(k - 1, 0)],
                                   dimension_numbers=('NWC', 'WIO', 'NWC'), feature_group_count=c)
    return out + b

def segsum(a):
    cs = jnp.cumsum(a, -1)
    t = a.shape[-1]
    diff = cs[..., :, None] - cs[..., None, :]
    mask = jnp.tril(jnp.ones((t, t), dtype=bool))
    return jnp.where(mask, diff, -jnp.inf)

def ssd_chunked(xs, dt, a, bm, cm, chunk):
    b, L, g, r, p = xs.shape
    n = bm.shape[-1]
    c = L // chunk
    xdt = (xs * dt[..., None]).reshape(b, c, chunk, g, r, p)
    bc = bm.reshape(b, c, chunk, g, n)
    cc = cm.reshape(b, c, chunk, g, n)
    adt = (dt * a).reshape(b, c, chunk, g, r).transpose(0, 3, 4, 1, 2)
    a_cs = jnp.cumsum(adt, -1)
    decay = jnp.exp(segsum(adt))
    cb = jnp.einsum('bclgn,bcsgn->bgcls', cc, bc)
    y_diag = jnp.einsum('bgcls,bgrcls,bcsgrp->bclgrp', cb, decay, xdt)
    decay_states = jnp.exp(a_cs[..., -1:] - a_cs)
    states = jnp.einsum('bclgn,bgrcl,bclgrp->bcgrpn', bc, decay_states, xdt)
    states = jnp.concatenate([jnp.zeros_like(states[:, :1]), states], 1)
    chunk_a = jnp.pad(a_cs[..., -1], ((0, 0), (0, 0), (0, 0), (1, 0)))
    chunk_decay = jnp.exp(segsum(chunk_a))
    new_states = jnp.einsum('bgrzc,bcgrpn->bzgrpn', chunk_decay, states)
    prev_states = new_states[:, :-1]
    y_off = jnp.einsum('bclgn,bcgrpn,bgrcl->bclgrp', cc, prev_states, jnp.exp(a_cs))
    return (y_diag + y_off).reshape(b, L, g, r, p)

def ssd_mixer(x, w_in, conv_w, conv_b, dt_bias, a_log, d_skip, norm_g, w_out):
    b, L, _ = x.shape
    proj = x @ w_in
    z, xbc, dt = jnp.split(proj, [SSD_D_INNER, SSD_D_INNER + SSD_CONV_DIM], -1)
    xbc = jax.nn.silu(causal_depthwise_conv(xbc, conv_w, conv_b))
    xs, bm, cm = jnp.split(xbc, [SSD_D_INNER, SSD_D_INNER + SSD_N_GROUPS * SSD_D_STATE], -1)
    g, r, p = SSD_N_GROUPS, SSD_HEADS_PER_GROUP, SSD_HEAD_DIM
    xs = xs.reshape(b, L, g, r, p)
    bm = bm.reshape(b, L, g, SSD_D_STATE)
    cm = cm.reshape(b, L, g, SSD_D_STATE)
    dt = jax.nn.softplus(dt.astype(jnp.float32) + dt_bias).reshape(b, L, g, r)
    a = -jnp.exp(a_log.astype(jnp.float32)).reshape(g, r)
    chunk = math.gcd(SSD_CHUNK, L)
    y = ssd_chunked(xs, dt, a, bm, cm, chunk)
    y = y + d_skip.reshape(g, r)[..., None] * xs
    y = y.reshape(b, L, SSD_D_INNER).astype(jnp.float32)
    yg = (y * jax.nn.silu(z.astype(jnp.float32))).reshape(b, L, g, SSD_NORM_GROUP)
    yg = yg * lax.rsqrt(jnp.mean(yg * yg, -1, keepdims=True) + RMS_EPS)
    yg = yg.reshape(b, L, SSD_D_INNER) * norm_g
    return yg.astype(x.dtype) @ w_out

def dsa_mixer(x, w_in, q_norm_g, kv_norm_g, w_uq, w_uk, w_uv, w_idx_q, w_out):
    b, L, _ = x.shape
    proj = x @ w_in
    s1 = DSA_Q_RANK
    s2 = s1 + DSA_KV_RANK
    s3 = s2 + IDX_HEAD_DIM
    s4 = s3 + IDX_N_HEADS
    c_q, c_kv, k_idx, w_idx, gate = jnp.split(proj, [s1, s2, s3, s4], -1)
    c_q = rms_norm(c_q, q_norm_g)
    c_kv = rms_norm(c_kv, kv_norm_g)
    q = (c_q @ w_uq).reshape(b, L, DSA_N_HEADS, DSA_HEAD_DIM)
    q_lat = jnp.einsum('bthd,hcd->bthc', q, w_uk)
    q_idx = (c_q @ w_idx_q).reshape(b, L, IDX_N_HEADS, IDX_HEAD_DIM)
    w_idx = w_idx.astype(jnp.float32) * (IDX_N_HEADS ** -0.5)
    k_idx_f = k_idx.astype(jnp.float32)
    k_top = min(IDX_TOPK, L // 4)
    nblk = L // Q_BLOCK
    key_pos = jnp.arange(L)
    idx_scale = IDX_HEAD_DIM ** -0.5
    attn_scale = DSA_HEAD_DIM ** -0.5

    def to_blocks(t):
        return t.reshape((b, nblk, Q_BLOCK) + t.shape[2:]).swapaxes(0, 1)

    def block(args):
        qi, wi, ql, tpos = args
        s = jnp.einsum('bthd,bsd->bths', qi.astype(jnp.float32), k_idx_f)
        score = jnp.einsum('bths,bth->bts', jax.nn.relu(s), wi) * idx_scale
        causal = key_pos[None, :] <= tpos[:, None]
        score = jnp.where(causal[None], score, -jnp.inf)
        _, sel = lax.top_k(score, k_top)
        kv_sel = jax.vmap(lambda c, i: c[i])(c_kv, sel)
        logits = jnp.einsum('bthc,btkc->bthk', ql, kv_sel).astype(jnp.float32) * attn_scale
        valid = sel <= tpos[None, :, None]
        logits = jnp.where(valid[:, :, None, :], logits, -jnp.inf)
        pr = jax.nn.softmax(logits, -1).astype(kv_sel.dtype)
        return jnp.einsum('bthk,btkc->bthc', pr, kv_sel)

    pos = jnp.arange(L).reshape(nblk, Q_BLOCK)
    o_lat = lax.map(block, (to_blocks(q_idx), to_blocks(w_idx), to_blocks(q_lat), pos))
    o_lat = o_lat.swapaxes(0, 1).reshape(b, L, DSA_N_HEADS, DSA_KV_RANK)
    o = jnp.einsum('bthc,hcv->bthv', o_lat, w_uv).reshape(b, L, DSA_WIDTH)
    return (o * jax.nn.silu(gate)) @ w_out

def first_inputs(seed: int = 0) -> dict:
    key = jax.random.key(seed)
    ks = jax.random.split(key, 24)
    f32 = jnp.float32

    def nrm(k, shape, fan_in, scale=1.0):
        return jax.random.normal(k, shape, f32) * (scale * fan_in ** -0.5)

    x = jax.random.normal(ks[0], (BATCH, SEQ, D_MODEL), f32)
    ns, nd = N_SSD_LAYERS, N_DSA_LAYERS
    ssd_w_in = nrm(ks[1], (ns, D_MODEL, SSD_IN_DIM), D_MODEL)
    ssd_conv_w = nrm(ks[2], (ns, SSD_D_CONV, SSD_CONV_DIM), SSD_D_CONV)
    ssd_conv_b = 0.02 * jax.random.normal(ks[3], (ns, SSD_CONV_DIM), f32)
    u = jax.random.uniform(ks[4], (ns, SSD_N_HEADS), f32)
    dt0 = jnp.exp(u * (math.log(0.1) - math.log(0.001)) + math.log(0.001))
    ssd_dt_bias = dt0 + jnp.log(-jnp.expm1(-dt0))
    ssd_a_log = jnp.log(jax.random.uniform(ks[5], (ns, SSD_N_HEADS), f32, 1.0, 16.0))
    ssd_d_skip = 1.0 + 0.02 * jax.random.normal(ks[6], (ns, SSD_N_HEADS), f32)
    ssd_norm_g = 1.0 + 0.02 * jax.random.normal(ks[7], (ns, SSD_D_INNER), f32)
    ssd_w_out = nrm(ks[8], (ns, SSD_D_INNER, D_MODEL), SSD_D_INNER, DN_BETA)
    dsa_w_in = nrm(ks[9], (nd, D_MODEL, DSA_IN_DIM), D_MODEL)
    dsa_q_norm_g = 1.0 + 0.02 * jax.random.normal(ks[10], (nd, DSA_Q_RANK), f32)
    dsa_kv_norm_g = 1.0 + 0.02 * jax.random.normal(ks[11], (nd, DSA_KV_RANK), f32)
    dsa_w_uq = nrm(ks[12], (nd, DSA_Q_RANK, DSA_WIDTH), DSA_Q_RANK)
    dsa_w_uk = nrm(ks[13], (nd, DSA_N_HEADS, DSA_KV_RANK, DSA_HEAD_DIM), DSA_KV_RANK)
    dsa_w_uv = nrm(ks[14], (nd, DSA_N_HEADS, DSA_KV_RANK, DSA_HEAD_DIM), DSA_KV_RANK)
    dsa_w_idx_q = nrm(ks[15], (nd, DSA_Q_RANK, IDX_N_HEADS * IDX_HEAD_DIM), DSA_Q_RANK)
    dsa_w_out = nrm(ks[16], (nd, DSA_WIDTH, D_MODEL), DSA_WIDTH, DN_BETA)
    ln_g = 1.0 + 0.02 * jax.random.normal(ks[17], (DEPTH, D_MODEL), f32)
    ln_b = 0.02 * jax.random.normal(ks[18], (DEPTH, D_MODEL), f32)
    return {'x': x, 'ssd_w_in': ssd_w_in, 'ssd_conv_w': ssd_conv_w, 'ssd_conv_b': ssd_conv_b,
            'ssd_dt_bias': ssd_dt_bias, 'ssd_a_log': ssd_a_log, 'ssd_d_skip': ssd_d_skip,
            'ssd_norm_g': ssd_norm_g, 'ssd_w_out': ssd_w_out, 'dsa_w_in': dsa_w_in,
            'dsa_q_norm_g': dsa_q_norm_g, 'dsa_kv_norm_g': dsa_kv_norm_g, 'dsa_w_uq': dsa_w_uq,
            'dsa_w_uk': dsa_w_uk, 'dsa_w_uv': dsa_w_uv, 'dsa_w_idx_q': dsa_w_idx_q,
            'dsa_w_out': dsa_w_out, 'ln_g': ln_g, 'ln_b': ln_b}

def first_block(x, ssd_w_in, ssd_conv_w, ssd_conv_b, ssd_dt_bias, ssd_a_log, ssd_d_skip,
              ssd_norm_g, ssd_w_out, dsa_w_in, dsa_q_norm_g, dsa_kv_norm_g, dsa_w_uq,
              dsa_w_uk, dsa_w_uv, dsa_w_idx_q, dsa_w_out, ln_g, ln_b):
    for i in range(DEPTH):
        j = i // N_MIXERS
        if i % N_MIXERS == 0:
            h = ssd_mixer(x, ssd_w_in[j], ssd_conv_w[j], ssd_conv_b[j], ssd_dt_bias[j],
                          ssd_a_log[j], ssd_d_skip[j], ssd_norm_g[j], ssd_w_out[j])
        else:
            h = dsa_mixer(x, dsa_w_in[j], dsa_q_norm_g[j], dsa_kv_norm_g[j], dsa_w_uq[j],
                          dsa_w_uk[j], dsa_w_uv[j], dsa_w_idx_q[j], dsa_w_out[j])
        x = layer_norm(DN_ALPHA * x + h, ln_g[i], ln_b[i])
    return x


CHUNK = 128
GMLP_EXPAND = 2
GMLP_WIDTH = GMLP_EXPAND * D_MODEL
GMLP_GROUPS = 16
GMLP_GROUP_DIM = GMLP_WIDTH // GMLP_GROUPS
SB_HEAD_DIM = 128
SB_HEADS = D_MODEL // SB_HEAD_DIM
SB_WIDTH = SB_HEADS * SB_HEAD_DIM
N_A = (DEPTH + 1) // 2
N_B = DEPTH // 2
EPS = 1e-6


def rms_norm_2(x, g):
    xf = x.astype(jnp.float32)
    y = xf * lax.rsqrt(jnp.mean(xf * xf, axis=-1, keepdims=True) + EPS)
    return (y * g.astype(jnp.float32)).astype(x.dtype)

def gmlp_branch(xn, w_in, v_g, w_s, b_s, w_out):
    B, S, _ = xn.shape
    proj = xn @ w_in
    uv = jax.nn.gelu(proj[..., :2 * GMLP_WIDTH])
    zg = proj[..., 2 * GMLP_WIDTH:]
    u, v = jnp.split(uv, 2, axis=-1)
    v = rms_norm_2(v, v_g)
    vc = v.reshape(B, S // CHUNK, CHUNK, GMLP_GROUPS, GMLP_GROUP_DIM)
    causal = jnp.tril(jnp.ones((CHUNK, CHUNK), dtype=w_s.dtype))
    ws = w_s * causal[None]
    mixed = jnp.einsum('gts,bnsgc->bntgc', ws, vc) + jnp.transpose(b_s)[None, None, :, :, None]
    mixed = mixed.reshape(B, S, GMLP_WIDTH)
    y = u * mixed * jax.nn.silu(zg)
    return y @ w_out

def stick_breaking_attention(q, k, v):
    B, S, H, dh = q.shape
    nb = S // Q_BLOCK
    qh = jnp.transpose(q, (0, 2, 1, 3)) * (dh ** -0.5)
    kh = jnp.transpose(k, (0, 2, 1, 3))
    vh = jnp.transpose(v, (0, 2, 1, 3))
    qb = jnp.transpose(qh.reshape(B, H, nb, Q_BLOCK, dh), (2, 0, 1, 3, 4))
    t0 = jnp.arange(nb, dtype=jnp.int32) * Q_BLOCK
    s_idx = jnp.arange(S, dtype=jnp.int32)[None, :]

    def block(args):
        qblk, start = args
        z = jnp.einsum('bhqd,bhkd->bhqk', qblk, kh).astype(jnp.float32)
        t_idx = start + jnp.arange(Q_BLOCK, dtype=jnp.int32)[:, None]
        mask = s_idx < t_idx
        log_fail = jnp.where(mask, jax.nn.log_sigmoid(-z), 0.0)
        tail = lax.cumsum(log_fail, axis=3, reverse=True) - log_fail
        log_a = jax.nn.log_sigmoid(z) + tail
        a = jnp.where(mask, jnp.exp(log_a), 0.0)
        return jnp.einsum('bhqk,bhkd->bhqd', a.astype(vh.dtype), vh)

    ob = lax.map(block, (qb, t0))
    return jnp.transpose(ob, (1, 0, 3, 2, 4)).reshape(B, S, H, dh)

def stick_breaking_branch(xn, w_in, w_out):
    B, S, _ = xn.shape
    proj = xn @ w_in
    q, k, v, zg = jnp.split(proj, 4, axis=-1)
    shp = (B, S, SB_HEADS, SB_HEAD_DIM)
    o = stick_breaking_attention(q.reshape(shp), k.reshape(shp), v.reshape(shp))
    o = o.reshape(B, S, SB_WIDTH) * jax.nn.silu(zg)
    return o @ w_out

def second_inputs(seed: int = 0) -> dict:
    key = jax.random.key(seed)
    ks = jax.random.split(key, 12)
    f32 = jnp.float32
    x = jax.random.normal(ks[0], (BATCH, SEQ, D_MODEL), f32)
    norm_g = 1.0 + 0.02 * jax.random.normal(ks[1], (DEPTH, D_MODEL), f32)
    a_w_in = jax.random.normal(ks[2], (N_A, D_MODEL, 3 * GMLP_WIDTH), f32) * D_MODEL ** -0.5
    a_v_norm_g = 1.0 + 0.02 * jax.random.normal(ks[3], (N_A, GMLP_WIDTH), f32)
    a_w_s = jax.random.normal(ks[4], (N_A, GMLP_GROUPS, CHUNK, CHUNK), f32) * (0.5 * CHUNK ** -0.5)
    a_b_s = 1.0 + 0.1 * jax.random.normal(ks[5], (N_A, GMLP_GROUPS, CHUNK), f32)
    a_w_out = jax.random.normal(ks[6], (N_A, GMLP_WIDTH, D_MODEL), f32) * GMLP_WIDTH ** -0.5
    b_w_in = jax.random.normal(ks[7], (N_B, D_MODEL, 4 * SB_WIDTH), f32) * D_MODEL ** -0.5
    b_w_out = jax.random.normal(ks[8], (N_B, SB_WIDTH, D_MODEL), f32) * SB_WIDTH ** -0.5
    final_g = 1.0 + 0.02 * jax.random.normal(ks[9], (D_MODEL,), f32)
    return {"x": x, "norm_g": norm_g, "a_w_in": a_w_in, "a_v_norm_g": a_v_norm_g,
            "a_w_s": a_w_s, "a_b_s": a_b_s, "a_w_out": a_w_out,
            "b_w_in": b_w_in, "b_w_out": b_w_out, "final_g": final_g}

def second_block(x, norm_g, a_w_in, a_v_norm_g, a_w_s, a_b_s, a_w_out, b_w_in, b_w_out, final_g):
    h = x
    for i in range(DEPTH):
        hn = rms_norm_2(h, norm_g[i])
        j = i // N_MIXERS
        if i % N_MIXERS == 0:
            y = gmlp_branch(hn, a_w_in[j], a_v_norm_g[j], a_w_s[j], a_b_s[j], a_w_out[j])
        else:
            y = stick_breaking_branch(hn, b_w_in[j], b_w_out[j])
        h = h + y
    return rms_norm_2(h, final_g)


def setup_inputs(seed=0):
    out = dict(first_inputs(seed))
    for name, value in second_inputs(seed + 1).items():
        if name != "x":
            out[name + "_2"] = value
    return out


def reference(
    x, ssd_w_in, ssd_conv_w, ssd_conv_b, ssd_dt_bias, ssd_a_log, ssd_d_skip, ssd_norm_g,
    ssd_w_out, dsa_w_in, dsa_q_norm_g, dsa_kv_norm_g, dsa_w_uq, dsa_w_uk, dsa_w_uv, dsa_w_idx_q,
    dsa_w_out, ln_g, ln_b, norm_g_2, a_w_in_2, a_v_norm_g_2, a_w_s_2, a_b_s_2, a_w_out_2,
    b_w_in_2, b_w_out_2, final_g_2,
):
    x = first_block(
        x, ssd_w_in, ssd_conv_w, ssd_conv_b, ssd_dt_bias, ssd_a_log, ssd_d_skip, ssd_norm_g,
        ssd_w_out, dsa_w_in, dsa_q_norm_g, dsa_kv_norm_g, dsa_w_uq, dsa_w_uk, dsa_w_uv,
        dsa_w_idx_q, dsa_w_out, ln_g, ln_b,
    )
    return second_block(
        x, norm_g_2, a_w_in_2, a_v_norm_g_2, a_w_s_2, a_b_s_2, a_w_out_2, b_w_in_2, b_w_out_2,
        final_g_2,
    )


_drawn_inputs = setup_inputs


def setup_inputs(seed=0):
    import zlib

    import numpy as np

    out = dict(_drawn_inputs(seed))
    spreads = {}
    factors = {'ssd_conv_b': 4.812,
     'ssd_d_skip': 8.0,
     'ssd_norm_g': 6.341,
     'dsa_q_norm_g': 8.0,
     'dsa_kv_norm_g': 8.0,
     'norm_g_2': 3.431,
     'a_v_norm_g_2': 8.0,
     'final_g_2': 2.848}
    for name, (base, spread) in spreads.items():
        noise = np.random.default_rng([zlib.crc32(name.encode()), seed]).standard_normal(out[name].shape)
        drawn = base * np.exp(spread * noise) if base else spread * noise
        out[name] = __import__('jax').numpy.asarray(drawn.astype(out[name].dtype))
    for name, factor in factors.items():
        out[name] = (out[name] * factor).astype(out[name].dtype)
    return out
```

```python
from collections import deque
from contextlib import ExitStack

import numpy as np

import concourse.bass as bass
from concourse import mybir

F = mybir.dt.float32
R = mybir.dt.float32r
ALU = mybir.AluOpType
ACT = mybir.ActivationFunctionType
AX = mybir.AxisListType

P = 128
T = 256
DM = 2048
NR = 5
NH = 3
UW = 1024
ALPHA = 4.0 ** 0.25
LN_EPS = 1e-5
RMS_EPS = 1e-6
NEG = -1.0e30


class Line:

    def __init__(self, eng, sem):
        self.eng, self.sem, self.n, self.seen = eng, sem, 0, {}

    def wait(self, *toks):
        for t in toks:
            if t is None:
                continue
            if isinstance(t, list):
                self.wait(*t)
                continue
            sem, v = t
            if self.seen.get(sem.name, 0) < v:
                self.seen[sem.name] = v
                self.eng.wait_ge(sem, v)

    def __call__(self, fn, *toks):
        self.wait(*toks)
        fn(self.eng).then_inc(self.sem, 1)
        self.n += 1
        return (self.sem, self.n)


class DmaSem:
    def __init__(self, sem):
        self.sem, self.n = sem, 0


class Banks:

    def __init__(self, ids):
        self.free = deque((i, []) for i in ids)

    def get(self):
        return self.free.popleft()

    def put(self, i, toks):
        self.free.append((i, toks))


def build(nc, A, out):
    ctx = ExitStack()
    with ctx:
        def sb(name, shape, dt=F, c=None):
            return (c or ctx).enter_context(nc.sbuf_tensor(name, shape, dt))

        def sem(name):
            return ctx.enter_context(nc.semaphore(name))

        PE = Line(nc.tensor, sem("s_pe"))
        AC = Line(nc.scalar, sem("s_act"))
        DV = Line(nc.vector, sem("s_dve"))
        PL = Line(nc.gpsimd, sem("s_pool"))
        SP = Line(nc.sync, sem("s_sp"))

        def dma(ds, dst, src, *toks, line=None):
            ln = line or SP
            ln.wait(*toks)
            ln.eng.dma_start(dst, src).then_inc(ds.sem, 16)
            ds.n += 16
            return (ds.sem, ds.n)

        d_raw = [DmaSem(sem(f"d_raw{i}")) for i in range(NR)]
        n_ds = [0]

        def new_ds():
            n_ds[0] += 1
            return DmaSem(sem(f"d_m{n_ds[0]}"))

        G = ctx.enter_context(nc.psum_tensor("G", [P, 4, 512], F))
        M = ctx.enter_context(nc.psum_tensor("M", [P, 4, 512], F))
        mb = Banks(range(4))
        grel = [[], []]
        gpar = [0]

        RAW = sb("RAW", [P, NR, UW])
        WH = sb("WH", [P, NH, UW], R)
        WL = sb("WL", [P, NH, UW], R)
        AH = sb("AH", [P, 16, T], R)
        AL = sb("AL", [P, 16, T], R)
        ident = sb("ident", [P, P])
        ones = sb("ones", [P, P])
        triu = sb("triu", [P, 384])
        VC = sb("VC", [P, 4, P])
        dcol = sb("dcol", [P, 32])
        eps6 = sb("eps6", [P, 2])
        DB = sb("DB", [P, 64])
        alog = sb("alog", [64, 1])
        dtb = sb("dtb", [64, 1])

        units = []

        def plan(wap, r0, K, cols, width):
            nk = UW // width
            nt = K // P
            blk = []
            k = 0
            while k < nt:
                n = min(nk, nt - k)
                pieces = []
                for c0, cn, o in cols:
                    src = wap[r0 + k * P:r0 + (k + n) * P, c0:c0 + cn].rearrange(
                        "(k p) n -> p k n", p=P)
                    pieces.append((n, width, o, cn, src))
                units.append(pieces)
                blk.append((len(units) - 1, list(range(k, k + n))))
                k += n
            return blk, width

        def plan_rows(wap, row0):
            src = wap[row0:row0 + 1024, :].rearrange("(q p) n -> p q n", p=P)
            units.append([(8, 128, 0, 128, src)])
            return len(units) - 1

        fetched, ready = [0], [0]
        raw_tok, raw_free, w_tok, w_free = {}, {}, {}, {}

        def fetch_to(n):
            while fetched[0] < min(n, len(units)):
                u = fetched[0]
                s = u % NR
                for nk, width, o, cn, src in units[u]:
                    dst = RAW[:, s, 0:nk * width].rearrange("p (k n) -> p k n", k=nk)[:, :, o:o + cn]
                    raw_tok[u] = dma(d_raw[s], dst, src, raw_free.get(u - NR))
                fetched[0] += 1

        def split_to(n):
            while ready[0] < min(n, len(units)):
                u = ready[0]
                fetch_to(u + 1)
                s, r = u % NH, u % NR
                ta = AC(lambda e: e.copy(WH[:, s, :], RAW[:, r, :]), raw_tok[u], w_free.get(u - NH))
                td = DV(lambda e: e.tensor_tensor(WL[:, s, :], RAW[:, r, :], WH[:, s, :].bitcast(F),
                                                  ALU.subtract), ta, raw_tok[u], w_free.get(u - NH))
                raw_free[u] = [ta, td]
                w_tok[u] = [ta, td]
                ready[0] += 1
                fetch_to(u + NR)

        bg = deque()

        def step(n=2):
            for _ in range(n):
                if not bg:
                    return
                g = bg.popleft()
                try:
                    next(g)
                    bg.append(g)
                except StopIteration:
                    pass

        def drain():
            while bg:
                step(1)

        def mm(o, l, r, start, stop_):
            return nc.tensor.matmul(o, l, r, start=start, stop=stop_, skip_group_check=True)

        def end_unit(u, last):
            last.then_inc(PE.sem, 1)
            PE.n += 1
            w_free[u] = (PE.sem, PE.n)
            return (PE.sem, PE.n)

        def gemm(blk, a, at, token_major=False, steps=2, extra=None):
            us, width = blk
            ah, al = a
            par = gpar[0]
            gpar[0] ^= 1
            PE.wait(grel[par])
            nk = us[-1][1][-1] + 1
            for u, kts in us:
                split_to(u + NH)
                PE.wait(w_tok[u])
                wh = WH[:, u % NH, 0:len(kts) * width].rearrange("p (k n) -> p k n", k=len(kts))
                wl = WL[:, u % NH, 0:len(kts) * width].rearrange("p (k n) -> p k n", k=len(kts))
                for i, k in enumerate(kts):
                    PE.wait(at[k])
                    lastk = k == nk - 1 and extra is None
                    if token_major:
                        for t in range(2):
                            o = G[:, 2 * par + t, 0:width]
                            xh, xl = ah[:, k, t * P:(t + 1) * P], al[:, k, t * P:(t + 1) * P]
                            mm(o, xh, wh[:, i, :], k == 0, False)
                            mm(o, xh, wl[:, i, :], False, False)
                            last = mm(o, xl, wh[:, i, :], False, lastk)
                    else:
                        for f in range(width // P):
                            o = G[:, 2 * par + f // 2, (f % 2) * T:(f % 2 + 1) * T]
                            h, l = wh[:, i, f * P:(f + 1) * P], wl[:, i, f * P:(f + 1) * P]
                            mm(o, h, ah[:, k, :], k == 0 and f % 2 == 0, False)
                            mm(o, h, al[:, k, :], False, False)
                            last = mm(o, l, ah[:, k, :], False, lastk)
                tok = end_unit(u, last)
                step(steps)
            if extra is not None:
                tok = extra(par)
            g = G[:, 2 * par:2 * par + 2, :].rearrange("p a n -> p (a n)")
            return par, g, tok

        def release(par, *toks):
            grel[par] = list(toks)

        def split_act(h, l, src, *toks):
            ta = AC(lambda e: e.copy(h, src), *toks)
            td = DV(lambda e: e.tensor_tensor(l, src, h.bitcast(F), ALU.subtract), ta, *toks)
            return [ta, td]

        ssd_in = A["ssd_w_in"][0]
        B_dt = plan(ssd_in, 0, DM, [(10240, 64, 0), (10240, 64, 64)], 128)
        B_bc = [plan(ssd_in, 0, DM, [(8192 + 512 * i, 512, 0)], 512) for i in range(4)]
        B_xz = []
        for g in range(8):
            B_xz.append((plan(ssd_in, 0, DM, [(4096 + 512 * g, 512, 0)], 512),
                         plan(ssd_in, 0, DM, [(512 * g, 512, 0)], 512)))
        B_o1 = [plan(A["ssd_w_out"][0], 0, 4096, [(512 * j, 512, 0)], 512) for j in range(4)]
        din = A["dsa_w_in"][0]
        uq, uk, uv = A["dsa_w_uq"][0], A["dsa_w_uk"][0], A["dsa_w_uv"][0]
        uk = uk.rearrange("h c d -> (h c) d")
        uv = uv.rearrange("h c d -> (h c) d")

        def p_gate(j):
            return plan(din, 0, DM, [(848 + 512 * j, 512, 0)], 512)

        B_cq = plan(din, 0, DM, [(0, 512, 0)], 512)
        B_ms = plan(din, 0, DM, [(512, 320, 0), (768, 64, 320), (832, 128, 384)], 512)
        B_gate = [p_gate(0)]
        B_qi = [plan(A["dsa_w_idx_q"][0], 0, 512, [(512 * i, 512, 0)], 512) for i in range(2)]
        B_gate.append(p_gate(1))
        B_qkv = []
        for j in range(8):
            B_qkv.append((plan(uq, 0, 512, [(512 * j, 512, 0)], 512),
                          plan_rows(uk, 1024 * j), plan_rows(uv, 1024 * j)))
            if j + 2 < 8:
                B_gate.append(p_gate(j + 2))
        B_o2 = [plan(A["dsa_w_out"][0], 0, 4096, [(512 * j, 512, 0)], 512) for j in range(4)]
        ain = A["a_w_in_2"][0]
        B_v = [plan(ain, 0, DM, [(4096 + 512 * j, 512, 0)], 512) for j in range(8)]
        B_uz = [(plan(ain, 0, DM, [(512 * j, 512, 0)], 512),
                 plan(ain, 0, DM, [(8192 + 512 * j, 512, 0)], 512)) for j in range(8)]
        B_o3 = [plan(A["a_w_out_2"][0], 0, 4096, [(512 * j, 512, 0)], 512) for j in range(4)]
        bin_ = A["b_w_in_2"][0]
        B_at = [[plan(bin_, 0, DM, [(2048 * c + 512 * j, 512, 0)], 512) for c in range(4)]
                for j in range(4)]
        B_o4 = [plan(A["b_w_out_2"][0], 0, DM, [(512 * j, 512, 0)], 512) for j in range(4)]

        cs_d = nc.dram_tensor("cs_scratch", [64, T], F)
        h_d = nc.dram_tensor("h_scratch", [P, 16 * T], F)

        c0 = ExitStack()
        XS = sb("XS", [P, 2, DM], F, c0)
        VS = sb("VS", [P, 4, P], F, c0)
        x = A["x"][0]
        t_x = [dma(new_ds(), XS[:, i, :], x[i * P:(i + 1) * P, :]) for i in range(2)]

        col = {}
        d_vs = new_ds()
        pos = [0, 0]

        def rows(name, ap, n):
            done = 0
            ts = []
            while done < n:
                k = min(n - done, P - pos[1])
                ts.append(dma(d_vs, VS[pos[1]:pos[1] + k, pos[0], :], ap[done:done + k, :]))
                for i in range(k):
                    col[(name, done + i)] = (pos[0], pos[1] + i)
                done += k
                pos[1] += k
                if pos[1] == P:
                    pos[0], pos[1] = pos[0] + 1, 0
            return ts[-1]

        def as_rows(ap):
            return ap.rearrange("(n p) -> n p", p=P)

        t_vs = rows("cw", A["ssd_conv_w"][0].rearrange("j (n p) -> (j n) p", p=P), 192)
        t_vs = rows("cb", as_rows(A["ssd_conv_b"][0]), 48)
        t_vs = rows("ng", as_rows(A["ssd_norm_g"][0]), 32)
        t_vs = rows("lg", A["ln_g"].rearrange("d (n p) -> (d n) p", p=P), 32)
        t_vs = rows("lb", A["ln_b"].rearrange("d (n p) -> (d n) p", p=P), 32)
        t_vs = rows("qg", as_rows(A["dsa_q_norm_g"][0]), 4)
        t_vs = rows("kg", as_rows(A["dsa_kv_norm_g"][0]), 2)
        t_vs = rows("n2", A["norm_g_2"].rearrange("d (n p) -> (d n) p", p=P), 32)
        t_vs = rows("vg", as_rows(A["a_v_norm_g_2"][0]), 32)
        nrows = pos[0] * P + pos[1]

        def vc(name, i):
            a, b = col[(name, i)]
            return VC[:, a, b:b + 1]

        d_s = new_ds()
        dma(d_s, dtb[:, :], A["ssd_dt_bias"][0].rearrange("(h a) -> h a", a=1))
        dma(d_s, alog[:, :], A["ssd_a_log"][0].rearrange("(h a) -> h a", a=1))
        t_sm = dma(d_s, DB[:, :], A["ssd_d_skip"][0].partition_broadcast(P))
        for q in range(2):
            t_dc = DV(lambda e: e.tensor_copy(dcol[64 * q:64 * q + 64, :], DB[64 * q:64 * q + 64, q::2]), t_sm)

        ti = PL(lambda e: e.memset(ident[:, :], 0.0))
        t_id = PL(lambda e: e.affine_select(out=ident[:, :], in_=ident[:, :], compare_op=ALU.not_equal,
                                            fill=1.0, base=0, pattern=[[-1, P]], channel_multiplier=1), ti)
        t_one = PL(lambda e: e.memset(ones[:, :], 1.0))
        tr = PL(lambda e: e.memset(triu[:, :], 1.0))
        for o in (0, 256):
            t_tri = PL(lambda e: e.affine_select(out=triu[:, o:o + P], in_=triu[:, o:o + P],
                                                 compare_op=ALU.is_ge, fill=0.0, base=0,
                                                 pattern=[[1, P]], channel_multiplier=-1), tr)

        b, rel = mb.get()
        PE.wait(t_id, t_vs)
        nv = [min(P, nrows - P * i) for i in range(4) if nrows > P * i]
        for i, n in enumerate(nv):
            def tv(e, i=i, n=n):
                return e.transpose(M[:, b, i * P:i * P + n], VS[0:n, i, :], ident[0:n, 0:n])
            tp = PE(tv)
        for i, n in enumerate(nv):
            t_vc = DV(lambda e: e.tensor_copy(VC[:, i, 0:n], M[:, b, i * P:i * P + n]), tp)
        mb.put(b, [t_vc])

        xt = {}
        for k in range(0, 16, 2):
            b, rel = mb.get()
            PE.wait(t_x, t_id, rel)
            for i in range(2):
                for t in range(2):
                    last = nc.tensor.transpose(M[:, b, (2 * i + t) * P:(2 * i + t + 1) * P],
                                               XS[:, t, (k + i) * P:(k + i + 1) * P], ident[:, :])
            last.then_inc(PE.sem, 1)
            PE.n += 1
            toks = split_act(AH[:, k:k + 2, :].rearrange("p a n -> p (a n)"),
                             AL[:, k:k + 2, :].rearrange("p a n -> p (a n)"), M[:, b, :],
                             (PE.sem, PE.n))
            xt[k] = xt[k + 1] = toks
            mb.put(b, toks)
        last_x = [(PE.sem, PE.n)]
        c0.close()

        def brc(ap, n):
            return ap.unsqueeze(1).to_broadcast([P, n, ap.shape[1]])

        cy = ExitStack()
        YH = sb("YH", [P, 32, T], R, cy)
        YL = sb("YL", [P, 32, T], R, cy)
        c1 = ExitStack()
        BT = sb("BT", [P, 8, T], F, c1)
        CT = sb("CT", [P, 8, T], F, c1)
        XG = sb("XG", [P, 4, T], F, c1)
        CSB = sb("CSB", [P, 8, T], F, c1)
        E2 = sb("E2", [P, 8, 384], F, c1)
        XD = sb("XD", [P, 2, 512], F, c1)
        YT = sb("YT", [P, 4, T], F, c1)
        SZ = sb("SZ", [P, 4, T], F, c1)
        CB = sb("CB", [P, 384], F, c1)
        RI = sb("RI", [P, T], F, c1)
        dtT = sb("dtT", [P, 2, 64], F, c1)
        csT = sb("csT", [P, 2, 64], F, c1)

        A1 = (AH, AL)
        par, g, tok = gemm(B_dt, A1, xt)
        xb, ab, sp_, ad, cs_ = (YT[0:64, i, :] for i in (0, 1, 2, 3, 1))
        dtv = SZ[0:64, 0, :]
        nea = SZ[0:64, 1, 0:1]
        t1 = DV(lambda e: e.tensor_scalar(xb, g[0:64, 0:T], dtb[:, 0:1], None, ALU.add), tok, t_sm, last_x)
        release(par, t1)
        t2 = DV(lambda e: e.scalar_tensor_tensor(out=ab, in0=xb, scalar=-1.0, in1=xb, op0=ALU.mult, op1=ALU.max), t1)
        t3 = AC(lambda e: e.activation(nea, alog[:, :], ACT.Exp), t_sm, last_x)
        t4 = AC(lambda e: e.activation(ab, ab, ACT.Exp, scale=-1.0), t2)
        t5 = AC(lambda e: e.activation(sp_, ab, ACT.Ln, bias=1.0), t4)
        t6 = DV(lambda e: e.scalar_tensor_tensor(out=dtv, in0=xb, scalar=0.0, in1=sp_, op0=ALU.max,
                                                 op1=ALU.add), t5)
        t7 = DV(lambda e: e.tensor_scalar(ad, dtv, nea, -1.0, ALU.mult, ALU.mult), t6, t3)
        t7b = DV(lambda e: e.memset(xb, 1.0), t6)
        t8 = DV(lambda e: e.tensor_tensor_scan(cs_, xb, ad, 0.0, ALU.mult, ALU.add), t7, t7b, t5)
        t_csd = dma(new_ds(), cs_d[:, :], cs_, t8)
        b, rel = mb.get()
        PE.wait(rel, t8, t6)
        for t in range(2):
            nc.tensor.transpose(M[:, b, t * P:t * P + 64], dtv[:, t * P:(t + 1) * P], ident[0:64, 0:64])
            last = nc.tensor.transpose(M[:, b, 256 + t * P:256 + t * P + 64], cs_[:, t * P:(t + 1) * P],
                                       ident[0:64, 0:64])
        last.then_inc(PE.sem, 1)
        PE.n += 1
        tp = (PE.sem, PE.n)
        m = M[:, b, :].rearrange("p (a t n) -> p a t n", a=2, t=2)
        t9 = DV(lambda e: e.tensor_copy(dtT[:, :, :], m[:, 0, :, 0:64]), tp)
        t_csT = DV(lambda e: e.tensor_scalar(csT[:, :, :], m[:, 1, :, 0:64], -1.0, None, ALU.mult), tp)
        mb.put(b, [t_csT])

        def conv(g, tok, ch, dst, free):
            ts = []
            for f in range(4):
                u = g[:, f * T:(f + 1) * T]
                ts.append(DV(lambda e: e.tensor_scalar(dst[:, f, :], u, vc("cw", 3 * 48 + ch + f),
                                                       vc("cb", ch + f), ALU.mult, ALU.add),
                             tok, t_vc, free))
            for j in (2, 1, 0):
                s = 3 - j
                for f in range(4):
                    u = g[:, f * T:(f + 1) * T]
                    ts[f] = DV(lambda e: e.scalar_tensor_tensor(
                        out=dst[:, f, s:T], in0=u[:, 0:T - s], scalar=vc("cw", j * 48 + ch + f),
                        in1=dst[:, f, s:T], op0=ALU.mult, op1=ALU.add), ts[f])
            d = dst.rearrange("p a n -> p (a n)")
            return ts[-1], AC(lambda e: e.activation(d, d, ACT.Silu), ts)

        bct = [None] * 4
        for i in range(4):
            par, g, tok = gemm(B_bc[i], A1, xt)
            dst = (BT, CT)[i // 2][:, 4 * (i % 2):4 * (i % 2) + 4, :]
            tc, ta = conv(g, tok, 32 + 4 * i, dst, last_x)
            release(par, tc)
            bct[i] = ta

        yt = {}
        d_csb = new_ds()
        state = {"csb": None, "xg": None, "e": None, "xd": None, "yt": None, "yt_free": [], "xg_free": []}

        def decay(g, h0, tcs):
            for h in range(h0, h0 + 4):
                hh = 8 * g + h
                DV(lambda e: e.tensor_scalar(E2[:, h, 0:256], CSB[:, h, :], csT[:, 0, hh:hh + 1], 0.0,
                                             ALU.add, ALU.min), tcs, t_csT, state["e"])
                td = DV(lambda e: e.tensor_scalar(E2[:, h, 256:384], CSB[:, h, P:T], csT[:, 1, hh:hh + 1],
                                                  0.0, ALU.add, ALU.min))
            state["csb"] = td
            ev = E2[:, h0:h0 + 4, :].rearrange("p h n -> p (h n)")
            return AC(lambda e: e.activation(ev, ev, ACT.Exp), td)

        def ssd(g, t_xg):
            tcs = dma(d_csb, CSB[:, :, :], cs_d[8 * g:8 * g + 8, :].rearrange("h t -> (h t)")
                      .partition_broadcast(P), t_csd, state["csb"])
            b, rel = mb.get()
            PE.wait(rel, bct)
            mm(M[:, b, 0:256], BT[:, g, 0:P], CT[:, g, :], True, True)
            tp = PE(lambda e: mm(M[:, b, 256:384], BT[:, g, P:T], CT[:, g, P:T], False, True))
            tcb = DV(lambda e: e.tensor_tensor(CB[:, :], M[:, b, 0:384], triu[:, :], ALU.mult),
                     tp, t_tri, state["e"])
            mb.put(b, [tcb])
            te = decay(g, 0, tcs)
            yield
            txd = []
            for t in range(2):
                b, rel = mb.get()
                PE.wait(rel, t_xg)
                for f in range(4):
                    last = nc.tensor.transpose(M[:, b, f * P:(f + 1) * P], XG[:, f, t * P:(t + 1) * P],
                                               ident[:, :])
                last.then_inc(PE.sem, 1)
                PE.n += 1
                bd = dtT[:, t, 8 * g:8 * g + 8].unsqueeze(2).to_broadcast([P, 8, 64])
                txd.append(DV(lambda e: e.tensor_tensor(
                    XD[:, t, :].rearrange("p (h d) -> p h d", h=8),
                    M[:, b, :].rearrange("p (h d) -> p h d", h=8), bd, ALU.mult),
                    (PE.sem, PE.n), state["xd"]))
                mb.put(b, [txd[-1]])
            cbb = CB[:, :].unsqueeze(1).to_broadcast([P, 4, 384])
            tm = [DV(lambda e: e.tensor_tensor(E2[:, 0:4, :], E2[:, 0:4, :], cbb, ALU.mult), te, tcb)]
            yield
            te = decay(g, 4, tcs)
            yield
            tm.append(DV(lambda e: e.tensor_tensor(E2[:, 4:8, :], E2[:, 4:8, :], cbb, ALU.mult), te, tcb))
            yield
            ty = []
            for q in range(4):
                b, rel = mb.get()
                PE.wait(rel, tm[q // 2], txd)
                for r in range(2):
                    h = 2 * q + r
                    o = M[64 * r:64 * r + 64, b, :]
                    mm(o[:, 0:256], XD[:, 0, 64 * h:64 * h + 64], E2[:, h, 0:256], True, False)
                    last = mm(o[:, 128:256], XD[:, 1, 64 * h:64 * h + 64], E2[:, h, 256:384], False, True)
                last.then_inc(PE.sem, 1)
                PE.n += 1
                tp = (PE.sem, PE.n)
                yield
                ty.append(DV(lambda e: e.scalar_tensor_tensor(
                    out=YT[:, q, :], in0=XG[:, q, :], scalar=dcol[:, 4 * g + q:4 * g + q + 1],
                    in1=M[:, b, 0:T], op0=ALU.mult, op1=ALU.add), tp, t_xg, t_dc, state["yt_free"]))
                mb.put(b, [ty[-1]])
            state["e"] = tp
            state["xd"] = tp
            state["xg_free"] = [ty[-1], tp]
            state["yt"] = ty

        def gate_z(g, tz, ty):
            sz = SZ[:, :, :].rearrange("p a n -> p (a n)")
            yv = YT[:, :, :].rearrange("p a n -> p (a n)")
            t1 = DV(lambda e: e.tensor_tensor(yv, yv, sz, ALU.mult), tz, ty)
            t2 = AC(lambda e: e.activation(sz, yv, ACT.Square), t1)
            yield
            b, rel = mb.get()
            PE.wait(rel, t2, t_one)
            for f in range(4):
                last = mm(M[:, b, 0:T], ones[:, :], SZ[:, f, :], f == 0, f == 3)
            last.then_inc(PE.sem, 1)
            PE.n += 1
            t3 = AC(lambda e: e.activation(RI[:, :], M[:, b, 0:T], ACT.Sqrt, scale=1.0 / 512, bias=eps6[:, 0:1]),
                    (PE.sem, PE.n), t_eps, state.get("ri"))
            mb.put(b, [t3])
            yield
            t4 = DV(lambda e: e.reciprocal(RI[:, :], RI[:, :]), t3)
            for f in range(4):
                t5 = DV(lambda e: e.scalar_tensor_tensor(out=SZ[:, f, :], in0=YT[:, f, :],
                                                         scalar=vc("ng", 4 * g + f), in1=RI[:, :],
                                                         op0=ALU.mult, op1=ALU.mult),
                        t4, (PE.sem, PE.n), t1)
            state["yt_free"] = [t5]
            state["ri"] = t5
            yield
            toks = split_act(YH[:, 4 * g:4 * g + 4, :].rearrange("p a n -> p (a n)"),
                             YL[:, 4 * g:4 * g + 4, :].rearrange("p a n -> p (a n)"), sz, t5)
            state["sz_free"] = toks
            for f in range(4):
                yt[4 * g + f] = toks

        te1 = PL(lambda e: e.memset(eps6[:, 0:1], RMS_EPS))
        t_eps = PL(lambda e: e.memset(eps6[:, 1:2], LN_EPS))

        for gi in range(8):
            par, g, tok = gemm(B_xz[gi][0], A1, xt)
            drain()
            tc, ta = conv(g, tok, 4 * gi, XG[:, :, :], state["xg_free"])
            release(par, tc)
            bg.append(ssd(gi, ta))
            par, g, tok = gemm(B_xz[gi][1], A1, xt)
            drain()
            tz = AC(lambda e: e.activation(SZ[:, :, :].rearrange("p a n -> p (a n)"), g, ACT.Silu),
                    tok, state.get("sz_free"), t9, t7, t_csd)
            release(par, tz)
            bg.append(gate_z(gi, tz, state["yt"]))

        def ln_tail(blocks, yt, RES, cn, li):
            PV = sb(f"PV{li}", [P, T], F, cn)
            SQ = sb(f"SQ{li}", [P, 4, T], F, cn)
            MU = sb(f"MU{li}", [P, T], F, cn)
            RS = sb(f"RS{li}", [P, T], F, cn)
            b1, b2 = None, None
            sq_free = None
            for j in range(4):
                par, g, tok = gemm(blocks[j], (YH, YL), yt)
                r = RES[:, 4 * j:4 * j + 4, :].rearrange("p a n -> p (a n)")
                xh = AH[:, 4 * j:4 * j + 4, :].rearrange("p a n -> p (a n)").bitcast(F)
                xl = AL[:, 4 * j:4 * j + 4, :].rearrange("p a n -> p (a n)").bitcast(F)
                t1 = DV(lambda e: e.scalar_tensor_tensor(out=r, in0=xh, scalar=ALPHA, in1=g, op0=ALU.mult,
                                                         op1=ALU.add), tok)
                release(par, t1)
                t1 = DV(lambda e: e.scalar_tensor_tensor(out=r, in0=xl, scalar=ALPHA, in1=r, op0=ALU.mult,
                                                         op1=ALU.add), t1)
                if j == 0:
                    b, rel = mb.get()
                    PE.wait(rel, t1)
                    for f in range(4):
                        last = mm(M[:, b, 0:T], ones[:, :], RES[:, f, :], f == 0, f == 3)
                    last.then_inc(PE.sem, 1)
                    PE.n += 1
                    tpv = AC(lambda e: e.activation(PV[:, :], M[:, b, 0:T], ACT.Copy, scale=1.0 / 512),
                             (PE.sem, PE.n))
                    mb.put(b, [tpv])
                r3 = RES[:, 4 * j:4 * j + 4, :]
                t2 = DV(lambda e: e.tensor_tensor(r3, r3, brc(PV[:, :], 4), ALU.subtract), t1, tpv)
                t3 = AC(lambda e: e.activation(SQ[:, :, :].rearrange("p a n -> p (a n)"), r, ACT.Square),
                        t2, sq_free)
                if j == 0:
                    (b1, rel1), (b2, rel2) = mb.get(), mb.get()
                    PE.wait(rel1, rel2)
                PE.wait(t2)
                for f in range(4):
                    mm(M[:, b1, 0:T], ones[:, :], RES[:, 4 * j + f, :], j == 0 and f == 0, j == 3 and f == 3)
                PE.wait(t3)
                for f in range(4):
                    last = mm(M[:, b2, 0:T], ones[:, :], SQ[:, f, :], j == 0 and f == 0, j == 3 and f == 3)
                last.then_inc(PE.sem, 1)
                PE.n += 1
                sq_free = (PE.sem, PE.n)
            tp = sq_free
            t1 = DV(lambda e: e.tensor_scalar(MU[:, :], M[:, b1, 0:T], 1.0 / DM, None, ALU.mult), tp)
            t2 = DV(lambda e: e.tensor_tensor(PV[:, :], MU[:, :], MU[:, :], ALU.mult), t1)
            t3 = DV(lambda e: e.scalar_tensor_tensor(out=RS[:, :], in0=M[:, b2, 0:T], scalar=1.0 / DM,
                                                     in1=PV[:, :], op0=ALU.mult, op1=ALU.subtract), t2)
            mb.put(b1, [t1])
            mb.put(b2, [t3])
            t4 = AC(lambda e: e.activation(RS[:, :], RS[:, :], ACT.Sqrt, bias=eps6[:, 1:2]), t3, t_eps)
            t5 = DV(lambda e: e.reciprocal(RS[:, :], RS[:, :]), t4)
            res = {}
            for j in range(4):
                r3 = RES[:, 4 * j:4 * j + 4, :]
                t6 = DV(lambda e: e.tensor_tensor(r3, r3, brc(MU[:, :], 4), ALU.subtract), t1)
                t7 = DV(lambda e: e.tensor_tensor(r3, r3, brc(RS[:, :], 4), ALU.mult), t6, t5)
                for f in range(4):
                    k = 4 * j + f
                    res[k] = AC(lambda e: e.activation(RES[:, k, :], RES[:, k, :], ACT.Identity,
                                                       scale=vc("lg", 16 * li + k), bias=vc("lb", 16 * li + k)), t7)
            return res

        def rms_to_a(RES, rt, SQ, RS, gname, g0, sq_free=None):
            b, rel = mb.get()
            PE.wait(rel)
            for j in range(4):
                t1 = AC(lambda e: e.activation(SQ[:, :, :].rearrange("p a n -> p (a n)"),
                                               RES[:, 4 * j:4 * j + 4, :].rearrange("p a n -> p (a n)"),
                                               ACT.Square), [rt[4 * j + f] for f in range(4)], sq_free)
                PE.wait(t1)
                for f in range(4):
                    last = mm(M[:, b, 0:T], ones[:, :], SQ[:, f, :], j == 0 and f == 0, j == 3 and f == 3)
                last.then_inc(PE.sem, 1)
                PE.n += 1
                sq_free = (PE.sem, PE.n)
            t2 = AC(lambda e: e.activation(RS[:, :], M[:, b, 0:T], ACT.Sqrt, scale=1.0 / DM, bias=eps6[:, 0:1]),
                    sq_free)
            mb.put(b, [t2])
            t3 = DV(lambda e: e.reciprocal(RS[:, :], RS[:, :]), t2)
            at = {}
            for j in range(4):
                for f in range(4):
                    k = 4 * j + f
                    t4 = DV(lambda e: e.scalar_tensor_tensor(
                        out=SQ[:, f, :], in0=RES[:, k, :], scalar=vc(gname, g0 + k), in1=RS[:, :],
                        op0=ALU.mult, op1=ALU.mult), t3, sq_free, at.get(k - 4))
                toks = split_act(AH[:, 4 * j:4 * j + 4, :].rearrange("p a n -> p (a n)"),
                                 AL[:, 4 * j:4 * j + 4, :].rearrange("p a n -> p (a n)"),
                                 SQ[:, :, :].rearrange("p a n -> p (a n)"), t4)
                for f in range(4):
                    at[4 * j + f] = toks
            return at

        def ln_to_a(RES, rt):
            at = {}
            for j in range(4):
                toks = split_act(AH[:, 4 * j:4 * j + 4, :].rearrange("p a n -> p (a n)"),
                                 AL[:, 4 * j:4 * j + 4, :].rearrange("p a n -> p (a n)"),
                                 RES[:, 4 * j:4 * j + 4, :].rearrange("p a n -> p (a n)"),
                                 [rt[4 * j + f] for f in range(4)])
                for f in range(4):
                    at[4 * j + f] = toks
            return at

        def fence():
            return [(PE.sem, PE.n), (AC.sem, AC.n), (DV.sem, DV.n)]

        drain()
        c1.close()
        c2 = ExitStack()
        RES = sb("RES2", [P, 16, T], F, c2)
        f2 = fence()
        for l in (AC, DV, PE):
            l.wait(f2)
        rt = ln_tail(B_o1, yt, RES, c2, 0)
        at = ln_to_a(RES, rt)
        f3 = fence()
        c2.close()

        c3 = ExitStack()
        QK = sb("QK", [P, 2, 4, T], F, c3)
        VV = sb("VV", [P, 2, 512], F, c3)
        SG = sb("SG", [P, 3, 4, T], F, c3)
        OT = sb("OT", [P, 4, T], F, c3)
        CQH = sb("CQH", [P, 4, T], R, c3)
        CQL = sb("CQL", [P, 4, T], R, c3)
        CKH = sb("CKH", [P, 2, T], R, c3)
        CKL = sb("CKL", [P, 2, T], R, c3)
        KI = sb("KI", [P, T], F, c3)
        WT = sb("WT", [P, 2, 16], F, c3)
        SC = sb("SC", [P, 384], F, c3)
        MA = sb("MA", [P, 384], F, c3)
        TRL = sb("TRL", [P, 384], F, c3)
        PX = sb("PX", [P, 384], F, c3)
        PT = sb("PT", [P, 384], F, c3)
        M8 = sb("M8", [P, 8], F, c3)
        MX = sb("MX", [P, 8], F, c3)
        RQ = sb("RQ", [P, T], F, c3)
        A3 = (AH, AL)
        tl = PL(lambda e: e.memset(TRL[:, :], 1.0), f3)
        for o in (0, 256):
            t_trl = PL(lambda e: e.affine_select(out=TRL[:, o:o + P], in_=TRL[:, o:o + P],
                                                 compare_op=ALU.is_ge, fill=0.0, base=0,
                                                 pattern=[[-1, P]], channel_multiplier=1), tl)

        def small_rms(src, n, tsrc, tmp, gname, H, L, ttmp):
            s2 = src.rearrange("p a n -> p (a n)")
            tm = tmp.rearrange("p a n -> p (a n)")
            t1 = AC(lambda e: e.activation(tm, s2, ACT.Square), tsrc, ttmp)
            b, rel = mb.get()
            PE.wait(rel, t1)
            for f in range(n):
                last = mm(M[:, b, 0:T], ones[:, :], tmp[:, f, :], f == 0, f == n - 1)
            last.then_inc(PE.sem, 1)
            PE.n += 1
            t2 = AC(lambda e: e.activation(RQ[:, :], M[:, b, 0:T], ACT.Sqrt, scale=1.0 / (n * P),
                                           bias=eps6[:, 0:1]), (PE.sem, PE.n), state.get("rq"))
            mb.put(b, [t2])
            t3 = DV(lambda e: e.reciprocal(RQ[:, :], RQ[:, :]), t2)
            for f in range(n):
                t4 = DV(lambda e: e.scalar_tensor_tensor(out=src[:, f, :], in0=src[:, f, :],
                                                         scalar=vc(gname, f), in1=RQ[:, :],
                                                         op0=ALU.mult, op1=ALU.mult), t3, tsrc)
            state["rq"] = t4
            return split_act(H[:, :, :].rearrange("p a n -> p (a n)"),
                             L[:, :, :].rearrange("p a n -> p (a n)"), s2, t4)

        par, g, tok = gemm(B_cq, A3, at)
        qv = QK[:, 0].rearrange("p a n -> p (a n)")
        t1 = DV(lambda e: e.tensor_copy(qv, g), tok, f3)
        release(par, t1)
        par, g, tok = gemm(B_ms, A3, at)
        cqt = small_rms(QK[:, 0], 4, t1, QK[:, 1], "qg", CQH, CQL, f3)
        t2 = DV(lambda e: e.tensor_copy(OT[:, 0:2, :].rearrange("p a n -> p (a n)"), g[:, 0:512]), tok, f3)
        t_ki = DV(lambda e: e.tensor_copy(KI[:, :], g[:, 512:768]), tok)
        t_w = DV(lambda e: e.tensor_copy(VV[0:16, 0, 0:T], g[0:16, 768:1024]), tok)
        release(par, t_w)
        par, g, tok = gemm(B_gate[0], A3, at)
        ckt = small_rms(OT[:, 0:2, :], 2, t2, OT[:, 2:4, :], "kg", CKH, CKL, f3)
        b, rel = mb.get()
        PE.wait(rel, t_w)
        for t in range(2):
            last = nc.tensor.transpose(M[:, b, 16 * t:16 * t + 16], VV[0:16, 0, t * P:(t + 1) * P],
                                       ident[0:16, 0:16])
        last.then_inc(PE.sem, 1)
        PE.n += 1
        t_wt = DV(lambda e: e.tensor_scalar(WT[:, :, :].rearrange("p a n -> p (a n)"), M[:, b, 0:32],
                                            0.25, 0.125, ALU.mult, ALU.mult), (PE.sem, PE.n), f3)
        mb.put(b, [t_wt])

        sg_tok, sg_free = {}, {}

        def put_gate(j, par, g, tok):
            sg_tok[j] = AC(lambda e: e.activation(SG[:, j % 3].rearrange("p a n -> p (a n)"), g, ACT.Silu),
                           tok, sg_free.get(j - 3), f3)
            release(par, sg_tok[j])

        put_gate(0, par, g, tok)
        qit = []
        cq_at = {k: cqt for k in range(4)}
        for i in range(2):
            par, g, tok = gemm(B_qi[i], (CQH, CQL), cq_at)
            ti = DV(lambda e: e.tensor_copy(QK[:, i].rearrange("p a n -> p (a n)"), g), tok, cqt)
            release(par, ti)
            qit.append(ti)
        mask_done = {}

        def index_scores():
            acc = [None, None]
            RL = PT
            rl_free = None
            for h in range(16):
                f, o = h // 2, 64 * (h % 2)
                b, rel = mb.get()
                PE.wait(rel, qit, t_ki)
                qh = QK[o:o + 64, f // 4, f % 4, :]
                mm(M[:, b, 0:P], qh[:, 0:P], KI[o:o + 64, 0:P], True, True)
                tp = PE(lambda e: mm(M[:, b, P:P + T], qh[:, P:T], KI[o:o + 64, :], False, True))
                yield
                ta = AC(lambda e: e.activation(RL[:, :], M[:, b, 0:384], ACT.Relu), tp, rl_free)
                mb.put(b, [ta])
                for t, (a, z) in enumerate(((0, P), (P, 384))):
                    w = WT[:, t, h:h + 1]
                    if h == 0:
                        acc[t] = DV(lambda e: e.tensor_scalar(SC[:, a:z], RL[:, a:z], w, None, ALU.mult),
                                    ta, t_wt, f3)
                    else:
                        acc[t] = DV(lambda e: e.scalar_tensor_tensor(
                            out=SC[:, a:z], in0=RL[:, a:z], scalar=w, in1=SC[:, a:z], op0=ALU.mult,
                            op1=ALU.add), ta, acc[t])
                rl_free = acc[1]
                yield
            t1 = DV(lambda e: e.tensor_scalar(MA[:, :], TRL[:, :], -NEG * 1e8, NEG * 1e8, ALU.mult, ALU.add),
                    t_trl, f3)
            t2 = DV(lambda e: e.tensor_tensor(SC[:, :], SC[:, :], TRL[:, :], ALU.mult), acc)
            t3 = DV(lambda e: e.tensor_tensor(SC[:, :], SC[:, :], MA[:, :], ALU.add), t2, t1)
            yield
            tr = t3
            for a, z in ((0, P), (P, 384)):
                for i in range(8):
                    tm = DV(lambda e: e.max(M8[:, :], SC[:, a:z]), tr)
                    tr = DV(lambda e: e.match_replace(SC[:, a:z], M8[:, :], SC[:, a:z], -3.0e38), tm)
                    yield
            t4 = DV(lambda e: e.tensor_scalar(SC[:, :], SC[:, :], -2.0e38, None, ALU.is_lt), tr)
            t5 = DV(lambda e: e.tensor_tensor(SC[:, :], SC[:, :], TRL[:, :], ALU.mult), t4)
            mask_done["t"] = DV(lambda e: e.tensor_scalar(MA[:, :], SC[:, :], -NEG, NEG, ALU.mult, ALU.add), t5)
            mask_done["rl"] = rl_free

        bg.append(index_scores())
        par, g, tok = gemm(B_gate[1], A3, at, steps=4)
        put_gate(1, par, g, tok)
        yt = {}
        st = {"px": None, "pt": None, "qkv": None, "ot": None, "mx": None}
        SCALE = 128.0 ** -0.5

        def attend(j, tq, tk, tv):
            tm = mask_done["t"]
            ot = []
            for h in range(4):
                b, rel = mb.get()
                PE.wait(rel, tq, tk)
                q, k = QK[:, 0, h, :], QK[:, 1, h, :]
                mm(M[:, b, 0:P], q[:, 0:P], k[:, 0:P], True, True)
                tp = PE(lambda e: mm(M[:, b, P:384], q[:, P:T], k[:, :], False, True))
                yield
                spans = ((0, P), (P, 384))
                tmx = []
                for t, (a, z) in enumerate(spans):
                    tmx.append(DV(lambda e: e.tensor_tensor_reduce(
                        out=PX[:, a:z], in0=M[:, b, a:z], in1=MA[:, a:z], scale=SCALE, scalar=-3.0e38,
                        op0=ALU.add, op1=ALU.max, accum_out=MX[:, t:t + 1]), tp, tm, st["px"], st["mx"]))
                mb.put(b, [tmx[-1]])
                tn = DV(lambda e: e.tensor_scalar(MX[:, 2:4], MX[:, 0:2], -1.0, None, ALU.mult), tmx)
                te = []
                for t, (a, z) in enumerate(spans):
                    te.append(AC(lambda e: e.activation(PX[:, a:z], PX[:, a:z], ACT.Exp, bias=MX[:, 2 + t:3 + t],
                                                        accum_out=MX[:, 4 + t:5 + t]), tn))
                yield
                tr = DV(lambda e: e.reciprocal(MX[:, 6:8], MX[:, 4:6]), te)
                for t, (a, z) in enumerate(spans):
                    ts = DV(lambda e: e.tensor_scalar(PX[:, a:z], PX[:, a:z], MX[:, 6 + t:7 + t], None,
                                                      ALU.mult), tr)
                st["mx"] = ts
                yield
                b, rel = mb.get()
                PE.wait(rel, ts)
                nc.tensor.transpose(M[:, b, 0:P], PX[:, 0:P], ident[:, :])
                nc.tensor.transpose(M[:, b, P:T], PX[:, P:T], ident[:, :])
                tp = PE(lambda e: e.transpose(M[:, b, T:384], PX[:, T:384], ident[:, :]))
                st["px"] = tp
                tc = AC(lambda e: e.copy(PT[:, :], M[:, b, 0:384]), tp, st["pt"], mask_done["rl"])
                mb.put(b, [tc])
                yield
                b, rel = mb.get()
                PE.wait(rel, tc, tv)
                mm(M[:, b, 0:T], VV[:, 0, h * P:(h + 1) * P], PT[:, 0:T], True, False)
                tp = PE(lambda e: mm(M[:, b, P:T], VV[:, 1, h * P:(h + 1) * P], PT[:, T:384], False, True))
                st["pt"] = tp
                st["qkv"] = tp
                yield
                ot.append(DV(lambda e: e.tensor_tensor(OT[:, h, :], M[:, b, 0:T], SG[:, j % 3, h, :],
                                                       ALU.mult), tp, sg_tok[j], st["ot"]))
                mb.put(b, [ot[-1]])
            sg_free[j] = ot[-1]
            toks = split_act(YH[:, 4 * j:4 * j + 4, :].rearrange("p a n -> p (a n)"),
                             YL[:, 4 * j:4 * j + 4, :].rearrange("p a n -> p (a n)"),
                             OT[:, :, :].rearrange("p a n -> p (a n)"), ot)
            st["ot"] = toks
            for f in range(4):
                yt[4 * j + f] = toks

        def kv_gemm(u, values):
            par = gpar[0]
            gpar[0] ^= 1
            PE.wait(grel[par])
            split_to(u + NH)
            PE.wait(w_tok[u], ckt)
            wh = WH[:, u % NH, :].rearrange("p (h c n) -> p h c n", h=4, c=2)
            wl = WL[:, u % NH, :].rearrange("p (h c n) -> p h c n", h=4, c=2)
            if values:
                for t in range(2):
                    o = G[:, 2 * par + t, :]
                    for c in range(2):
                        xh, xl = CKH[:, c, t * P:(t + 1) * P], CKL[:, c, t * P:(t + 1) * P]
                        mm(o, xh, wh[:, :, c, :], c == 0, False)
                        mm(o, xh, wl[:, :, c, :], False, False)
                        last = mm(o, xl, wh[:, :, c, :], False, c == 1)
            else:
                for h in range(4):
                    o = G[:, 2 * par + h // 2, (h % 2) * T:(h % 2 + 1) * T]
                    for c in range(2):
                        mm(o, wh[:, h, c, :], CKH[:, c, :], c == 0 and h % 2 == 0, False)
                        mm(o, wh[:, h, c, :], CKL[:, c, :], False, False)
                        last = mm(o, wl[:, h, c, :], CKH[:, c, :], False, c == 1)
            tok = end_unit(u, last)
            step(2)
            return par, G[:, 2 * par:2 * par + 2, :].rearrange("p a n -> p (a n)"), tok

        for j in range(8):
            parq, gq, tokq = gemm(B_qkv[j][0], (CQH, CQL), cq_at)
            if j > 0:
                drain()
            if j == 0:
                drain()
            tq = DV(lambda e: e.tensor_copy(QK[:, 0].rearrange("p a n -> p (a n)"), gq), tokq, st["qkv"],
                    (PE.sem, PE.n))
            release(parq, tq)
            par, g, tok = kv_gemm(B_qkv[j][1], False)
            tk = AC(lambda e: e.copy(QK[:, 1].rearrange("p a n -> p (a n)"), g), tok, st["qkv"], tq)
            release(par, tk)
            par, g, tok = kv_gemm(B_qkv[j][2], True)
            tv = DV(lambda e: e.tensor_copy(VV[:, :, :].rearrange("p a n -> p (a n)"), g), tok, st["qkv"])
            release(par, tv)
            bg.append(attend(j, tq, tk, tv))
            if j + 2 < 8:
                par, g, tok = gemm(B_gate[j + 2], A3, at, steps=3)
                put_gate(j + 2, par, g, tok)
        drain()
        f4 = fence()
        c3.close()

        c4 = ExitStack()
        RES = sb("RES4", [P, 16, T], F, c4)
        for l in (AC, DV, PE):
            l.wait(f4)
        rt = ln_tail(B_o2, yt, RES, c4, 1)
        SQ4 = sb("SQ4", [P, 4, T], F, c4)
        RS4 = sb("RS4", [P, T], F, c4)
        d_h = new_ds()
        for k in range(4):
            t_hd = dma(d_h, h_d[:, 4 * k * T:4 * (k + 1) * T],
                       RES[:, 4 * k:4 * k + 4, :].rearrange("p a n -> p (a n)"), rt[4 * k + 3])
        at = rms_to_a(RES, rt, SQ4, RS4, "n2", 0)
        f5 = fence() + [t_hd]
        c4.close()

        c5 = ExitStack()
        V = sb("V5", [P, 2, 4096], F, c5)
        U = sb("U5", [P, 4, T], F, c5)
        Z = sb("Z5", [P, 4, T], F, c5)
        WS = sb("WS5", [P, 2, P], F, c5)
        WM = sb("WM5", [P, 2, P], F, c5)
        WR = sb("WR5", [P, 2, 2, P], F, c5)
        BS = sb("BS5", [P, 2, P], F, c5)
        VS5 = sb("VS5", [P, 2, 8], F, c5)
        VR = sb("VR5", [P, 2], F, c5)
        tvb = []
        for j in range(8):
            par, g, tok = gemm(B_v[j], (AH, AL), at, token_major=True)
            for t in range(2):
                tv = AC(lambda e: e.activation(V[:, t, 512 * j:512 * j + 512], g[:, 512 * t:512 * t + 512],
                                               ACT.Gelu_apprx_tanh), tok, f5)
                tvb.append(tv)
                ts = DV(lambda e: e.tensor_tensor_reduce(
                    out=U[:, 2 * t:2 * t + 2, :].rearrange("p a n -> p (a n)"),
                    in0=V[:, t, 512 * j:512 * j + 512], in1=V[:, t, 512 * j:512 * j + 512], scale=1.0,
                    scalar=0.0, op0=ALU.mult, op1=ALU.add, accum_out=VS5[:, t, j:j + 1]), tv, f5,
                    tvb[-3:-2] and state.get(("v5", t)))
                state[("v5", t)] = ts
            release(par, tv)
        t1 = DV(lambda e: e.tensor_reduce(VR[:, :], VS5[:, :, :], AX.X, ALU.add),
                state[("v5", 0)], state[("v5", 1)])
        t2 = AC(lambda e: e.activation(VR[:, :], VR[:, :], ACT.Sqrt, scale=1.0 / 4096, bias=eps6[:, 0:1]), t1)
        t_vr = DV(lambda e: e.reciprocal(VR[:, :], VR[:, :]), t2)
        yt = {}
        d_ws, d_bs = new_ds(), new_ds()
        s5 = {"ws": f5, "wm": None, "wr": None, "bs": None, "z": None}

        def mixing(j, tu, tz, res):
            tw = dma(d_ws, WS[:, :, :], A["a_w_s_2"][0, 2 * j:2 * j + 2].rearrange("g t s -> t g s"),
                     s5["ws"])
            tb = dma(d_bs, BS[:, :, :].rearrange("p g t -> p (g t)"),
                     A["a_b_s_2"][0, 2 * j:2 * j + 2].rearrange("g t -> (g t)").partition_broadcast(P),
                     s5["bs"], f5)
            b, rel = mb.get()
            PE.wait(rel, tw)
            for q in range(2):
                last = nc.tensor.transpose(M[:, b, q * P:(q + 1) * P], WS[:, q, :], ident[:, :])
            last.then_inc(PE.sem, 1)
            PE.n += 1
            tp = (PE.sem, PE.n)
            s5["ws"] = tp
            tm = DV(lambda e: e.tensor_tensor(WM[:, :, :], M[:, b, 0:T].rearrange("p (g t) -> p g t", g=2),
                                              brc(triu[:, 0:P], 2), ALU.mult), tp)
            mb.put(b, [tm])
            for n in range(2):
                twr = DV(lambda e: e.tensor_scalar(WR[:, n], WM[:, :, :], VR[:, n:n + 1], None, ALU.mult),
                         tm, t_vr, s5["wr"])
            yield
            res.append(twr)
            res.append(tb)

        def mix_mm(j, twr, tb, tu, tz, dst_free):
            uz = []
            for f in range(4):
                b, rel = mb.get()
                PE.wait(rel, twr, tvb)
                c = 4 * j + f
                for n in range(2):
                    last = mm(M[:, b, n * P:(n + 1) * P], V[:, n, c * P:(c + 1) * P], WR[:, n, f // 2, :],
                              n == 0, True)
                last.then_inc(PE.sem, 1)
                PE.n += 1
                tp = (PE.sem, PE.n)
                s5["wr"] = tp
                yield
                m3 = M[:, b, 0:T].rearrange("p (n t) -> p n t", n=2)
                z3 = Z[:, f, :].rearrange("p (n t) -> p n t", n=2)
                tmx = DV(lambda e: e.scalar_tensor_tensor(out=z3, in0=m3, scalar=vc("vg", c),
                                                          in1=brc(BS[:, f // 2, :], 2), op0=ALU.mult,
                                                          op1=ALU.add), tp, tb, s5["z"])
                mb.put(b, [tmx])
                uz.append(tmx)
            s5["bs"] = tmx
            t1 = DV(lambda e: e.tensor_tensor(Z[:, :, :], Z[:, :, :], U[:, :, :], ALU.mult), uz, tu)
            s5["u"] = t1
            s5["mixed"] = t1

        for j in range(8):
            res = []
            bg.append(mixing(j, None, None, res))
            par, g, tok = gemm(B_uz[j][0], (AH, AL), at)
            drain()
            tu = AC(lambda e: e.activation(U[:, :, :].rearrange("p a n -> p (a n)"), g, ACT.Gelu_apprx_tanh),
                    tok, s5.get("u"), t1)
            release(par, tu)
            bg.append(mix_mm(j, res[0], res[1], tu, None, None))
            par, g, tok = gemm(B_uz[j][1], (AH, AL), at)
            drain()
            tz = AC(lambda e: e.activation(U[:, :, :].rearrange("p a n -> p (a n)"), g, ACT.Silu),
                    tok, s5["u"])
            release(par, tz)
            ty = DV(lambda e: e.tensor_tensor(Z[:, :, :], Z[:, :, :], U[:, :, :], ALU.mult), tz, s5["mixed"])
            s5["u"] = ty
            toks = split_act(YH[:, 4 * j:4 * j + 4, :].rearrange("p a n -> p (a n)"),
                             YL[:, 4 * j:4 * j + 4, :].rearrange("p a n -> p (a n)"),
                             Z[:, :, :].rearrange("p a n -> p (a n)"), ty)
            s5["z"] = toks
            for f in range(4):
                yt[4 * j + f] = toks
        f6 = fence()
        c5.close()

        c6 = ExitStack()
        RES = sb("RES6", [P, 16, T], F, c6)
        t_hr = dma(new_ds(), RES[:, :, :].rearrange("p a n -> p (a n)"), h_d[:, :], f6, t_hd)
        SQ6 = sb("SQ6", [P, 4, T], F, c6)
        RS6 = sb("RS6", [P, T], F, c6)
        rt = {}
        for j in range(4):
            par, g, tok = gemm(B_o3[j], (YH, YL), yt)
            r = RES[:, 4 * j:4 * j + 4, :].rearrange("p a n -> p (a n)")
            t1 = DV(lambda e: e.tensor_tensor(r, r, g, ALU.add), tok, t_hr)
            release(par, t1)
            for f in range(4):
                rt[4 * j + f] = t1
        at = rms_to_a(RES, rt, SQ6, RS6, "n2", 16, f6)
        h2t = rt

        c7 = ExitStack()
        Q7 = sb("Q7", [P, 4, T], F, c7)
        K7 = sb("K7", [P, 4, T], F, c7)
        V7 = sb("V7", [P, 2, 512], F, c7)
        Z7 = sb("Z7", [P, 4, T], F, c7)
        O7 = sb("O7", [P, 4, T], F, c7)
        ZM = sb("ZM", [P, 384], F, c7)
        LS = sb("LS", [P, 384], F, c7)
        SPX = sb("SPX", [P, 384], F, c7)
        NM = sb("NM", [P, 384], F, c7)
        TG = sb("TG", [P, P], F, c7)
        f7 = fence()
        tn = PL(lambda e: e.memset(NM[:, :], 0.0), f7)
        for o in (0, 256):
            t_nm = PL(lambda e: e.affine_select(out=NM[:, o:o + P], in_=NM[:, o:o + P],
                                                compare_op=ALU.is_gt, fill=NEG, base=0,
                                                pattern=[[1, P]], channel_multiplier=-1), tn)
        tg = PL(lambda e: e.memset(TG[:, :], 1.0), f7)
        t_tg = PL(lambda e: e.affine_select(out=TG[:, :], in_=TG[:, :], compare_op=ALU.is_ge, fill=0.0,
                                            base=0, pattern=[[-1, P]], channel_multiplier=1), tg)
        yt = {}
        s7 = {"qk": None, "v": None, "z": None, "o": f7, "zm": None, "sp": None, "ls": None}

        def stick(j, tq, tk, tv, res):
            ot = []
            for h in range(4):
                b, rel = mb.get()
                PE.wait(rel, tq, tk)
                q, k = Q7[:, h, :], K7[:, h, :]
                mm(M[:, b, 0:T], k[:, 0:P], q[:, :], True, True)
                tp = PE(lambda e: mm(M[:, b, T:384], k[:, P:T], q[:, P:T], False, True))
                s7["qk"] = tp
                yield
                t1 = DV(lambda e: e.scalar_tensor_tensor(out=ZM[:, :], in0=M[:, b, 0:384], scalar=SCALE,
                                                         in1=NM[:, :], op0=ALU.mult, op1=ALU.add),
                        tp, t_nm, s7["zm"], f7)
                mb.put(b, [t1])
                t2 = DV(lambda e: e.scalar_tensor_tensor(out=LS[:, :], in0=ZM[:, :], scalar=-1.0, in1=ZM[:, :],
                                                         op0=ALU.mult, op1=ALU.max), t1, s7["ls"], f7)
                t3 = AC(lambda e: e.activation(LS[:, :], LS[:, :], ACT.Exp, scale=-1.0), t2)
                t4 = AC(lambda e: e.activation(LS[:, :], LS[:, :], ACT.Ln, bias=1.0), t3)
                yield
                t5 = DV(lambda e: e.scalar_tensor_tensor(out=SPX[:, :], in0=ZM[:, :], scalar=0.0,
                                                         in1=LS[:, :], op0=ALU.max, op1=ALU.add),
                        t4, s7["sp"], f7)
                b, rel = mb.get()
                PE.wait(rel, t5, t_tg)
                mm(M[:, b, 0:T], TG[:, :], SPX[:, 0:T], True, False)
                mm(M[:, b, P:T], ones[:, :], SPX[:, T:384], False, True)
                tp = PE(lambda e: mm(M[:, b, T:384], TG[:, :], SPX[:, T:384], False, True))
                s7["sp"] = tp
                yield
                t6 = DV(lambda e: e.tensor_tensor(ZM[:, :], ZM[:, :], M[:, b, 0:384], ALU.subtract), tp)
                mb.put(b, [t6])
                t7 = AC(lambda e: e.activation(LS[:, :], ZM[:, :], ACT.Exp), t6, t5)
                s7["zm"] = t7
                yield
                b, rel = mb.get()
                PE.wait(rel, t7, tv)
                mm(M[:, b, 0:T], V7[:, 0, h * P:(h + 1) * P], LS[:, 0:T], True, False)
                tp = PE(lambda e: mm(M[:, b, P:T], V7[:, 1, h * P:(h + 1) * P], LS[:, T:384], False, True))
                s7["ls"] = tp
                s7["v"] = tp
                yield
                ot.append(AC(lambda e: e.copy(O7[:, h, :], M[:, b, 0:T]), tp, s7["o"]))
                mb.put(b, [ot[-1]])
            res.extend(ot)

        for j in range(4):
            par, g, tok = gemm(B_at[j][0], (AH, AL), at)
            tq = DV(lambda e: e.tensor_copy(Q7[:, :, :].rearrange("p a n -> p (a n)"), g), tok, s7["qk"], f7)
            release(par, tq)
            par, g, tok = gemm(B_at[j][1], (AH, AL), at)
            tk = DV(lambda e: e.tensor_copy(K7[:, :, :].rearrange("p a n -> p (a n)"), g), tok, s7["qk"], f7)
            release(par, tk)
            par, g, tok = gemm(B_at[j][2], (AH, AL), at, token_major=True)
            tv = DV(lambda e: e.tensor_copy(V7[:, :, :].rearrange("p a n -> p (a n)"), g), tok, s7["v"], f7)
            release(par, tv)
            res = []
            bg.append(stick(j, tq, tk, tv, res))
            par, g, tok = gemm(B_at[j][3], (AH, AL), at, steps=3)
            drain()
            tz = AC(lambda e: e.activation(Z7[:, :, :].rearrange("p a n -> p (a n)"), g, ACT.Silu),
                    tok, s7["z"], f7)
            release(par, tz)
            t1 = DV(lambda e: e.tensor_tensor(O7[:, :, :], O7[:, :, :], Z7[:, :, :], ALU.mult), tz, res)
            toks = split_act(YH[:, 4 * j:4 * j + 4, :].rearrange("p a n -> p (a n)"),
                             YL[:, 4 * j:4 * j + 4, :].rearrange("p a n -> p (a n)"),
                             O7[:, :, :].rearrange("p a n -> p (a n)"), t1)
            s7["z"] = t1
            s7["o"] = toks
            for f in range(4):
                yt[4 * j + f] = toks
        f8 = fence()
        c7.close()

        c8 = ExitStack()
        OUT = sb("OUT8", [P, 2, DM], F, c8)
        FG = sb("FG8", [P, DM], F, c8)
        TT = sb("TT8", [P, 512], F, c8)
        SS = sb("SS8", [P, 2, 4], F, c8)
        RR = sb("RR8", [P, 2], F, c8)
        t_fg = dma(new_ds(), FG[:, :], A["final_g_2"].partition_broadcast(P), f8)
        tsq = [None, None]
        for j in range(4):
            def resid(par):
                for t in range(2):
                    for f in range(4):
                        last = mm(G[:, 2 * par + t, f * P:(f + 1) * P], RES[:, 4 * j + f, t * P:(t + 1) * P],
                                  ident[:, :], False, f == 3)
                last.then_inc(PE.sem, 1)
                PE.n += 1
                return (PE.sem, PE.n)
            PE.wait(h2t[15])
            par, g, tok = gemm(B_o4[j], (YH, YL), yt, token_major=True, extra=resid)
            for t in range(2):
                o = OUT[:, t, 512 * j:512 * j + 512]
                tc = DV(lambda e: e.tensor_copy(o, g[:, 512 * t:512 * t + 512]), tok, f8)
                tsq[t] = DV(lambda e: e.tensor_tensor_reduce(
                    out=TT[:, :], in0=o, in1=o, scale=1.0, scalar=0.0, op0=ALU.mult, op1=ALU.add,
                    accum_out=SS[:, t, j:j + 1]), tc, tsq)
            release(par, tc)
        t1 = DV(lambda e: e.tensor_reduce(RR[:, :], SS[:, :, :], AX.X, ALU.add), tsq)
        t2 = AC(lambda e: e.activation(RR[:, :], RR[:, :], ACT.Sqrt, scale=1.0 / DM, bias=eps6[:, 0:1]), t1)
        t3 = DV(lambda e: e.reciprocal(RR[:, :], RR[:, :]), t2)
        d_o = new_ds()
        for t in range(2):
            for q in range(2):
                o = OUT[:, t, 1024 * q:1024 * q + 1024]
                t4 = DV(lambda e: e.scalar_tensor_tensor(out=o, in0=o, scalar=RR[:, t:t + 1],
                                                         in1=FG[:, 1024 * q:1024 * q + 1024],
                                                         op0=ALU.mult, op1=ALU.mult), t3, t_fg)
                t5 = dma(d_o, out[0, t * P:(t + 1) * P, 1024 * q:1024 * q + 1024], o, t4)
        SP.wait(t5)
        SP.wait(t_hd, t_csd)
        c8.close()
        c6.close()
        cy.close()


_INS = ['x', 'ssd_w_in', 'ssd_conv_w', 'ssd_conv_b', 'ssd_dt_bias', 'ssd_a_log', 'ssd_d_skip',
        'ssd_norm_g', 'ssd_w_out', 'dsa_w_in', 'dsa_q_norm_g', 'dsa_kv_norm_g', 'dsa_w_uq', 'dsa_w_uk',
        'dsa_w_uv', 'dsa_w_idx_q', 'dsa_w_out', 'ln_g', 'ln_b', 'norm_g_2', 'a_w_in_2', 'a_v_norm_g_2',
        'a_w_s_2', 'a_b_s_2', 'a_w_out_2', 'b_w_in_2', 'b_w_out_2', 'final_g_2']


def kernel(**inputs):
    import numpy as _np
    import concourse.bacc as _bacc
    from concourse import mybir as _mybir
    from concourse.bass_utils import run_bass_kernel_spmd as _run

    nc = _bacc.Bacc("TRN2", target_bir_lowering=False, num_devices=1)
    arrays, args = {}, {}
    for name in _INS:
        a = _np.ascontiguousarray(inputs[name])
        arrays[f"in_{name}"] = a
        args[name] = nc.dram_tensor(f"in_{name}", a.shape, _mybir.dt.from_np(a.dtype), kind="ExternalInput").ap()
    out = nc.dram_tensor("out_0", (1, 256, 2048), _mybir.dt.float32, kind="ExternalOutput").ap()
    build(nc, args, out)
    r = _run(nc, [arrays], core_ids=[0])
    return r.results[0]["out_0"]
```

```python
from collections import deque
from contextlib import ExitStack

import numpy as np

import concourse.bass as bass
from concourse import mybir

F = mybir.dt.float32
R = mybir.dt.float32r
ALU = mybir.AluOpType
ACT = mybir.ActivationFunctionType
AX = mybir.AxisListType

P = 128
T = 256
DM = 2048
NR = 4
NH = 3
UW = 1024
ALPHA = 4.0 ** 0.25
LN_EPS = 1e-5
RMS_EPS = 1e-6
NEG = -1.0e30


class Line:

    def __init__(self, eng, sem):
        self.eng, self.sem, self.n, self.seen = eng, sem, 0, {}

    def wait(self, *toks):
        for t in toks:
            if t is None:
                continue
            if isinstance(t, list):
                self.wait(*t)
                continue
            sem, v = t
            if self.seen.get(sem.name, 0) < v:
                self.seen[sem.name] = v
                self.eng.wait_ge(sem, v)

    def __call__(self, fn, *toks):
        self.wait(*toks)
        fn(self.eng).then_inc(self.sem, 1)
        self.n += 1
        return (self.sem, self.n)


class DmaSem:
    def __init__(self, sem):
        self.sem, self.n = sem, 0


class Banks:

    def __init__(self, ids):
        self.free = deque((i, []) for i in ids)

    def get(self):
        return self.free.popleft()

    def put(self, i, toks):
        self.free.append((i, toks))


def build(nc, A, out):
    ctx = ExitStack()
    with ctx:
        def sb(name, shape, dt=F, c=None):
            return (c or ctx).enter_context(nc.sbuf_tensor(name, shape, dt))

        def sem(name):
            return ctx.enter_context(nc.semaphore(name))

        PE = Line(nc.tensor, sem("s_pe"))
        AC = Line(nc.scalar, sem("s_act"))
        DV = Line(nc.vector, sem("s_dve"))
        PL = Line(nc.gpsimd, sem("s_pool"))
        SP = Line(nc.sync, sem("s_sp"))

        def dma(ds, dst, src, *toks, line=None):
            ln = line or SP
            ln.wait(*toks)
            ln.eng.dma_start(dst, src).then_inc(ds.sem, 16)
            ds.n += 16
            return (ds.sem, ds.n)

        d_raw = [DmaSem(sem(f"d_raw{i}")) for i in range(NR)]
        n_ds = [0]

        def new_ds():
            n_ds[0] += 1
            return DmaSem(sem(f"d_m{n_ds[0]}"))

        G = ctx.enter_context(nc.psum_tensor("G", [P, 4, 512], F))
        M = ctx.enter_context(nc.psum_tensor("M", [P, 4, 512], F))
        mb = Banks(range(4))
        grel = [[], []]
        gpar = [0]

        RAW = sb("RAW", [P, NR, UW])
        WH = sb("WH", [P, NH, UW], R)
        WL = sb("WL", [P, NH, UW], R)
        AH = sb("AH", [P, 16, T], R)
        AL = sb("AL", [P, 16, T], R)
        ident = sb("ident", [P, P])
        ones = sb("ones", [P, P])
        triu = sb("triu", [P, 384])
        VC = sb("VC", [P, 4, P])
        dcol = sb("dcol", [P, 32])
        eps6 = sb("eps6", [P, 2])
        RSK = sb("RSK", [P, T])
        CC = sb("CC", [P, 4])
        DB = sb("DB", [P, 64])
        alog = sb("alog", [64, 1])
        dtb = sb("dtb", [64, 1])

        units = []

        def plan(wap, r0, K, cols, width):
            nk = UW // width
            nt = K // P
            blk = []
            k = 0
            while k < nt:
                n = min(nk, nt - k)
                pieces = []
                for c0, cn, o in cols:
                    src = wap[r0 + k * P:r0 + (k + n) * P, c0:c0 + cn].rearrange(
                        "(k p) n -> p k n", p=P)
                    pieces.append((0, n, width, o, cn, src))
                units.append(pieces)
                blk.append((len(units) - 1, list(range(k, k + n))))
                k += n
            return blk, width

        def plan_rows(wap, row0):
            src = wap[row0:row0 + 1024, :].rearrange("(q p) n -> p q n", p=P)
            units.append([(0, 8, 128, 0, 128, src)])
            return len(units) - 1

        def plan_values(wap, row0):
            src = wap[row0:row0 + 1024, :].rearrange("(h c p) n -> c p h n", p=P, c=2)
            units.append([(512 * c, 4, 128, 0, 128, src[c]) for c in range(2)])
            return len(units) - 1

        def plan_out(wap):
            return [(f, n, plan(wap, 0, 4096, [(P * f, P * n, 0)], P * n))
                    for f, n in ((0, 4), (4, 4), (8, 4), (12, 2), (14, 2))]

        fetched, ready = [0], [0]
        raw_tok, raw_free, w_tok, w_free = {}, {}, {}, {}

        def fetch_to(n):
            while fetched[0] < min(n, len(units)):
                u = fetched[0]
                s = u % NR
                for a0, nk, width, o, cn, src in units[u]:
                    dst = RAW[:, s, a0:a0 + nk * width].rearrange("p (k n) -> p k n", k=nk)[:, :, o:o + cn]
                    raw_tok[u] = dma(d_raw[s], dst, src, raw_free.get(u - NR))
                fetched[0] += 1

        def split_to(n):
            while ready[0] < min(n, len(units)):
                u = ready[0]
                fetch_to(u + 1)
                s, r = u % NH, u % NR
                ta = AC(lambda e: e.copy(WH[:, s, :], RAW[:, r, :]), raw_tok[u], w_free.get(u - NH))
                td = DV(lambda e: e.tensor_tensor(WL[:, s, :], RAW[:, r, :], WH[:, s, :].bitcast(F),
                                                  ALU.subtract), ta, raw_tok[u], w_free.get(u - NH))
                raw_free[u] = [ta, td]
                w_tok[u] = [ta, td]
                ready[0] += 1
                fetch_to(u + NR)

        bg = deque()

        tick = [0]

        def task(gen):
            bg.append([gen, 0])

        def step():
            tick[0] += 1
            for t in list(bg):
                if t[1] <= tick[0]:
                    try:
                        t[1] = tick[0] + (next(t[0]) or 1)
                    except StopIteration:
                        bg.remove(t)

        def drain():
            while bg:
                step()

        def mm(o, l, r, start, stop_):
            return nc.tensor.matmul(o, l, r, start=start, stop=stop_, skip_group_check=True)

        def end_unit(u, last):
            last.then_inc(PE.sem, 1)
            PE.n += 1
            w_free[u] = (PE.sem, PE.n)
            return (PE.sem, PE.n)

        def gemm(blk, a, at, token_major=False):
            us, width = blk
            ah, al = a
            par = gpar[0]
            gpar[0] ^= 1
            take(par)
            nk = us[-1][1][-1] + 1
            for u, kts in us:
                split_to(u + NH)
                PE.wait(w_tok[u])
                wh = WH[:, u % NH, 0:len(kts) * width].rearrange("p (k n) -> p k n", k=len(kts))
                wl = WL[:, u % NH, 0:len(kts) * width].rearrange("p (k n) -> p k n", k=len(kts))
                for i, k in enumerate(kts):
                    while k not in at:
                        step()
                    PE.wait(at[k])
                    lastk = k == nk - 1
                    if token_major:
                        for t in range(2):
                            o = G[:, 2 * par + t, 0:width]
                            xh, xl = ah[:, k, t * P:(t + 1) * P], al[:, k, t * P:(t + 1) * P]
                            mm(o, xh, wh[:, i, :], k == 0, False)
                            mm(o, xh, wl[:, i, :], False, False)
                            last = mm(o, xl, wh[:, i, :], False, lastk)
                    else:
                        for f in range(width // P):
                            o = G[:, 2 * par + f // 2, (f % 2) * T:(f % 2 + 1) * T]
                            h, l = wh[:, i, f * P:(f + 1) * P], wl[:, i, f * P:(f + 1) * P]
                            mm(o, h, ah[:, k, :], k == 0 and f % 2 == 0, False)
                            mm(o, h, al[:, k, :], False, False)
                            last = mm(o, l, ah[:, k, :], False, lastk)
                tok = end_unit(u, last)
                step()
            g = G[:, 2 * par:2 * par + 2, :].rearrange("p a n -> p (a n)")
            return par, g, tok

        def take(par):
            while grel[par] is None:
                step()
            PE.wait(grel[par])
            grel[par] = None

        def release(par, *toks):
            grel[par] = list(toks)

        def pe_end(last):
            last.then_inc(PE.sem, 1)
            PE.n += 1
            return (PE.sem, PE.n)

        def flat(ap):
            return ap.rearrange("p a n -> p (a n)")

        def split_act(h, l, src, *toks):
            ta = AC(lambda e: e.copy(h, src), *toks)
            td = DV(lambda e: e.tensor_tensor(l, src, h.bitcast(F), ALU.subtract), ta, *toks)
            return [ta, td]

        ssd_in = A["ssd_w_in"][0]
        B_dt = plan(ssd_in, 0, DM, [(10240, 64, 0), (10240, 64, 64)], 128)
        B_bc = [plan(ssd_in, 0, DM, [(8192 + 512 * i, 512, 0)], 512) for i in range(4)]
        B_xz = []
        for g in range(8):
            B_xz.append((plan(ssd_in, 0, DM, [(4096 + 512 * g, 512, 0)], 512),
                         plan(ssd_in, 0, DM, [(512 * g, 512, 0)], 512)))
        B_o1 = plan_out(A["ssd_w_out"][0])
        din = A["dsa_w_in"][0]
        uq, uk, uv = A["dsa_w_uq"][0], A["dsa_w_uk"][0], A["dsa_w_uv"][0]
        uk = uk.rearrange("h c d -> (h c) d")
        uv = uv.rearrange("h c d -> (h c) d")

        def p_gate(j):
            return plan(din, 0, DM, [(848 + 512 * j, 512, 0)], 512)

        B_cq = plan(din, 0, DM, [(0, 512, 0)], 512)
        B_ms = plan(din, 0, DM, [(512, 320, 0), (768, 64, 320), (832, 128, 384)], 512)
        GATES = ((1, 2), (3,), (4,), (5,), (6,), (7,), (), ())
        B_gate = {0: p_gate(0)}
        B_qi = [plan(A["dsa_w_idx_q"][0], 0, 512, [(512 * i, 512, 0)], 512) for i in range(2)]
        B_qkv = []
        for j in range(8):
            B_qkv.append((plan(uq, 0, 512, [(512 * j, 512, 0)], 512),
                          plan_rows(uk, 1024 * j), plan_values(uv, 1024 * j)))
            for i in GATES[j]:
                B_gate[i] = p_gate(i)
        B_o2 = plan_out(A["dsa_w_out"][0])
        ain = A["a_w_in_2"][0]
        B_v = [plan(ain, 0, DM, [(4096 + 512 * j, 512, 0)], 512) for j in range(8)]
        B_uz = [(plan(ain, 0, DM, [(512 * j, 512, 0)], 512),
                 plan(ain, 0, DM, [(8192 + 512 * j, 512, 0)], 512)) for j in range(8)]
        B_o3 = plan_out(A["a_w_out_2"][0])
        bin_ = A["b_w_in_2"][0]
        B_at = [[plan(bin_, 0, DM, [(2048 * c + 512 * j, 512, 0)], 512) for c in range(4)]
                for j in range(4)]
        B_o4 = [plan(A["b_w_out_2"][0], 0, DM, [(512 * j, 512, 0)], 512) for j in range(4)]

        cs_d = nc.dram_tensor("cs_scratch", [64, T], F)
        h_d = nc.dram_tensor("h_scratch", [P, 16 * T], F)
        h2_d = nc.dram_tensor("h2_scratch", [2, 4, P, 512], F)

        c0 = ExitStack()
        XS = sb("XS", [P, 2, DM], F, c0)
        VS = sb("VS", [P, 4, P], F, c0)
        x = A["x"][0]
        t_x = [dma(new_ds(), XS[:, i, :], x[i * P:(i + 1) * P, :]) for i in range(2)]

        col = {}
        d_vs = new_ds()
        pos = [0, 0]

        def rows(name, ap, n):
            done = 0
            ts = []
            while done < n:
                k = min(n - done, P - pos[1])
                ts.append(dma(d_vs, VS[pos[1]:pos[1] + k, pos[0], :], ap[done:done + k, :]))
                for i in range(k):
                    col[(name, done + i)] = (pos[0], pos[1] + i)
                done += k
                pos[1] += k
                if pos[1] == P:
                    pos[0], pos[1] = pos[0] + 1, 0
            return ts[-1]

        def as_rows(ap):
            return ap.rearrange("(n p) -> n p", p=P)

        t_vs = rows("cw", A["ssd_conv_w"][0].rearrange("j (n p) -> (j n) p", p=P), 192)
        t_vs = rows("cb", as_rows(A["ssd_conv_b"][0]), 48)
        t_vs = rows("ng", as_rows(A["ssd_norm_g"][0]), 32)
        t_vs = rows("lg", A["ln_g"].rearrange("d (n p) -> (d n) p", p=P), 32)
        t_vs = rows("lb", A["ln_b"].rearrange("d (n p) -> (d n) p", p=P), 32)
        t_vs = rows("qg", as_rows(A["dsa_q_norm_g"][0]), 4)
        t_vs = rows("kg", as_rows(A["dsa_kv_norm_g"][0]), 2)
        t_vs = rows("n2", A["norm_g_2"].rearrange("d (n p) -> (d n) p", p=P), 32)
        t_vs = rows("vg", as_rows(A["a_v_norm_g_2"][0]), 32)
        nrows = pos[0] * P + pos[1]

        def vc(name, i):
            a, b = col[(name, i)]
            return VC[:, a, b:b + 1]

        d_s = new_ds()
        dma(d_s, dtb[:, :], A["ssd_dt_bias"][0].rearrange("(h a) -> h a", a=1))
        dma(d_s, alog[:, :], A["ssd_a_log"][0].rearrange("(h a) -> h a", a=1))
        t_sm = dma(d_s, DB[:, :], A["ssd_d_skip"][0].partition_broadcast(P))
        for q in range(2):
            t_dc = DV(lambda e: e.tensor_copy(dcol[64 * q:64 * q + 64, :], DB[64 * q:64 * q + 64, q::2]), t_sm)

        ti = PL(lambda e: e.memset(ident[:, :], 0.0))
        t_id = PL(lambda e: e.affine_select(out=ident[:, :], in_=ident[:, :], compare_op=ALU.not_equal,
                                            fill=1.0, base=0, pattern=[[-1, P]], channel_multiplier=1), ti)
        t_one = PL(lambda e: e.memset(ones[:, :], 1.0))
        tr = PL(lambda e: e.memset(triu[:, :], 1.0))
        for o in (0, 256):
            t_tri = PL(lambda e: e.affine_select(out=triu[:, o:o + P], in_=triu[:, o:o + P],
                                                 compare_op=ALU.is_ge, fill=0.0, base=0,
                                                 pattern=[[1, P]], channel_multiplier=-1), tr)

        b, rel = mb.get()
        PE.wait(t_id, t_vs)
        nv = [min(P, nrows - P * i) for i in range(4) if nrows > P * i]
        for i, n in enumerate(nv):
            def tv(e, i=i, n=n):
                return e.transpose(M[:, b, i * P:i * P + n], VS[0:n, i, :], ident[0:n, 0:n])
            tp = PE(tv)
        for i, n in enumerate(nv):
            t_vc = DV(lambda e: e.tensor_copy(VC[:, i, 0:n], M[:, b, i * P:i * P + n]), tp)
        mb.put(b, [t_vc])

        xt = {}
        for k in range(0, 16, 2):
            b, rel = mb.get()
            PE.wait(t_x, t_id, rel)
            for i in range(2):
                for t in range(2):
                    last = nc.tensor.transpose(M[:, b, (2 * i + t) * P:(2 * i + t + 1) * P],
                                               XS[:, t, (k + i) * P:(k + i + 1) * P], ident[:, :])
            last.then_inc(PE.sem, 1)
            PE.n += 1
            toks = split_act(AH[:, k:k + 2, :].rearrange("p a n -> p (a n)"),
                             AL[:, k:k + 2, :].rearrange("p a n -> p (a n)"), M[:, b, :],
                             (PE.sem, PE.n))
            xt[k] = xt[k + 1] = toks
            mb.put(b, toks)
        last_x = [(PE.sem, PE.n)]
        c0.close()

        def brc(ap, n):
            return ap.unsqueeze(1).to_broadcast([P, n, ap.shape[1]])

        cy = ExitStack()
        YH = sb("YH", [P, 32, T], R, cy)
        YL = sb("YL", [P, 32, T], R, cy)
        c1 = ExitStack()
        BT = sb("BT", [P, 8, T], F, c1)
        CT = sb("CT", [P, 8, T], F, c1)
        XG = sb("XG", [P, 4, T], F, c1)
        CSB = sb("CSB", [P, 8, T], F, c1)
        E2 = sb("E2", [P, 8, 384], F, c1)
        XD = sb("XD", [P, 2, 512], F, c1)
        YT = sb("YT", [P, 4, T], F, c1)
        SZ = sb("SZ", [P, 4, T], F, c1)
        CB = sb("CB", [P, 384], F, c1)
        RI = sb("RI", [P, T], F, c1)
        dtT = sb("dtT", [P, 2, 64], F, c1)
        csT = sb("csT", [P, 2, 64], F, c1)
        te1 = PL(lambda e: e.memset(eps6[:, 0:1], RMS_EPS))
        t_eps = PL(lambda e: e.memset(eps6[:, 1:2], LN_EPS))

        A1 = (AH, AL)
        tk = {}

        def get(*names):
            for n in names:
                while n not in tk:
                    step()
            return [tk[n] for n in names]

        def ones_sum(o, src, first=True, last=True):
            return mm(o, ones[:, :], src, first, last)

        def fold(sq, n, *toks):
            while n > 1:
                n //= 2
                t = DV(lambda e: e.tensor_tensor(sq[:, 0:n, :], sq[:, 0:n, :], sq[:, n:2 * n, :], ALU.add),
                       *toks)
                toks = (t,)
            return toks[0]

        def dt_task(par, g, tok):
            xb, ab, sp_, ad, cs_ = (YT[0:64, i, :] for i in (0, 1, 2, 3, 1))
            dtv = SZ[0:64, 0, :]
            nea = SZ[0:64, 1, 0:1]
            t1 = DV(lambda e: e.tensor_scalar(xb, g[0:64, 0:T], dtb[:, 0:1], None, ALU.add), tok, t_sm, last_x)
            release(par, t1)
            t2 = DV(lambda e: e.scalar_tensor_tensor(out=ab, in0=xb, scalar=-1.0, in1=xb, op0=ALU.mult,
                                                     op1=ALU.max), t1)
            t3 = AC(lambda e: e.activation(nea, alog[:, :], ACT.Exp), t_sm, last_x)
            t4 = AC(lambda e: e.activation(ab, ab, ACT.Exp, scale=-1.0), t2)
            t5 = AC(lambda e: e.activation(sp_, ab, ACT.Ln, bias=1.0), t4)
            yield
            t6 = DV(lambda e: e.scalar_tensor_tensor(out=dtv, in0=xb, scalar=0.0, in1=sp_, op0=ALU.max,
                                                     op1=ALU.add), t5)
            t7 = DV(lambda e: e.tensor_scalar(ad, dtv, nea, -1.0, ALU.mult, ALU.mult), t6, t3)
            t7b = DV(lambda e: e.memset(xb, 1.0), t6)
            t8 = DV(lambda e: e.tensor_tensor_scan(cs_, xb, ad, 0.0, ALU.mult, ALU.add), t7, t7b, t5)
            tk["csd"] = dma(new_ds(), cs_d[:, :], cs_, t8)
            yield
            b, rel = mb.get()
            PE.wait(rel, t8, t6)
            for t in range(2):
                nc.tensor.transpose(M[:, b, t * P:t * P + 64], dtv[:, t * P:(t + 1) * P], ident[0:64, 0:64])
                last = nc.tensor.transpose(M[:, b, 256 + t * P:256 + t * P + 64],
                                           cs_[:, t * P:(t + 1) * P], ident[0:64, 0:64])
            tp = pe_end(last)
            m = M[:, b, :].rearrange("p (a t n) -> p a t n", a=2, t=2)
            tk["dtT"] = DV(lambda e: e.tensor_copy(dtT[:, :, :], m[:, 0, :, 0:64]), tp)
            tk["csT"] = DV(lambda e: e.tensor_scalar(csT[:, :, :], m[:, 1, :, 0:64], -1.0, None, ALU.mult), tp)
            mb.put(b, [tk["csT"]])

        par, g, tok = gemm(B_dt, A1, xt)
        task(dt_task(par, g, tok))

        def conv(par, g, tok, ch, dst, free, name):
            ts = []
            for f in range(4):
                u = g[:, f * T:(f + 1) * T]
                ts.append(DV(lambda e: e.tensor_scalar(dst[:, f, :], u, vc("cw", 3 * 48 + ch + f),
                                                       vc("cb", ch + f), ALU.mult, ALU.add),
                             tok, t_vc, free))
            yield
            for j in (2, 1, 0):
                s = 3 - j
                for f in range(4):
                    u = g[:, f * T:(f + 1) * T]
                    ts[f] = DV(lambda e: e.scalar_tensor_tensor(
                        out=dst[:, f, s:T], in0=u[:, 0:T - s], scalar=vc("cw", j * 48 + ch + f),
                        in1=dst[:, f, s:T], op0=ALU.mult, op1=ALU.add), ts[f])
                yield
            release(par, ts[-1])
            d = flat(dst)
            tk[name] = AC(lambda e: e.activation(d, d, ACT.Silu), ts)

        for i in range(4):
            par, g, tok = gemm(B_bc[i], A1, xt)
            dst = (BT, CT)[i // 2][:, 4 * (i % 2):4 * (i % 2) + 4, :]
            task(conv(par, g, tok, 32 + 4 * i, dst, last_x, ("bc", i)))

        yt = {}
        d_csb = new_ds()
        st = {"csb": None, "e": None, "xd": None, "yt": None, "xg": None, "ri": None, "sz": None}

        def decay(g, h0, tcs):
            for h in range(h0, h0 + 4):
                hh = 8 * g + h
                DV(lambda e: e.tensor_scalar(E2[:, h, 0:256], CSB[:, h, :], csT[:, 0, hh:hh + 1], 0.0,
                                             ALU.add, ALU.min), tcs, tk["csT"], st["e"])
                td = DV(lambda e: e.tensor_scalar(E2[:, h, 256:384], CSB[:, h, P:T], csT[:, 1, hh:hh + 1],
                                                  0.0, ALU.add, ALU.min))
            st["csb"] = td
            ev = E2[:, h0:h0 + 4, :].rearrange("p h n -> p (h n)")
            return AC(lambda e: e.activation(ev, ev, ACT.Exp), td)

        def ssd(g, par, gx, tok):
            while not ("csT" in tk and "csd" in tk and all(("bc", i) in tk for i in range(4))):
                yield
            tcs = dma(d_csb, CSB[:, :, :], cs_d[8 * g:8 * g + 8, :].rearrange("h t -> (h t)")
                      .partition_broadcast(P), tk["csd"], st["csb"])
            while g > 0 and ("y", g - 1) not in tk:
                yield
            yield from conv(par, gx, tok, 4 * g, XG[:, :, :], st["xg"], ("xg", g))
            t_xg = tk[("xg", g)]
            yield
            b, rel = mb.get()
            PE.wait(rel, [tk[("bc", i)] for i in range(4)])
            mm(M[:, b, 0:256], BT[:, g, 0:P], CT[:, g, :], True, True)
            tp = PE(lambda e: mm(M[:, b, 256:384], BT[:, g, P:T], CT[:, g, P:T], False, True))
            tcb = DV(lambda e: e.tensor_tensor(CB[:, :], M[:, b, 0:384], triu[:, :], ALU.mult),
                     tp, t_tri, st["e"])
            mb.put(b, [tcb])
            yield
            yield
            te = decay(g, 0, tcs)
            yield
            txd = []
            for t in range(2):
                b, rel = mb.get()
                PE.wait(rel, t_xg)
                for f in range(4):
                    last = nc.tensor.transpose(M[:, b, f * P:(f + 1) * P], XG[:, f, t * P:(t + 1) * P],
                                               ident[:, :])
                tp = pe_end(last)
                bd = dtT[:, t, 8 * g:8 * g + 8].unsqueeze(2).to_broadcast([P, 8, 64])
                txd.append(DV(lambda e: e.tensor_tensor(
                    XD[:, t, :].rearrange("p (h d) -> p h d", h=8),
                    M[:, b, :].rearrange("p (h d) -> p h d", h=8), bd, ALU.mult),
                    tp, tk["dtT"], st["xd"]))
                mb.put(b, [txd[-1]])
                yield
            cbb = CB[:, :].unsqueeze(1).to_broadcast([P, 4, 384])
            tm = [DV(lambda e: e.tensor_tensor(E2[:, 0:4, :], E2[:, 0:4, :], cbb, ALU.mult), te, tcb)]
            yield
            te = decay(g, 4, tcs)
            yield
            tm.append(DV(lambda e: e.tensor_tensor(E2[:, 4:8, :], E2[:, 4:8, :], cbb, ALU.mult), te, tcb))
            yield
            while g > 0 and ("yt", g - 1) not in tk:
                yield
            ty = []
            for q in range(4):
                b, rel = mb.get()
                PE.wait(rel, tm[q // 2], txd)
                for r in range(2):
                    h = 2 * q + r
                    o = M[64 * r:64 * r + 64, b, :]
                    mm(o[:, 0:256], XD[:, 0, 64 * h:64 * h + 64], E2[:, h, 0:256], True, False)
                    last = mm(o[:, 128:256], XD[:, 1, 64 * h:64 * h + 64], E2[:, h, 256:384], False, True)
                tp = pe_end(last)
                ty.append(DV(lambda e: e.scalar_tensor_tensor(
                    out=YT[:, q, :], in0=XG[:, q, :], scalar=dcol[:, 4 * g + q:4 * g + q + 1],
                    in1=M[:, b, 0:T], op0=ALU.mult, op1=ALU.add), tp, t_xg, t_dc, tk["csd"], st["yt"]))
                mb.put(b, [ty[-1]])
                yield
            st["e"] = tp
            st["xd"] = tp
            st["xg"] = [ty[-1], tp]
            tk[("y", g)] = ty

        def gate_z(g, par, gz, tok):
            while ("dtT" not in tk) or (g > 0 and ("yt", g - 1) not in tk):
                yield
            tz = AC(lambda e: e.activation(flat(SZ[:, :, :]), gz, ACT.Silu), tok, st["sz"], tk["csT"], tk["dtT"])
            release(par, tz)
            while ("y", g) not in tk:
                yield
            sz, yv = flat(SZ[:, :, :]), flat(YT[:, :, :])
            t1 = DV(lambda e: e.tensor_tensor(yv, yv, sz, ALU.mult), tz, tk[("y", g)])
            t2 = AC(lambda e: e.activation(sz, yv, ACT.Square), t1)
            yield
            t2 = fold(SZ, 4, t2)
            yield 2
            b, rel = mb.get()
            PE.wait(rel, t2, t_one)
            tp = pe_end(ones_sum(M[:, b, 0:T], SZ[:, 0, :]))
            yield
            t3 = AC(lambda e: e.activation(RI[:, :], M[:, b, 0:T], ACT.Sqrt, scale=1.0 / 512, bias=eps6[:, 0:1]),
                    tp, t_eps, st["ri"])
            mb.put(b, [t3])
            t4 = DV(lambda e: e.reciprocal(RI[:, :], RI[:, :]), t3)
            for f in range(4):
                t5 = DV(lambda e: e.scalar_tensor_tensor(out=SZ[:, f, :], in0=YT[:, f, :],
                                                         scalar=vc("ng", 4 * g + f), in1=RI[:, :],
                                                         op0=ALU.mult, op1=ALU.mult), t4, tp, t1)
            st["yt"] = t5
            st["ri"] = t5
            yield
            toks = split_act(flat(YH[:, 4 * g:4 * g + 4, :]), flat(YL[:, 4 * g:4 * g + 4, :]), sz, t5)
            st["sz"] = toks
            for f in range(4):
                yt[4 * g + f] = toks
            tk[("yt", g)] = toks

        for gi in range(8):
            par, g, tok = gemm(B_xz[gi][0], A1, xt)
            task(ssd(gi, par, g, tok))
            par, g, tok = gemm(B_xz[gi][1], A1, xt)
            task(gate_z(gi, par, g, tok))

        def fence():
            return [(PE.sem, PE.n), (AC.sem, AC.n), (DV.sem, DV.n)]

        def ln_blocks(res0, blocks, yt, RES, cn, li):
            PV = sb(f"PV{li}", [P, T], F, cn)
            SQ = sb(f"SQ{li}", [P, 4, T], F, cn)
            SU = sb(f"SU{li}", [P, 2, T], F, cn)
            MU = sb(f"MU{li}", [P, T], F, cn)
            RS = sb(f"RS{li}", [P, T], F, cn)
            bank = {}
            done = [None] * len(blocks)

            def evac(i, par, g, tok):
                k0, n, _ = blocks[i]
                while i > 0 and done[i - 1] is None:
                    yield
                r3 = RES[:, k0:k0 + n, :]
                r, gv = flat(r3), g[:, 0:n * T]
                xh, xl = flat(AH[:, k0:k0 + n, :]).bitcast(F), flat(AL[:, k0:k0 + n, :]).bitcast(F)
                t1 = DV(lambda e: e.scalar_tensor_tensor(out=r, in0=xh, scalar=ALPHA, in1=gv, op0=ALU.mult,
                                                         op1=ALU.add), tok)
                release(par, t1)
                t1 = DV(lambda e: e.scalar_tensor_tensor(out=r, in0=xl, scalar=ALPHA, in1=r, op0=ALU.mult,
                                                         op1=ALU.add), t1)
                yield
                if i == 0:
                    yield
                    b, rel = mb.get()
                    PE.wait(rel, t1)
                    for f in range(4):
                        last = ones_sum(M[:, b, 0:T], RES[:, f, :], f == 0, f == 3)
                    tp = pe_end(last)
                    bank["pv"] = AC(lambda e: e.activation(PV[:, :], M[:, b, 0:T], ACT.Copy, scale=1.0 / 512),
                                    tp)
                    mb.put(b, [bank["pv"]])
                    (bank[1], rel1), (bank[2], rel2) = mb.get(), mb.get()
                    PE.wait(rel1, rel2)
                    yield
                t2 = DV(lambda e: e.tensor_tensor(r3, r3, brc(PV[:, :], n), ALU.subtract), t1, bank["pv"])
                t3 = AC(lambda e: e.activation(flat(SQ[:, 0:n, :]), r, ACT.Square), t2, bank.get("sq"))
                first, last_ = i == 0, i == len(blocks) - 1
                if n == 4:
                    t4 = DV(lambda e: e.tensor_tensor(SU[:, :, :], r3[:, 0:2, :], r3[:, 2:4, :], ALU.add),
                            t2, bank.get("sq"))
                    t4 = fold(SU, 2, t4)
                else:
                    t4 = DV(lambda e: e.tensor_tensor(SU[:, 0, :], r3[:, 0, :], r3[:, 1, :], ALU.add),
                            t2, bank.get("sq"))
                yield
                t5 = fold(SQ, n, t3)
                yield 2
                PE.wait(t4)
                ones_sum(M[:, bank[1], 0:T], SU[:, 0, :], first, last_)
                PE.wait(t5)
                bank["sq"] = pe_end(ones_sum(M[:, bank[2], 0:T], SQ[:, 0, :], first, last_))
                done[i] = bank["sq"]

            task(evac(0, *res0))
            for i in range(1, len(blocks)):
                par, g, tok = gemm(blocks[i][2], (YH, YL), yt)
                task(evac(i, par, g, tok))
            drain()
            b1, b2, tp = bank[1], bank[2], bank["sq"]
            t1 = DV(lambda e: e.tensor_scalar(MU[:, :], M[:, b1, 0:T], 1.0 / DM, None, ALU.mult), tp)
            t2 = DV(lambda e: e.tensor_tensor(PV[:, :], MU[:, :], MU[:, :], ALU.mult), t1)
            t3 = DV(lambda e: e.scalar_tensor_tensor(out=RS[:, :], in0=M[:, b2, 0:T], scalar=1.0 / DM,
                                                     in1=PV[:, :], op0=ALU.mult, op1=ALU.subtract), t2)
            mb.put(b1, [t1])
            mb.put(b2, [t3])
            t4 = AC(lambda e: e.activation(RS[:, :], RS[:, :], ACT.Sqrt, bias=eps6[:, 1:2]), t3, t_eps)
            tr = DV(lambda e: e.reciprocal(RS[:, :], RS[:, :]), t4)

            def apply(k, n):
                r3 = RES[:, k:k + n, :]
                t6 = DV(lambda e: e.tensor_tensor(r3, r3, brc(MU[:, :], n), ALU.subtract), t1)
                t7 = DV(lambda e: e.tensor_tensor(r3, r3, brc(RS[:, :], n), ALU.mult), t6, tr)
                return [AC(lambda e: e.activation(RES[:, i, :], RES[:, i, :], ACT.Identity,
                                                  scale=vc("lg", 16 * li + i), bias=vc("lb", 16 * li + i)), t7)
                        for i in range(k, k + n)]
            return apply, SQ, RS

        CHUNKS = ((0, 1), (1, 1), (2, 2), (4, 4), (8, 4), (12, 4))

        res0 = gemm(B_o1[0][2], (YH, YL), yt)
        drain()
        c1.close()
        c2 = ExitStack()
        RES = sb("RES2", [P, 16, T], F, c2)
        f2 = fence()
        for l in (AC, DV):
            l.wait(f2)
        apply, _, _ = ln_blocks(res0, B_o1, yt, RES, c2, 0)
        at = {}
        for k, n in CHUNKS:
            toks = split_act(flat(AH[:, k:k + n, :]), flat(AL[:, k:k + n, :]), flat(RES[:, k:k + n, :]),
                             apply(k, n))
            for i in range(k, k + n):
                at[i] = toks
        f3 = fence()
        c2.close()

        c3 = ExitStack()
        QKB = sb("QKB", [P, 2, 2, 4, T], F, c3)
        VVB = sb("VVB", [P, 2, 2, 512], F, c3)
        SG = sb("SG", [P, 3, 4, T], F, c3)
        OT = sb("OT", [P, 4, T], F, c3)
        CQH = sb("CQH", [P, 4, T], R, c3)
        CQL = sb("CQL", [P, 4, T], R, c3)
        CKH = sb("CKH", [P, 2, T], R, c3)
        CKL = sb("CKL", [P, 2, T], R, c3)
        KI = sb("KI", [P, T], F, c3)
        WT = sb("WT", [P, 2, 16], F, c3)
        SC = sb("SC", [P, 384], F, c3)
        MA = sb("MA", [P, 384], F, c3)
        TRL = sb("TRL", [P, 384], F, c3)
        PXB = sb("PXB", [P, 2, 384], F, c3)
        PT = sb("PT", [P, 384], F, c3)
        M8 = sb("M8", [P, 2, 8], F, c3)
        MXB = sb("MXB", [P, 2, 8], F, c3)
        RQ = sb("RQ", [P, 2, T], F, c3)
        A3 = (AH, AL)
        QI = QKB[:, 1]
        tl = PL(lambda e: e.memset(TRL[:, :], 1.0), f3)
        for o in (0, 256):
            t_trl = PL(lambda e: e.affine_select(out=TRL[:, o:o + P], in_=TRL[:, o:o + P],
                                                 compare_op=ALU.is_ge, fill=0.0, base=0,
                                                 pattern=[[-1, P]], channel_multiplier=1), tl)

        def small_rms(src, n, tsrc, tmp, gname, H, L, ttmp, rq, name):
            t1 = AC(lambda e: e.activation(flat(tmp), flat(src), ACT.Square), tsrc, ttmp)
            yield
            t1 = fold(tmp, n, t1)
            yield 2
            b, rel = mb.get()
            PE.wait(rel, t1)
            tp = pe_end(ones_sum(M[:, b, 0:T], tmp[:, 0, :]))
            yield
            t2 = AC(lambda e: e.activation(rq, M[:, b, 0:T], ACT.Sqrt, scale=1.0 / (n * P),
                                           bias=eps6[:, 0:1]), tp, f3)
            mb.put(b, [t2])
            t3 = DV(lambda e: e.reciprocal(rq, rq), t2)
            for f in range(n):
                t4 = DV(lambda e: e.scalar_tensor_tensor(out=src[:, f, :], in0=src[:, f, :],
                                                         scalar=vc(gname, f), in1=rq,
                                                         op0=ALU.mult, op1=ALU.mult), t3, tsrc)
            yield
            tk[name] = split_act(flat(H[:, :, :]), flat(L[:, :, :]), flat(src), t4)

        class At(dict):

            def __init__(self, name):
                self.name = name

            def __contains__(self, k):
                return self.name in tk

            def __missing__(self, k):
                return tk[self.name]

        def ev_cq(par, g, tok):
            t1 = DV(lambda e: e.tensor_copy(flat(QKB[:, 0, 0]), g), tok, f3)
            release(par, t1)
            yield
            yield from small_rms(QKB[:, 0, 0], 4, t1, QKB[:, 0, 1], "qg", CQH, CQL, f3, RQ[:, 0, :], "cq")

        def ev_ms(par, g, tok):
            t2 = DV(lambda e: e.tensor_copy(flat(OT[:, 0:2, :]), g[:, 0:512]), tok, f3)
            tk["ki"] = DV(lambda e: e.tensor_copy(KI[:, :], g[:, 512:768]), tok)
            t_w = DV(lambda e: e.tensor_copy(VVB[0:16, 0, 0, 0:T], g[0:16, 768:1024]), tok)
            release(par, t_w)
            yield
            yield from small_rms(OT[:, 0:2, :], 2, t2, OT[:, 2:4, :], "kg", CKH, CKL, f3, RQ[:, 1, :], "ck")
            b, rel = mb.get()
            PE.wait(rel, t_w)
            for t in range(2):
                last = nc.tensor.transpose(M[:, b, 16 * t:16 * t + 16], VVB[0:16, 0, 0, t * P:(t + 1) * P],
                                           ident[0:16, 0:16])
            tk["wt"] = DV(lambda e: e.tensor_scalar(WT[:, :, :].rearrange("p a n -> p (a n)"), M[:, b, 0:32],
                                                    0.25, 0.125, ALU.mult, ALU.mult), pe_end(last), f3)
            mb.put(b, [tk["wt"]])

        def ev_gate(j, par, g, tok):
            while j > 2 and ("og", j - 3) not in tk:
                yield
            tk[("sg", j)] = AC(lambda e: e.activation(flat(SG[:, j % 3]), g, ACT.Silu), tok,
                               tk.get(("og", j - 3)), f3)
            release(par, tk[("sg", j)])

        def ev_qi(i, par, g, tok):
            tk[("qi", i)] = DV(lambda e: e.tensor_copy(flat(QI[:, i]), g), tok, f3)
            release(par, tk[("qi", i)])
            yield

        task(ev_cq(*gemm(B_cq, A3, at)))
        task(ev_ms(*gemm(B_ms, A3, at)))
        task(ev_gate(0, *gemm(B_gate[0], A3, at)))
        for i in range(2):
            task(ev_qi(i, *gemm(B_qi[i], (CQH, CQL), At("cq"))))

        def index_scores():
            acc = [None, None]
            RL = PT
            rl_free = None
            while not (("qi", 1) in tk and "wt" in tk):
                yield
            for h in range(16):
                f, o = h // 2, 64 * (h % 2)
                b, rel = mb.get()
                PE.wait(rel, tk[("qi", 0)], tk[("qi", 1)], tk["ki"])
                qh = QI[o:o + 64, f // 4, f % 4, :]
                mm(M[:, b, 0:P], qh[:, 0:P], KI[o:o + 64, 0:P], True, True)
                tp = PE(lambda e: mm(M[:, b, P:P + T], qh[:, P:T], KI[o:o + 64, :], False, True))
                tk["qi_read"] = tp
                yield
                ta = AC(lambda e: e.activation(RL[:, :], M[:, b, 0:384], ACT.Relu), tp, rl_free, f3)
                mb.put(b, [ta])
                for t, (a, z) in enumerate(((0, P), (P, 384))):
                    w = WT[:, t, h:h + 1]
                    if h == 0:
                        acc[t] = DV(lambda e: e.tensor_scalar(SC[:, a:z], RL[:, a:z], w, None, ALU.mult),
                                    ta, tk["wt"], f3)
                    else:
                        acc[t] = DV(lambda e: e.scalar_tensor_tensor(
                            out=SC[:, a:z], in0=RL[:, a:z], scalar=w, in1=SC[:, a:z], op0=ALU.mult,
                            op1=ALU.add), ta, acc[t])
                rl_free = acc[1]
            t1 = DV(lambda e: e.tensor_scalar(MA[:, :], TRL[:, :], -NEG * 1e8, NEG * 1e8, ALU.mult, ALU.add),
                    t_trl, f3)
            t2 = DV(lambda e: e.tensor_tensor(SC[:, :], SC[:, :], TRL[:, :], ALU.mult), acc)
            t3 = DV(lambda e: e.tensor_tensor(SC[:, :], SC[:, :], MA[:, :], ALU.add), t2, t1)
            yield
            tr = [t3, t3]
            for i in range(8):
                tm = [None, None]
                for t, (a, z) in enumerate(((0, P), (P, 384))):
                    tm[t] = DV(lambda e: e.max(M8[:, t, :], SC[:, a:z]), tr[t], f3)
                for t, (a, z) in enumerate(((0, P), (P, 384))):
                    tr[t] = DV(lambda e: e.match_replace(SC[:, a:z], M8[:, t, :], SC[:, a:z], -3.0e38), tm[t])
                yield
            t4 = DV(lambda e: e.tensor_scalar(SC[:, :], SC[:, :], -2.0e38, None, ALU.is_lt), tr)
            t5 = DV(lambda e: e.tensor_tensor(SC[:, :], SC[:, :], TRL[:, :], ALU.mult), t4)
            tk["rl"] = rl_free
            tk["mask"] = DV(lambda e: e.tensor_scalar(MA[:, :], SC[:, :], -NEG, NEG, ALU.mult, ALU.add), t5)

        yt = {}
        PTB = (PT, SC)
        s3 = [{"px": None, "pt": None, "mx": None} for _ in range(2)]
        SCALE = 128.0 ** -0.5

        def attend(j, c):
            while not ("mask" in tk and ("v", j) in tk and (j == 0 or ("pv", j - 1, c) in tk)):
                yield
            QK, VV = QKB[:, j % 2], VVB[:, j % 2]
            PX, PT_, MX, s = PXB[:, c, :], PTB[c], MXB[:, c, :], s3[c]
            spans = ((0, P), (P, 384))
            ot = []
            for h in (c, c + 2):
                b, rel = mb.get()
                PE.wait(rel, tk[("q", j)], tk[("k", j)])
                q, k = QK[:, 0, h, :], QK[:, 1, h, :]
                mm(M[:, b, 0:P], q[:, 0:P], k[:, 0:P], True, True)
                tp = PE(lambda e: mm(M[:, b, P:384], q[:, P:T], k[:, :], False, True))
                tmx = []
                for t, (a, z) in enumerate(spans):
                    tmx.append(DV(lambda e: e.tensor_tensor_reduce(
                        out=PX[:, a:z], in0=M[:, b, a:z], in1=MA[:, a:z], scale=SCALE, scalar=-3.0e38,
                        op0=ALU.add, op1=ALU.max, accum_out=MX[:, t:t + 1]), tp, tk["mask"], s["px"],
                        s["mx"], f3))
                mb.put(b, [tmx[-1]])
                tn = DV(lambda e: e.tensor_scalar(MX[:, 2:4], MX[:, 0:2], -1.0, None, ALU.mult), tmx)
                te = []
                for t, (a, z) in enumerate(spans):
                    te.append(AC(lambda e: e.activation(PX[:, a:z], PX[:, a:z], ACT.Exp, bias=MX[:, 2 + t:3 + t],
                                                        accum_out=MX[:, 4 + t:5 + t]), tn))
                yield
                tr = DV(lambda e: e.reciprocal(MX[:, 6:8], MX[:, 4:6]), te)
                for t, (a, z) in enumerate(spans):
                    ts = DV(lambda e: e.tensor_scalar(PX[:, a:z], PX[:, a:z], MX[:, 6 + t:7 + t], None,
                                                      ALU.mult), tr)
                s["mx"] = ts
                yield
                b, rel = mb.get()
                PE.wait(rel, ts)
                nc.tensor.transpose(M[:, b, 0:P], PX[:, 0:P], ident[:, :])
                nc.tensor.transpose(M[:, b, P:T], PX[:, P:T], ident[:, :])
                tp = PE(lambda e: e.transpose(M[:, b, T:384], PX[:, T:384], ident[:, :]))
                s["px"] = tp
                tc = AC(lambda e: e.copy(PT_[:, :], M[:, b, 0:384]), tp, s["pt"], tk["rl"], tk["mask"])
                mb.put(b, [tc])
                yield
                b, rel = mb.get()
                PE.wait(rel, tc, tk[("v", j)])
                mm(M[:, b, 0:T], VV[:, 0, h * P:(h + 1) * P], PT_[:, 0:T], True, False)
                tp = PE(lambda e: mm(M[:, b, P:T], VV[:, 1, h * P:(h + 1) * P], PT_[:, T:384], False, True))
                s["pt"] = tp
                while j > 0 and ("ot", j - 1) not in tk:
                    yield
                ot.append(DV(lambda e: e.tensor_copy(OT[:, h, :], M[:, b, 0:T]), tp, tk.get(("ot", j - 1)),
                             tk["ck"]))
                mb.put(b, [ot[-1]])
                yield
            tk[("pv", j, c)] = [tp, ot]

        def gated(j):
            while not (("pv", j, 0) in tk and ("pv", j, 1) in tk and ("sg", j) in tk):
                yield
            pv = [tk[("pv", j, 0)], tk[("pv", j, 1)]]
            tk[("qkv_read", j)] = pv
            t1 = DV(lambda e: e.tensor_tensor(OT[:, :, :], OT[:, :, :], SG[:, j % 3], ALU.mult), pv,
                    tk[("sg", j)])
            tk[("og", j)] = t1
            yield
            toks = split_act(flat(YH[:, 4 * j:4 * j + 4, :]), flat(YL[:, 4 * j:4 * j + 4, :]),
                             flat(OT[:, :, :]), t1)
            tk[("ot", j)] = toks
            for f in range(4):
                yt[4 * j + f] = toks

        def kv_gemm(u, values):
            par = gpar[0]
            gpar[0] ^= 1
            take(par)
            split_to(u + NH)
            PE.wait(w_tok[u], get("ck"))
            if values:
                wh = WH[:, u % NH, :].rearrange("p (c m) -> p c m", c=2)
                wl = WL[:, u % NH, :].rearrange("p (c m) -> p c m", c=2)
                for t in range(2):
                    o = G[:, 2 * par + t, :]
                    for c in range(2):
                        xh, xl = CKH[:, c, t * P:(t + 1) * P], CKL[:, c, t * P:(t + 1) * P]
                        mm(o, xh, wh[:, c, :], c == 0, False)
                        mm(o, xh, wl[:, c, :], False, False)
                        last = mm(o, xl, wh[:, c, :], False, c == 1)
            else:
                wh = WH[:, u % NH, :].rearrange("p (h c n) -> p h c n", h=4, c=2)
                wl = WL[:, u % NH, :].rearrange("p (h c n) -> p h c n", h=4, c=2)
                for h in range(4):
                    o = G[:, 2 * par + h // 2, (h % 2) * T:(h % 2 + 1) * T]
                    for c in range(2):
                        mm(o, wh[:, h, c, :], CKH[:, c, :], c == 0 and h % 2 == 0, False)
                        mm(o, wh[:, h, c, :], CKL[:, c, :], False, False)
                        last = mm(o, wl[:, h, c, :], CKH[:, c, :], False, c == 1)
            tok = end_unit(u, last)
            step()
            return par, flat(G[:, 2 * par:2 * par + 2, :]), tok

        def ev_qkv(name, j, dst, par, g, tok, act):
            while (j > 1 and ("qkv_read", j - 2) not in tk) or (j == 1 and "mask" not in tk) or "wt" not in tk:
                yield
            free = tk.get(("qkv_read", j - 2)) if j > 1 else [tk.get("qi_read"), tk["cq"], tk["wt"]]
            if act:
                t = AC(lambda e: e.copy(dst, g), tok, free, f3)
            else:
                t = DV(lambda e: e.tensor_copy(dst, g), tok, free, f3)
            release(par, t)
            tk[(name, j)] = t

        task(index_scores())
        for j in range(8):
            task(ev_qkv("q", j, flat(QKB[:, j % 2, 0]), *gemm(B_qkv[j][0], (CQH, CQL), At("cq")), False))
            task(ev_qkv("k", j, flat(QKB[:, j % 2, 1]), *kv_gemm(B_qkv[j][1], False), True))
            task(ev_qkv("v", j, flat(VVB[:, j % 2]), *kv_gemm(B_qkv[j][2], True), False))
            task(attend(j, 0))
            task(attend(j, 1))
            task(gated(j))
            for i in GATES[j]:
                task(ev_gate(i, *gemm(B_gate[i], A3, at)))
        res0 = gemm(B_o2[0][2], (YH, YL), yt)
        drain()
        f4 = fence()
        c3.close()

        c4 = ExitStack()
        RES = sb("RES4", [P, 16, T], F, c4)
        for l in (AC, DV):
            l.wait(f4)
        apply, SQ, RS = ln_blocks(res0, B_o2, yt, RES, c4, 1)
        d_h = new_ds()

        def rms_sum(i, n, toks, SQ, bank, first, last):
            t1 = AC(lambda e: e.activation(flat(SQ[:, 0:n, :]), flat(RES[:, i:i + n, :]), ACT.Square), toks,
                    bank.get("sq"))
            t1 = fold(SQ, n, t1)
            yield 2
            if first:
                bank["b"], rel = mb.get()
                PE.wait(rel)
            PE.wait(t1)
            bank["sq"] = pe_end(ones_sum(M[:, bank["b"], 0:T], SQ[:, 0, :], first, last))

        def rms_scale(RSX, CS, bank, *toks):
            yield
            t2 = AC(lambda e: e.activation(RSX, M[:, bank["b"], 0:T], ACT.Sqrt, scale=1.0 / DM,
                                           bias=eps6[:, 0:1]), bank["sq"], *toks)
            mb.put(bank["b"], [t2])
            t3 = DV(lambda e: e.reciprocal(RSX, RSX), t2)
            yield 2
            b, rel = mb.get()
            PE.wait(rel, t3)
            for t in range(2):
                last = nc.tensor.transpose(M[:, b, t * P:(t + 1) * P], RSX[:, t * P:(t + 1) * P], ident[:, :])
            t4 = DV(lambda e: e.tensor_copy(CS, M[:, b, 0:T].rearrange("p (t n) -> p t n", t=2)[:, :, 0]),
                    pe_end(last), *toks)
            mb.put(b, [t4])
            return t3, t4

        def scaled(src, gname, g0, k, n, GH, toks, free):
            for i in range(n):
                t = DV(lambda e: e.tensor_scalar(GH[:, i, :], src[:, i, :], vc(gname, g0 + k + i), None,
                                                 ALU.mult), toks, free)
            return split_act(flat(AH[:, k:k + n, :]), flat(AL[:, k:k + n, :]), flat(GH[:, 0:n, :]), t)

        GH = sb("GH4", [P, 4, T], F, c4)
        at = {}
        free = None
        applied = []
        for k, n in CHUNKS:
            ta = apply(k, n)
            applied.append((k, n, ta))
            free = scaled(RES[:, k:k + n, :], "n2", 0, k, n, GH, ta, free)
            t_hd = dma(d_h, h_d[:, k * T:(k + n) * T], flat(RES[:, k:k + n, :]), ta)
            for i in range(k, k + n):
                at[i] = free
        bank = {}

        def rms4():
            for i, (k, n, ta) in enumerate(applied):
                yield from rms_sum(k, n, ta, SQ, bank, i == 0, i == len(applied) - 1)
            tk["r5"], tk["c5"] = yield from rms_scale(RSK[:, :], CC[:, 0:2], bank)

        task(rms4())
        v0 = gemm(B_v[0], (AH, AL), at, token_major=True)
        drain()
        f5 = fence() + [t_hd]
        c4.close()
        c5 = ExitStack()
        V = sb("V5", [P, 2, 4096], F, c5)
        U = sb("U5", [P, 4, T], F, c5)
        Z = sb("Z5", [P, 4, T], F, c5)
        WS = sb("WS5", [P, 2, P], F, c5)
        WM = sb("WM5", [P, 2, P], F, c5)
        WR = sb("WR5", [P, 2, 2, P], F, c5)
        BS = sb("BS5", [P, 2, P], F, c5)
        VS5 = sb("VS5", [P, 2, 8], F, c5)
        VR = sb("VR5", [P, 2], F, c5)
        tvb = []
        s5 = {"vs0": None, "vs1": None, "ws": f5, "wr": None, "bs": f5, "z": None, "u": None}

        def ev_v(j, par, g, tok):
            for t in range(2):
                tv = AC(lambda e: e.activation(V[:, t, 512 * j:512 * j + 512], g[:, 512 * t:512 * t + 512],
                                               ACT.Gelu_apprx_tanh, scale=C5[:, t:t + 1]), tok, f5, t_r5)
                tvb.append(tv)
                ts = DV(lambda e: e.tensor_tensor_reduce(
                    out=flat(U[:, 2 * t:2 * t + 2, :]),
                    in0=V[:, t, 512 * j:512 * j + 512], in1=V[:, t, 512 * j:512 * j + 512], scale=1.0,
                    scalar=0.0, op0=ALU.mult, op1=ALU.add, accum_out=VS5[:, t, j:j + 1]), tv, f5,
                    s5[f"vs{t}"])
                s5[f"vs{t}"] = ts
            release(par, tv)
            if j == 7:
                t1 = DV(lambda e: e.tensor_reduce(VR[:, :], VS5[:, :, :], AX.X, ALU.add), s5["vs0"], s5["vs1"])
                t2 = AC(lambda e: e.activation(VR[:, :], VR[:, :], ACT.Sqrt, scale=1.0 / 4096,
                                               bias=eps6[:, 0:1]), t1)
                tk["vr"] = DV(lambda e: e.reciprocal(VR[:, :], VR[:, :]), t2)
                s5["u"] = t1
            yield

        C5, R5 = CC[:, 0:2], RSK
        t_r5 = [tk["r5"], tk["c5"]]
        task(ev_v(0, *v0))
        for j in range(1, 8):
            task(ev_v(j, *gemm(B_v[j], (AH, AL), at, token_major=True)))
        yt = {}
        d_ws, d_bs = new_ds(), new_ds()

        def mix_w(j):
            while j > 0 and ("mixed", j - 1) not in tk:
                yield
            tw = dma(d_ws, WS[:, :, :], A["a_w_s_2"][0, 2 * j:2 * j + 2].rearrange("g t s -> t g s"), s5["ws"])
            tk[("bs", j)] = dma(d_bs, BS[:, :, :].rearrange("p g t -> p (g t)"),
                                A["a_b_s_2"][0, 2 * j:2 * j + 2].rearrange("g t -> (g t)")
                                .partition_broadcast(P), s5["bs"])
            yield
            yield
            b, rel = mb.get()
            PE.wait(rel, tw)
            for q in range(2):
                last = nc.tensor.transpose(M[:, b, q * P:(q + 1) * P], WS[:, q, :], ident[:, :])
            tp = pe_end(last)
            s5["ws"] = tp
            tm = DV(lambda e: e.tensor_tensor(WM[:, :, :], M[:, b, 0:T].rearrange("p (g t) -> p g t", g=2),
                                              brc(triu[:, 0:P], 2), ALU.mult), tp, f5)
            mb.put(b, [tm])
            yield
            while "vr" not in tk:
                yield
            for n in range(2):
                tk[("wr", j)] = DV(lambda e: e.tensor_scalar(WR[:, n], WM[:, :, :], VR[:, n:n + 1], None,
                                                             ALU.mult), tm, tk["vr"], s5["wr"])

        def ev_u(j, par, g, tok):
            while not (("wr", j) in tk and "vr" in tk and (j == 0 or ("yt5", j - 1) in tk)):
                yield
            t0 = DV(lambda e: e.tensor_tensor(U[:, :, :], g.rearrange("p (a n) -> p a n", a=4),
                                              brc(R5[:, :], 4), ALU.mult), tok, s5["u"], t_r5)
            release(par, t0)
            yield
            tu = AC(lambda e: e.activation(flat(U[:, :, :]), flat(U[:, :, :]), ACT.Gelu_apprx_tanh), t0)
            yield
            uz = []
            for f in range(4):
                b, rel = mb.get()
                PE.wait(rel, tk[("wr", j)], tvb)
                c = 4 * j + f
                for n in range(2):
                    last = mm(M[:, b, n * P:(n + 1) * P], V[:, n, c * P:(c + 1) * P], WR[:, n, f // 2, :],
                              n == 0, True)
                tp = pe_end(last)
                s5["wr"] = tp
                m3 = M[:, b, 0:T].rearrange("p (n t) -> p n t", n=2)
                z3 = Z[:, f, :].rearrange("p (n t) -> p n t", n=2)
                tmx = DV(lambda e: e.scalar_tensor_tensor(out=z3, in0=m3, scalar=vc("vg", c),
                                                          in1=brc(BS[:, f // 2, :], 2), op0=ALU.mult,
                                                          op1=ALU.add), tp, tk[("bs", j)], s5["z"], f5)
                mb.put(b, [tmx])
                uz.append(tmx)
                yield
            s5["bs"] = tmx
            t1 = DV(lambda e: e.tensor_tensor(Z[:, :, :], Z[:, :, :], U[:, :, :], ALU.mult), uz, tu)
            s5["u"] = t1
            tk[("mixed", j)] = t1

        def ev_z(j, par, g, tok):
            while ("mixed", j) not in tk:
                yield
            t0 = DV(lambda e: e.tensor_tensor(U[:, :, :], g.rearrange("p (a n) -> p a n", a=4),
                                              brc(R5[:, :], 4), ALU.mult), tok, s5["u"])
            release(par, t0)
            yield
            tz = AC(lambda e: e.activation(flat(U[:, :, :]), flat(U[:, :, :]), ACT.Silu), t0)
            yield
            ty = DV(lambda e: e.tensor_tensor(Z[:, :, :], Z[:, :, :], U[:, :, :], ALU.mult), tz,
                    tk[("mixed", j)])
            s5["u"] = ty
            yield
            toks = split_act(flat(YH[:, 4 * j:4 * j + 4, :]), flat(YL[:, 4 * j:4 * j + 4, :]),
                             flat(Z[:, :, :]), ty)
            s5["z"] = toks
            for f in range(4):
                yt[4 * j + f] = toks
            tk[("yt5", j)] = toks

        for j in range(8):
            task(mix_w(j))
            task(ev_u(j, *gemm(B_uz[j][0], (AH, AL), at)))
            task(ev_z(j, *gemm(B_uz[j][1], (AH, AL), at)))
        res0 = gemm(B_o3[0][2], (YH, YL), yt)
        drain()
        f6 = fence()
        c5.close()

        c6 = ExitStack()
        RES = sb("RES6", [P, 16, T], F, c6)
        RS7 = RSK
        c6b = ExitStack()
        SQ6 = sb("SQ6", [P, 4, T], F, c6b)
        GH6 = sb("GH6", [P, 4, T], F, c6b)
        t_hr = dma(new_ds(), flat(RES[:, :, :]), h_d[:, :], f6, t_hd)
        for l in (AC, DV):
            l.wait(f6)
        at = {}
        s6 = {"gh": None}
        bank = {}

        def ev_o3(i, par, g, tok):
            k, n, _ = B_o3[i]
            while i > 0 and ("o3", i - 1) not in tk:
                yield
            r = flat(RES[:, k:k + n, :])
            t1 = DV(lambda e: e.tensor_tensor(r, r, g[:, 0:n * T], ALU.add), tok, t_hr)
            release(par, t1)
            yield
            s6["gh"] = scaled(RES[:, k:k + n, :], "n2", 16, k, n, GH6, t1, s6["gh"])
            for f in range(n):
                at[k + f] = s6["gh"]
            tk[("o3", i)] = t1
            yield
            if i > 0:
                while ("sum", i - 1) not in tk:
                    yield
            yield from rms_sum(k, n, t1, SQ6, bank, i == 0, i == len(B_o3) - 1)
            tk[("sum", i)] = True
            if i == len(B_o3) - 1:
                tk["r7"], tk["c7"] = yield from rms_scale(RS7[:, :], CC[:, 2:4], bank)

        task(ev_o3(0, *res0))
        for i in range(1, len(B_o3)):
            task(ev_o3(i, *gemm(B_o3[i][2], (YH, YL), yt)))

        q0 = gemm(B_at[0][0], (AH, AL), at)
        drain()
        f7 = fence()
        c6b.close()
        c7 = ExitStack()
        Q7 = sb("Q7", [P, 4, T], F, c7)
        K7 = sb("K7", [P, 4, T], F, c7)
        V7 = sb("V7", [P, 2, 512], F, c7)
        Z7 = sb("Z7", [P, 4, T], F, c7)
        O7 = sb("O7", [P, 4, T], F, c7)
        ZMB = sb("ZMB", [P, 2, 384], F, c7)
        LSB = sb("LSB", [P, 2, 384], F, c7)
        SPB = sb("SPB", [P, 2, 384], F, c7)
        NM = sb("NM", [P, 384], F, c7)
        TG = sb("TG", [P, P], F, c7)
        HT = sb("HT", [P, 2, 512], F, c7)
        tn = PL(lambda e: e.memset(NM[:, :], 0.0), f7)
        for o in (0, 256):
            t_nm = PL(lambda e: e.affine_select(out=NM[:, o:o + P], in_=NM[:, o:o + P],
                                                compare_op=ALU.is_gt, fill=NEG, base=0,
                                                pattern=[[1, P]], channel_multiplier=-1), tn)
        tg = PL(lambda e: e.memset(TG[:, :], 1.0), f7)
        t_tg = PL(lambda e: e.affine_select(out=TG[:, :], in_=TG[:, :], compare_op=ALU.is_ge, fill=0.0,
                                            base=0, pattern=[[-1, P]], channel_multiplier=1), tg)
        yt = {}
        s7 = {"z": None, "ht": None}
        s7c = [{"zm": None, "sp": None, "ls": None} for _ in range(2)]

        def stick(j, c):
            while not (("v7", j) in tk and (j == 0 or ("s7", j - 1, c) in tk)):
                yield
            ZM, LS, SPX, s = ZMB[:, c, :], LSB[:, c, :], SPB[:, c, :], s7c[c]
            ot = []
            for h in (c, c + 2):
                b, rel = mb.get()
                PE.wait(rel, tk[("q7", j)], tk[("k7", j)])
                q, k = Q7[:, h, :], K7[:, h, :]
                mm(M[:, b, 0:T], k[:, 0:P], q[:, :], True, True)
                tp = PE(lambda e: mm(M[:, b, T:384], k[:, P:T], q[:, P:T], False, True))
                t1 = DV(lambda e: e.scalar_tensor_tensor(out=ZM[:, :], in0=M[:, b, 0:384], scalar=SCALE,
                                                         in1=NM[:, :], op0=ALU.mult, op1=ALU.add),
                        tp, t_nm, s["zm"], f7)
                mb.put(b, [t1])
                t2 = DV(lambda e: e.scalar_tensor_tensor(out=LS[:, :], in0=ZM[:, :], scalar=-1.0,
                                                         in1=ZM[:, :], op0=ALU.mult, op1=ALU.max),
                        t1, s["ls"], f7)
                t3 = AC(lambda e: e.activation(LS[:, :], LS[:, :], ACT.Exp, scale=-1.0), t2)
                t4 = AC(lambda e: e.activation(LS[:, :], LS[:, :], ACT.Ln, bias=1.0), t3)
                yield
                t5 = DV(lambda e: e.scalar_tensor_tensor(out=SPX[:, :], in0=ZM[:, :], scalar=0.0,
                                                         in1=LS[:, :], op0=ALU.max, op1=ALU.add),
                        t4, s["sp"], f7)
                yield
                b, rel = mb.get()
                PE.wait(rel, t5, t_tg)
                mm(M[:, b, 0:T], TG[:, :], SPX[:, 0:T], True, False)
                mm(M[:, b, P:T], ones[:, :], SPX[:, T:384], False, True)
                tp = PE(lambda e: mm(M[:, b, T:384], TG[:, :], SPX[:, T:384], False, True))
                s["sp"] = tp
                t6 = DV(lambda e: e.tensor_tensor(ZM[:, :], ZM[:, :], M[:, b, 0:384], ALU.subtract), tp)
                mb.put(b, [t6])
                t7 = AC(lambda e: e.activation(LS[:, :], ZM[:, :], ACT.Exp), t6, t5)
                s["zm"] = t7
                yield
                b, rel = mb.get()
                PE.wait(rel, t7, tk[("v7", j)])
                mm(M[:, b, 0:T], V7[:, 0, h * P:(h + 1) * P], LS[:, 0:T], True, False)
                tp = PE(lambda e: mm(M[:, b, P:T], V7[:, 1, h * P:(h + 1) * P], LS[:, T:384], False, True))
                s["ls"] = tp
                while j > 0 and ("o7", j - 1) not in tk:
                    yield
                ot.append(AC(lambda e: e.copy(O7[:, h, :], M[:, b, 0:T]), tp, tk.get(("o7", j - 1)), f7))
                mb.put(b, [ot[-1]])
                yield
            tk[("s7", j, c)] = [tp, ot]

        def gated7(j):
            while not (("s7", j, 0) in tk and ("s7", j, 1) in tk and ("z7", j) in tk):
                yield
            t1 = DV(lambda e: e.tensor_tensor(O7[:, :, :], O7[:, :, :], Z7[:, :, :], ALU.mult),
                    tk[("z7", j)], tk[("s7", j, 0)], tk[("s7", j, 1)])
            s7["z"] = t1
            yield
            toks = split_act(flat(YH[:, 4 * j:4 * j + 4, :]), flat(YL[:, 4 * j:4 * j + 4, :]),
                             flat(O7[:, :, :]), t1)
            for f in range(4):
                yt[4 * j + f] = toks
            tk[("o7", j)] = toks

        def ev7(name, j, dst, par, g, tok):
            while j > 0 and not (("s7", j - 1, 0) in tk and ("s7", j - 1, 1) in tk):
                yield
            free = [tk.get(("s7", j - 1, c)) for c in range(2)]
            if name == "v7":
                for t in range(2):
                    t1 = DV(lambda e: e.tensor_scalar(dst[:, t, :], g[:, 512 * t:512 * t + 512],
                                                      CC[:, 2 + t:3 + t], None, ALU.mult), tok, free, f7,
                            tk["c7"])
            else:
                t1 = DV(lambda e: e.tensor_tensor(dst, g.rearrange("p (a n) -> p a n", a=4),
                                                  brc(RS7[:, :], 4), ALU.mult), tok, free, f7, tk["r7"])
            release(par, t1)
            tk[(name, j)] = t1

        def ev7z(j, par, g, tok):
            while j > 0 and ("o7", j - 1) not in tk:
                yield
            t1 = DV(lambda e: e.tensor_tensor(Z7[:, :, :], g.rearrange("p (a n) -> p a n", a=4),
                                              brc(RS7[:, :], 4), ALU.mult), tok, f7, tk["r7"], s7["z"])
            release(par, t1)
            yield
            tk[("z7", j)] = AC(lambda e: e.activation(flat(Z7[:, :, :]), flat(Z7[:, :, :]), ACT.Silu), t1)

        d_ht = new_ds()

        def turn_h():
            for j in range(4):
                for t in range(2):
                    b, rel = mb.get()
                    PE.wait(rel)
                    for f in range(4):
                        last = nc.tensor.transpose(M[:, b, f * P:(f + 1) * P],
                                                   RES[:, 4 * j + f, t * P:(t + 1) * P], ident[:, :])
                    tc = DV(lambda e: e.tensor_copy(HT[:, t, :], M[:, b, :]), pe_end(last), s7["ht"], f7)
                    mb.put(b, [tc])
                    yield
                s7["ht"] = dma(d_ht, h2_d[:, j, :, :].rearrange("t p n -> p t n"), HT[:, :, :], tc)

        for j in range(4):
            if j == 0:
                task(ev7("q7", 0, Q7[:, :, :], *q0))
            else:
                task(ev7("q7", j, Q7[:, :, :], *gemm(B_at[j][0], (AH, AL), at)))
            task(ev7("k7", j, K7[:, :, :], *gemm(B_at[j][1], (AH, AL), at)))
            task(ev7("v7", j, V7[:, :, :], *gemm(B_at[j][2], (AH, AL), at, token_major=True)))
            task(stick(j, 0))
            task(stick(j, 1))
            task(gated7(j))
            if j == 0:
                task(turn_h())
            task(ev7z(j, *gemm(B_at[j][3], (AH, AL), at)))
        res0 = gemm(B_o4[0], (YH, YL), yt, token_major=True)
        drain()
        f8 = fence()
        c7.close()

        c8 = ExitStack()
        OUT = sb("OUT8", [P, 2, DM], F, c8)
        FG = sb("FG8", [P, DM], F, c8)
        TT = sb("TT8", [P, 512], F, c8)
        SS = sb("SS8", [P, 2, 4], F, c8)
        RR = sb("RR8", [P, 2], F, c8)
        t_fg = dma(new_ds(), FG[:, :], A["final_g_2"].partition_broadcast(P), f8)
        t_o = dma(new_ds(), OUT[:, :, :].rearrange("p t (j n) -> p t j n", j=4),
                  h2_d[:, :, :, :].rearrange("t j p n -> p t j n"), f8, s7["ht"])
        tsq = [None, None]

        def ev_o(j, par, g, tok):
            for t in range(2):
                o = OUT[:, t, 512 * j:512 * j + 512]
                tc = DV(lambda e: e.tensor_tensor(o, o, g[:, 512 * t:512 * t + 512], ALU.add), tok, t_o)
                tsq[t] = DV(lambda e: e.tensor_tensor_reduce(
                    out=TT[:, :], in0=o, in1=o, scale=1.0, scalar=0.0, op0=ALU.mult, op1=ALU.add,
                    accum_out=SS[:, t, j:j + 1]), tc, tsq, f8)
            release(par, tc)
            yield

        task(ev_o(0, *res0))
        for j in range(1, 4):
            task(ev_o(j, *gemm(B_o4[j], (YH, YL), yt, token_major=True)))
        drain()
        d_o = new_ds()
        for t in range(2):
            t1 = DV(lambda e: e.tensor_reduce(RR[:, t:t + 1], SS[:, t, :], AX.X, ALU.add), tsq)
            t2 = AC(lambda e: e.activation(RR[:, t:t + 1], RR[:, t:t + 1], ACT.Sqrt, scale=1.0 / DM,
                                           bias=eps6[:, 0:1]), t1)
            t3 = DV(lambda e: e.reciprocal(RR[:, t:t + 1], RR[:, t:t + 1]), t2)
            for q in range(2):
                o = OUT[:, t, 1024 * q:1024 * q + 1024]
                t4 = DV(lambda e: e.scalar_tensor_tensor(out=o, in0=o, scalar=RR[:, t:t + 1],
                                                         in1=FG[:, 1024 * q:1024 * q + 1024],
                                                         op0=ALU.mult, op1=ALU.mult), t3, t_fg)
                t5 = dma(d_o, out[0, t * P:(t + 1) * P, 1024 * q:1024 * q + 1024], o, t4)
        SP.wait(t5)
        SP.wait(t_hd, tk["csd"], s7["ht"])
        c8.close()
        c6.close()
        cy.close()


_INS = ['x', 'ssd_w_in', 'ssd_conv_w', 'ssd_conv_b', 'ssd_dt_bias', 'ssd_a_log', 'ssd_d_skip',
        'ssd_norm_g', 'ssd_w_out', 'dsa_w_in', 'dsa_q_norm_g', 'dsa_kv_norm_g', 'dsa_w_uq', 'dsa_w_uk',
        'dsa_w_uv', 'dsa_w_idx_q', 'dsa_w_out', 'ln_g', 'ln_b', 'norm_g_2', 'a_w_in_2', 'a_v_norm_g_2',
        'a_w_s_2', 'a_b_s_2', 'a_w_out_2', 'b_w_in_2', 'b_w_out_2', 'final_g_2']


def kernel(**inputs):
    import numpy as _np
    import concourse.bacc as _bacc
    from concourse import mybir as _mybir
    from concourse.bass_utils import run_bass_kernel_spmd as _run

    nc = _bacc.Bacc("TRN2", target_bir_lowering=False, num_devices=1)
    arrays, args = {}, {}
    for name in _INS:
        a = _np.ascontiguousarray(inputs[name])
        arrays[f"in_{name}"] = a
        args[name] = nc.dram_tensor(f"in_{name}", a.shape, _mybir.dt.from_np(a.dtype), kind="ExternalInput").ap()
    out = nc.dram_tensor("out_0", (1, 256, 2048), _mybir.dt.float32, kind="ExternalOutput").ap()
    build(nc, args, out)
    r = _run(nc, [arrays], core_ids=[0])
    return r.results[0]["out_0"]
```

```python
from collections import deque
from contextlib import ExitStack

import numpy as np

import concourse.bass as bass
from concourse import mybir

F = mybir.dt.float32
R = mybir.dt.float32r
ALU = mybir.AluOpType
ACT = mybir.ActivationFunctionType
AX = mybir.AxisListType

P = 128
T = 256
DM = 2048
NR = 4
NH = 3
UW = 1024
STEP = 8
ALPHA = 4.0 ** 0.25
LN_EPS = 1e-5
RMS_EPS = 1e-6
NEG = -1.0e30


class Line:

    def __init__(self, eng, sem):
        self.eng, self.sem, self.n, self.seen = eng, sem, 0, {}

    def wait(self, *toks):
        for t in toks:
            if t is None:
                continue
            if isinstance(t, list):
                self.wait(*t)
                continue
            sem, v = t
            if self.seen.get(sem.name, 0) < v:
                self.seen[sem.name] = v
                self.eng.wait_ge(sem, v)

    def __call__(self, fn, *toks):
        self.wait(*toks)
        fn(self.eng).then_inc(self.sem, 1)
        self.n += 1
        return (self.sem, self.n)


class DmaSem:
    def __init__(self, sem):
        self.sem, self.n = sem, 0


class Banks:

    def __init__(self, ids):
        self.free = deque((i, []) for i in ids)

    def get(self):
        return self.free.popleft()

    def put(self, i, toks):
        self.free.append((i, toks))


def build(nc, A, out):
    ctx = ExitStack()
    with ctx:
        def sb(name, shape, dt=F, c=None):
            return (c or ctx).enter_context(nc.sbuf_tensor(name, shape, dt))

        def sem(name):
            return ctx.enter_context(nc.semaphore(name))

        PE = Line(nc.tensor, sem("s_pe"))
        AC = Line(nc.scalar, sem("s_act"))
        DV = Line(nc.vector, sem("s_dve"))
        PL = Line(nc.gpsimd, sem("s_pool"))
        SP = Line(nc.sync, sem("s_sp"))

        def dma(ds, dst, src, *toks, line=None):
            ln = line or SP
            ln.wait(*toks)
            ln.eng.dma_start(dst, src).then_inc(ds.sem, 16)
            ds.n += 16
            return (ds.sem, ds.n)

        d_raw = [DmaSem(sem(f"d_raw{i}")) for i in range(NR)]
        n_ds = [0]

        def new_ds():
            n_ds[0] += 1
            return DmaSem(sem(f"d_m{n_ds[0]}"))

        G = ctx.enter_context(nc.psum_tensor("G", [P, 4, 512], F))
        M = ctx.enter_context(nc.psum_tensor("M", [P, 4, 512], F))
        mb = Banks(range(4))
        grel = [[], []]
        gpar = [0]

        RAW = sb("RAW", [P, NR, UW])
        def w_pair(name, c=None):
            return sb(f"WH{name}", [P, UW], R, c), sb(f"WL{name}", [P, UW], R, c)

        w_slots = deque((w_pair(i), None) for i in range(NH))
        n_slots = [NH]
        spare, leaving, slot_end = {}, [], {}
        AH = sb("AH", [P, 16, T], R)
        AL = sb("AL", [P, 16, T], R)
        TB = sb("TB", [P, 2])
        ident = sb("ident", [P, P])
        ones = sb("ones", [P, P])
        triu = sb("triu", [P, 384])
        VC = sb("VC", [P, 4, P])
        dcol = sb("dcol", [P, 32])
        eps6 = sb("eps6", [P, 2])
        RSK = sb("RSK", [P, T])
        CC = sb("CC", [P, 4])
        DB = sb("DB", [P, 64])
        alog = sb("alog", [64, 1])
        dtb = sb("dtb", [64, 1])

        units = []

        def plan(wap, r0, K, cols, width):
            nk = UW // width
            nt = K // P
            blk = []
            k = 0
            while k < nt:
                n = min(nk, nt - k)
                pieces = []
                for c0, cn, o in cols:
                    src = wap[r0 + k * P:r0 + (k + n) * P, c0:c0 + cn].rearrange(
                        "(k p) n -> p k n", p=P)
                    pieces.append((0, n, width, o, cn, src))
                units.append(pieces)
                blk.append((len(units) - 1, list(range(k, k + n))))
                k += n
            return blk, width

        def plan_pair(blocks, i, n):
            pair = [blocks[i + q][-1] if len(blocks[i]) == 3 else blocks[i + q] for q in range(2)]
            order = [(q, v) for q, vs in ((0, range(n)), (1, range(n)), (0, range(n, len(pair[0][0]))),
                                          (1, range(n, len(pair[1][0])))) for v in vs]
            first = pair[0][0][0][0]
            old = [units[pair[q][0][v][0]] for q, v in order]
            for x, (q, v) in enumerate(order):
                units[first + x] = old[x]
                pair[q][0][v] = (first + x, pair[q][0][v][1])

        def plan_rows(wap, row0):
            src = wap[row0:row0 + 1024, :].rearrange("(q p) n -> p q n", p=P)
            units.append([(0, 8, 128, 0, 128, src)])
            return len(units) - 1

        def plan_values(wap, row0):
            src = wap[row0:row0 + 1024, :].rearrange("(h c p) n -> c p h n", p=P, c=2)
            units.append([(512 * c, 4, 128, 0, 128, src[c]) for c in range(2)])
            return len(units) - 1

        def plan_out(wap):
            return [(f, n, plan(wap, 0, 4096, [(P * f, P * n, 0)], P * n))
                    for f, n in ((0, 4), (4, 4), (8, 4), (12, 2), (14, 1), (15, 1))]

        fetched, ready = [0], [0]
        raw_tok, raw_free, w_tok, w_at = {}, {}, {}, {}

        def fetch_to(n):
            while fetched[0] < min(n, len(units)):
                u = fetched[0]
                s = u % NR
                for a0, nk, width, o, cn, src in units[u]:
                    dst = RAW[:, s, a0:a0 + nk * width].rearrange("p (k n) -> p k n", k=nk)[:, :, o:o + cn]
                    raw_tok[u] = dma(d_raw[s], dst, src, raw_free.get(u - NR))
                fetched[0] += 1

        def split_ahead(u0):
            while ready[0] < min(u0 + n_slots[0], len(units)) and w_slots:
                u = ready[0]
                fetch_to(u + 1)
                r = u % NR
                w_at[u], free = w_slots.popleft()
                wh, wl = w_at[u]
                n = max(p[1] * p[2] for p in units[u]) if len(units[u]) == 1 else UW
                ta = AC(lambda e: e.copy(wh[:, 0:n], RAW[:, r, 0:n]), raw_tok[u], free)
                td = DV(lambda e: e.tensor_tensor(wl[:, 0:n], RAW[:, r, 0:n], wh[:, 0:n].bitcast(F),
                                                  ALU.subtract), ta, raw_tok[u], free)
                raw_free[u] = [ta, td]
                w_tok[u] = [ta, td]
                ready[0] += 1
                fetch_to(u + NR)

        def add_slot(name, pair, *toks):
            n_slots[0] += 1
            spare[name] = pair
            w_slots.append((pair, list(toks)))

        def drop_slot(name):
            n_slots[0] -= 1
            for x in list(w_slots):
                if x[0] is spare[name]:
                    w_slots.remove(x)
                    slot_end[name] = x[1]
                    return
            leaving.append(name)

        bg = deque()

        tick = [0]

        def task(gen):
            bg.append([gen, 0])

        def advance(t):
            try:
                t[1] = tick[0] + (next(t[0]) or 1)
            except StopIteration:
                bg.remove(t)

        def step():
            tick[0] += 1
            n = DV.n
            for t in list(bg):
                if t[1] <= tick[0] and DV.n - n < STEP:
                    advance(t)

        def now(gen):
            bg.append([gen, 0])
            advance(bg[-1])

        def drain():
            while bg:
                step()

        def mm(o, l, r, start, stop_):
            return nc.tensor.matmul(o, l, r, start=start, stop=stop_, skip_group_check=True)

        def end_unit(u, last):
            last.then_inc(PE.sem, 1)
            PE.n += 1
            gone = [x for x in leaving if w_at[u] is spare[x]]
            if gone:
                leaving.remove(gone[0])
                slot_end[gone[0]] = (PE.sem, PE.n)
            else:
                w_slots.append((w_at[u], (PE.sem, PE.n)))
            return (PE.sem, PE.n)

        def gemm_open(blk):
            step()
            par = gpar[0]
            gpar[0] ^= 1
            take(par)
            return [par, blk, 0]

        def gemm_run(job, a, at, token_major=False, n=None):
            par, (us, width), done = job
            ah, al = a
            nk = us[-1][1][-1] + 1
            todo = us[done:] if n is None else us[done:done + n]
            job[2] += len(todo)
            for u, kts in todo:
                split_ahead(u)
                PE.wait(w_tok[u])
                wh = w_at[u][0][:, 0:len(kts) * width].rearrange("p (k n) -> p k n", k=len(kts))
                wl = w_at[u][1][:, 0:len(kts) * width].rearrange("p (k n) -> p k n", k=len(kts))
                for i, k in enumerate(kts):
                    while k not in at:
                        step()
                    PE.wait(at[k])
                    lastk = k == nk - 1
                    if token_major:
                        for t in range(2):
                            o = G[:, 2 * par + t, 0:width]
                            xh, xl = ah[:, k, t * P:(t + 1) * P], al[:, k, t * P:(t + 1) * P]
                            mm(o, xh, wh[:, i, :], k == 0, False)
                            mm(o, xh, wl[:, i, :], False, False)
                            last = mm(o, xl, wh[:, i, :], False, lastk)
                    else:
                        for f in range(width // P):
                            o = G[:, 2 * par + f // 2, (f % 2) * T:(f % 2 + 1) * T]
                            h, l = wh[:, i, f * P:(f + 1) * P], wl[:, i, f * P:(f + 1) * P]
                            mm(o, h, ah[:, k, :], k == 0 and f % 2 == 0, False)
                            mm(o, h, al[:, k, :], False, False)
                            last = mm(o, l, ah[:, k, :], False, lastk)
                tok = end_unit(u, last)
                if not lastk:
                    step()
            return par, flat(G[:, 2 * par:2 * par + 2, :]), tok

        def gemm(blk, a, at, token_major=False):
            return gemm_run(gemm_open(blk), a, at, token_major)

        def take(par):
            while grel[par] is None:
                step()
            PE.wait(grel[par])
            grel[par] = None

        def release(par, *toks):
            grel[par] = list(toks)

        def pe_end(last):
            last.then_inc(PE.sem, 1)
            PE.n += 1
            return (PE.sem, PE.n)

        def flat(ap):
            return ap.rearrange("p a n -> p (a n)")

        def split_act(h, l, src, *toks):
            ta = AC(lambda e: e.copy(h, src), *toks)
            td = DV(lambda e: e.tensor_tensor(l, src, h.bitcast(F), ALU.subtract), ta, *toks)
            return [ta, td]

        ssd_in = A["ssd_w_in"][0]
        B_bc = [plan(ssd_in, 0, DM, [(8192, 512, 0)], 512)]
        B_dt = plan(ssd_in, 0, DM, [(10240, 64, 0), (10240, 64, 64)], 128)
        B_bc += [plan(ssd_in, 0, DM, [(8192 + 512 * i, 512, 0)], 512) for i in range(1, 4)]
        B_xz = []
        for g in range(8):
            B_xz.append((plan(ssd_in, 0, DM, [(4096 + 512 * g, 512, 0)], 512),
                         plan(ssd_in, 0, DM, [(512 * g, 512, 0)], 512)))
        B_o1 = plan_out(A["ssd_w_out"][0])
        plan_pair(B_o1, 0, 14)
        din = A["dsa_w_in"][0]
        uq, uk, uv = A["dsa_w_uq"][0], A["dsa_w_uk"][0], A["dsa_w_uv"][0]
        uk = uk.rearrange("h c d -> (h c) d")
        uv = uv.rearrange("h c d -> (h c) d")

        def p_gate(j):
            return plan(din, 0, DM, [(848 + 512 * j, 512, 0)], 512)

        B_cq = plan(din, 0, DM, [(0, 512, 0)], 512)
        B_ms = plan(din, 0, DM, [(512, 384, 0)], 384)
        GATES = ((1, 2), (3,), (4,), (5,), (6,), (7,), (), ())
        B_gate = {0: p_gate(0)}
        B_qi = [plan(A["dsa_w_idx_q"][0], 0, 512, [(512 * i, 512, 0)], 512) for i in range(2)]
        B_qkv = []
        for j in range(8):
            B_qkv.append((plan(uq, 0, 512, [(512 * j, 512, 0)], 512),
                          plan_rows(uk, 1024 * j), plan_values(uv, 1024 * j)))
            for i in GATES[j]:
                B_gate[i] = p_gate(i)
        B_o2 = plan_out(A["dsa_w_out"][0])
        ain = A["a_w_in_2"][0]
        B_v = [plan(ain, 0, DM, [(4096 + 512 * j, 512, 0)], 512) for j in range(8)]
        B_uz = [(plan(ain, 0, DM, [(512 * j, 512, 0)], 512),
                 plan(ain, 0, DM, [(8192 + 512 * j, 512, 0)], 512)) for j in range(8)]
        B_o3 = plan_out(A["a_w_out_2"][0])
        bin_ = A["b_w_in_2"][0]
        B_at = [[plan(bin_, 0, DM, [(2048 * c + 512 * j, 512, 0)], 512) for c in range(4)]
                for j in range(4)]
        OUTS = ((0, 512), (512, 512), (1024, 512), (1536, 256), (1792, 256))
        B_o4 = [plan(A["b_w_out_2"][0], 0, DM, [(o, w, 0)], w) for o, w in OUTS]
        plan_pair(B_o4, 0, 6)

        cs_d = nc.dram_tensor("cs_scratch", [64, T], F)
        h2_d = nc.dram_tensor("h2_scratch", [2, 4, P, 512], F)

        c0 = ExitStack()
        XS = sb("XS", [P, 2, DM], F, c0)
        VS = sb("VS", [P, 4, P], F, c0)
        x = A["x"][0].rearrange("(t p) n -> p t n", p=P)
        t_x = {}
        for i, (c, w) in enumerate(((0, 256), (256, 256), (512, 512), (1024, 512), (1536, 512))):
            t = dma(new_ds(), XS[:, :, c:c + w], x[:, :, c:c + w])
            for k in range(c // P, (c + w) // P, 2):
                t_x[k] = t
            fetch_to(min(i + 1, NR))

        col = {}
        d_vs = new_ds()
        pos = [0, 0]

        def rows(name, ap, n):
            done = 0
            ts = []
            while done < n:
                k = min(n - done, P - pos[1])
                ts.append(dma(d_vs, VS[pos[1]:pos[1] + k, pos[0], :], ap[done:done + k, :]))
                for i in range(k):
                    col[(name, done + i)] = (pos[0], pos[1] + i)
                done += k
                pos[1] += k
                if pos[1] == P:
                    pos[0], pos[1] = pos[0] + 1, 0
            return ts[-1]

        def as_rows(ap):
            return ap.rearrange("(n p) -> n p", p=P)

        t_vs = rows("cw", A["ssd_conv_w"][0].rearrange("j (n p) -> (j n) p", p=P), 192)
        t_vs = rows("cb", as_rows(A["ssd_conv_b"][0]), 48)
        t_vs = rows("ng", as_rows(A["ssd_norm_g"][0]), 32)
        t_vs = rows("lg", A["ln_g"].rearrange("d (n p) -> (d n) p", p=P), 32)
        t_vs = rows("lb", A["ln_b"].rearrange("d (n p) -> (d n) p", p=P), 32)
        t_vs = rows("qg", as_rows(A["dsa_q_norm_g"][0]), 4)
        t_vs = rows("kg", as_rows(A["dsa_kv_norm_g"][0]), 2)
        t_vs = rows("n2", A["norm_g_2"].rearrange("d (n p) -> (d n) p", p=P), 32)
        t_vs = rows("vg", as_rows(A["a_v_norm_g_2"][0]), 32)
        nrows = pos[0] * P + pos[1]

        def vc(name, i):
            a, b = col[(name, i)]
            return VC[:, a, b:b + 1]

        d_s = new_ds()
        dma(d_s, dtb[:, :], A["ssd_dt_bias"][0].rearrange("(h a) -> h a", a=1))
        dma(d_s, alog[:, :], A["ssd_a_log"][0].rearrange("(h a) -> h a", a=1))
        t_sm = dma(d_s, DB[:, :], A["ssd_d_skip"][0].partition_broadcast(P))

        ti = PL(lambda e: e.memset(ident[:, :], 0.0))
        t_id = PL(lambda e: e.affine_select(out=ident[:, :], in_=ident[:, :], compare_op=ALU.not_equal,
                                            fill=1.0, base=0, pattern=[[-1, P]], channel_multiplier=1), ti)
        t_one = PL(lambda e: e.memset(ones[:, :], 1.0))
        tr = PL(lambda e: e.memset(triu[:, :], 1.0))
        for o in (0, 256):
            t_tri = PL(lambda e: e.affine_select(out=triu[:, o:o + P], in_=triu[:, o:o + P],
                                                 compare_op=ALU.is_ge, fill=0.0, base=0,
                                                 pattern=[[1, P]], channel_multiplier=-1), tr)

        xt = {}
        tv = {}

        def turn_in():
            for k in range(0, 16, 2):
                b, rel = mb.get()
                PE.wait(t_x[k], t_id, rel)
                for i in range(2):
                    for t in range(2):
                        last = nc.tensor.transpose(M[:, b, (2 * i + t) * P:(2 * i + t + 1) * P],
                                                   XS[:, t, (k + i) * P:(k + i + 1) * P], ident[:, :])
                toks = split_act(flat(AH[:, k:k + 2, :]), flat(AL[:, k:k + 2, :]), M[:, b, :], pe_end(last))
                xt[k] = xt[k + 1] = toks
                mb.put(b, toks)
                if k % 4 == 2:
                    yield
            b, rel = mb.get()
            PE.wait(rel, t_vs)
            nv = [min(P, nrows - P * i) for i in range(4) if nrows > P * i]
            for i, n in enumerate(nv):
                last = nc.tensor.transpose(M[:, b, i * P:i * P + n], VS[0:n, i, :], ident[0:n, 0:n])
            tp = pe_end(last)
            for i, n in enumerate(nv):
                tv[0] = DV(lambda e: e.tensor_copy(VC[:, i, 0:n], M[:, b, i * P:i * P + n]), tp)
            mb.put(b, [tv[0]])
            for q in range(2):
                tv[1] = DV(lambda e: e.tensor_copy(dcol[64 * q:64 * q + 64, :], DB[64 * q:64 * q + 64, q::2]),
                           t_sm)

        task(turn_in())
        bc0 = gemm(B_bc[0], (AH, AL), xt)
        drain()
        t_vc, t_dc = tv[0], tv[1]
        last_x = [(PE.sem, PE.n)]
        c0.close()

        def brc(ap, n):
            return ap.unsqueeze(1).to_broadcast([P, n, ap.shape[1]])

        cy = ExitStack()
        YH = sb("YH", [P, 32, T], R, cy)
        YL = sb("YL", [P, 32, T], R, cy)
        c1 = ExitStack()
        BT = sb("BT", [P, 8, T], F, c1)
        CT = sb("CT", [P, 8, T], F, c1)
        XGB = sb("XG", [P, 2, 4, T], F, c1)
        add_slot("y1", (flat(YH[:, 28:32, :]), flat(YL[:, 28:32, :])), last_x)
        add_slot("z1", (flat(YH[:, 24:28, :]), flat(YL[:, 24:28, :])), last_x)
        CSB = sb("CSB", [P, 8, T], F, c1)
        E2 = sb("E2", [P, 8, 384], F, c1)
        XD = sb("XD", [P, 2, 512], F, c1)
        YT = sb("YT", [P, 4, T], F, c1)
        SZ = sb("SZ", [P, 4, T], F, c1)
        CB = sb("CB", [P, 384], F, c1)
        RI = sb("RI", [P, T], F, c1)
        dtT = sb("dtT", [P, 2, 64], F, c1)
        csT = sb("csT", [P, 2, 64], F, c1)
        PL(lambda e: e.memset(eps6[:, 0:1], RMS_EPS))
        t_eps = PL(lambda e: e.memset(eps6[:, 1:2], LN_EPS))

        A1 = (AH, AL)
        tk = {}

        def get(*names):
            for n in names:
                while n not in tk:
                    step()
            return [tk[n] for n in names]

        def ones_sum(o, src, first=True, last=True):
            return mm(o, ones[:, :], src, first, last)

        def fold(sq, n, *toks, line=DV):
            while n > 1:
                n //= 2
                t = line(lambda e: e.tensor_tensor(sq[:, 0:n, :], sq[:, 0:n, :], sq[:, n:2 * n, :], ALU.add),
                       *toks)
                toks = (t,)
            return toks[0]

        def dt_task(par, g, tok):
            xb, ab, sp_, ad, cs_ = (YT[0:64, i, :] for i in (0, 1, 2, 3, 1))
            dtv = SZ[0:64, 0, :]
            nea = SZ[0:64, 1, 0:1]
            t1 = DV(lambda e: e.tensor_scalar(xb, g[0:64, 0:T], dtb[:, 0:1], None, ALU.add), tok, t_sm, last_x)
            release(par, t1)
            t2 = DV(lambda e: e.scalar_tensor_tensor(out=ab, in0=xb, scalar=-1.0, in1=xb, op0=ALU.mult,
                                                     op1=ALU.max), t1)
            t3 = AC(lambda e: e.activation(nea, alog[:, :], ACT.Exp), t_sm, last_x)
            t4 = AC(lambda e: e.activation(ab, ab, ACT.Exp, scale=-1.0), t2)
            t5 = AC(lambda e: e.activation(sp_, ab, ACT.Ln, bias=1.0), t4)
            yield 2
            t6 = DV(lambda e: e.scalar_tensor_tensor(out=dtv, in0=xb, scalar=0.0, in1=sp_, op0=ALU.max,
                                                     op1=ALU.add), t5)
            t7 = DV(lambda e: e.tensor_scalar(ad, dtv, nea, -1.0, ALU.mult, ALU.mult), t6, t3)
            t7b = DV(lambda e: e.memset(xb, 1.0), t6)
            t8 = DV(lambda e: e.tensor_tensor_scan(cs_, xb, ad, 0.0, ALU.mult, ALU.add), t7, t7b, t5)
            tk["csd"] = dma(new_ds(), cs_d[:, :], cs_, t8)
            yield 3
            b, rel = mb.get()
            PE.wait(rel, t8, t6)
            for t in range(2):
                nc.tensor.transpose(M[:, b, t * P:t * P + 64], dtv[:, t * P:(t + 1) * P], ident[0:64, 0:64])
                last = nc.tensor.transpose(M[:, b, 256 + t * P:256 + t * P + 64],
                                           cs_[:, t * P:(t + 1) * P], ident[0:64, 0:64])
            tp = pe_end(last)
            m = M[:, b, :].rearrange("p (a t n) -> p a t n", a=2, t=2)
            tk["dtT"] = DV(lambda e: e.tensor_copy(dtT[:, :, :], m[:, 0, :, 0:64]), tp)
            tk["csT"] = DV(lambda e: e.tensor_scalar(csT[:, :, :], m[:, 1, :, 0:64], -1.0, None, ALU.mult), tp)
            mb.put(b, [tk["csT"]])


        def conv(par, g, tok, ch, dst, free, name, stage=None):
            ts = []
            if stage is not None:
                tok = AC(lambda e: e.copy(stage, g), tok, free)
                release(par, tok)
                g = stage
            for f in range(4):
                u = g[:, f * T:(f + 1) * T]
                ts.append(DV(lambda e: e.tensor_scalar(dst[:, f, :], u, vc("cw", 3 * 48 + ch + f),
                                                       vc("cb", ch + f), ALU.mult, ALU.add),
                             tok, t_vc, free))
            yield
            for j in (2, 1, 0):
                s = 3 - j
                for f in range(4):
                    u = g[:, f * T:(f + 1) * T]
                    ts[f] = DV(lambda e: e.scalar_tensor_tensor(
                        out=dst[:, f, s:T], in0=u[:, 0:T - s], scalar=vc("cw", j * 48 + ch + f),
                        in1=dst[:, f, s:T], op0=ALU.mult, op1=ALU.add), ts[f])
                yield
            if stage is None:
                release(par, ts[-1])
            else:
                st["csb"] = ts[-1]
            yield
            d = flat(dst)
            tk[name] = AC(lambda e: e.activation(d, d, ACT.Silu), ts)

        st = {"csb": None, "e": None, "xd": None, "yt": None, "ri": None, "sz": None}
        for i in range(4):
            par, g, tok = bc0 if i == 0 else gemm(B_bc[i], A1, xt)
            dst = (BT, CT)[i // 2][:, 4 * (i % 2):4 * (i % 2) + 4, :]
            task(conv(par, g, tok, 32 + 4 * i, dst, last_x, ("bc", i), flat(CSB[:, 0:4, :]) if i == 0 else None))
            if i == 0:
                task(dt_task(*gemm(B_dt, A1, xt)))

        yt = {}
        d_csb = new_ds()

        def decay(g, h0, tcs):
            for h in range(h0, h0 + 4):
                hh = 8 * g + h
                DV(lambda e: e.tensor_scalar(E2[:, h, 0:256], CSB[:, h, :], csT[:, 0, hh:hh + 1], 0.0,
                                             ALU.add, ALU.min), tcs, tk["csT"], st["e"])
                td = DV(lambda e: e.tensor_scalar(E2[:, h, 256:384], CSB[:, h, P:T], csT[:, 1, hh:hh + 1],
                                                  0.0, ALU.add, ALU.min))
            st["csb"] = td
            ev = E2[:, h0:h0 + 4, :].rearrange("p h n -> p (h n)")
            return AC(lambda e: e.activation(ev, ev, ACT.Exp), td)

        def ssd(g, par, gx, tok):
            XG = XGB[:, g % 2]
            yield from conv(par, gx, tok, 4 * g, XG, tk.get(("y", g - 2), last_x), ("xg", g))
            t_xg = tk[("xg", g)]
            while not ("csT" in tk and "csd" in tk and all(("bc", i) in tk for i in range(4))
                       and (g == 0 or ("y", g - 1) in tk)):
                yield
            tcs = dma(d_csb, CSB[:, :, :], cs_d[8 * g:8 * g + 8, :].rearrange("h t -> (h t)")
                      .partition_broadcast(P), tk["csd"], st["csb"])
            yield
            b, rel = mb.get()
            PE.wait(rel, [tk[("bc", i)] for i in range(4)])
            mm(M[:, b, 0:256], BT[:, g, 0:P], CT[:, g, :], True, True)
            tp = PE(lambda e: mm(M[:, b, 256:384], BT[:, g, P:T], CT[:, g, P:T], False, True))
            tcb = DV(lambda e: e.tensor_tensor(CB[:, :], M[:, b, 0:384], triu[:, :], ALU.mult),
                     tp, t_tri, st["e"])
            mb.put(b, [tcb])
            yield
            yield
            te = decay(g, 0, tcs)
            yield
            txd = []
            for t in range(2):
                b, rel = mb.get()
                PE.wait(rel, t_xg)
                for f in range(4):
                    last = nc.tensor.transpose(M[:, b, f * P:(f + 1) * P], XG[:, f, t * P:(t + 1) * P],
                                               ident[:, :])
                tp = pe_end(last)
                bd = dtT[:, t, 8 * g:8 * g + 8].unsqueeze(2).to_broadcast([P, 8, 64])
                txd.append(DV(lambda e: e.tensor_tensor(
                    XD[:, t, :].rearrange("p (h d) -> p h d", h=8),
                    M[:, b, :].rearrange("p (h d) -> p h d", h=8), bd, ALU.mult),
                    tp, tk["dtT"], st["xd"]))
                mb.put(b, [txd[-1]])
                yield
            cbb = CB[:, :].unsqueeze(1).to_broadcast([P, 4, 384])
            tm = [DV(lambda e: e.tensor_tensor(E2[:, 0:4, :], E2[:, 0:4, :], cbb, ALU.mult), te, tcb)]
            yield
            te = decay(g, 4, tcs)
            yield
            tm.append(DV(lambda e: e.tensor_tensor(E2[:, 4:8, :], E2[:, 4:8, :], cbb, ALU.mult), te, tcb))
            yield
            while g > 0 and ("yt", g - 1) not in tk:
                yield
            ty = []
            for q in range(4):
                b, rel = mb.get()
                PE.wait(rel, tm[q // 2], txd)
                for r in range(2):
                    h = 2 * q + r
                    o = M[64 * r:64 * r + 64, b, :]
                    mm(o[:, 0:256], XD[:, 0, 64 * h:64 * h + 64], E2[:, h, 0:256], True, False)
                    last = mm(o[:, 128:256], XD[:, 1, 64 * h:64 * h + 64], E2[:, h, 256:384], False, True)
                tp = pe_end(last)
                ty.append(DV(lambda e: e.scalar_tensor_tensor(
                    out=YT[:, q, :], in0=XG[:, q, :], scalar=dcol[:, 4 * g + q:4 * g + q + 1],
                    in1=M[:, b, 0:T], op0=ALU.mult, op1=ALU.add), tp, t_xg, t_dc, tk["csd"], st["yt"]))
                mb.put(b, [ty[-1]])
                yield
            st["e"] = tp
            st["xd"] = tp
            tk[("y", g)] = [ty, tp]

        def gate_z(g, par, gz, tok):
            while ("dtT" not in tk) or (g > 0 and ("yt", g - 1) not in tk):
                yield
            tz = AC(lambda e: e.activation(flat(SZ[:, :, :]), gz, ACT.Silu), tok, st["sz"], tk["csT"], tk["dtT"])
            release(par, tz)
            while ("y", g) not in tk:
                yield
            sz, yv = flat(SZ[:, :, :]), flat(YT[:, :, :])
            t1 = PL(lambda e: e.tensor_tensor(yv, yv, sz, ALU.mult), tz, tk[("y", g)])
            t2 = AC(lambda e: e.activation(sz, yv, ACT.Square), t1)
            yield
            t2 = fold(SZ, 4, t2, line=PL)
            yield 2
            b, rel = mb.get()
            PE.wait(rel, t2, t_one)
            tp = pe_end(ones_sum(M[:, b, 0:T], SZ[:, 0, :]))
            yield
            t3 = AC(lambda e: e.activation(RI[:, :], M[:, b, 0:T], ACT.Sqrt, scale=1.0 / 512, bias=eps6[:, 0:1]),
                    tp, t_eps, st["ri"])
            mb.put(b, [t3])
            t4 = DV(lambda e: e.reciprocal(RI[:, :], RI[:, :]), t3)
            yield
            for f in range(4):
                t5 = DV(lambda e: e.scalar_tensor_tensor(out=SZ[:, f, :], in0=YT[:, f, :],
                                                         scalar=vc("ng", 4 * g + f), in1=RI[:, :],
                                                         op0=ALU.mult, op1=ALU.mult), t4, tp, t1)
            st["yt"] = t5
            st["ri"] = t5
            yield
            toks = split_act(flat(YH[:, 4 * g:4 * g + 4, :]), flat(YL[:, 4 * g:4 * g + 4, :]), sz, t5,
                             slot_end[("z1", "y1")[g - 6]] if g > 5 else None)
            st["sz"] = toks
            for f in range(4):
                yt[4 * g + f] = toks
            tk[("yt", g)] = toks

        for gi in range(8):
            par, g, tok = gemm(B_xz[gi][0], A1, xt)
            task(ssd(gi, par, g, tok))
            par, g, tok = gemm(B_xz[gi][1], A1, xt)
            task(gate_z(gi, par, g, tok))
            if gi > 5:
                drop_slot(("z1", "y1")[gi - 6])

        def fence():
            return [(PE.sem, PE.n), (AC.sem, AC.n), (DV.sem, DV.n)]

        def ln_blocks(res0, job1, blocks, yt, RES, PV, SQ, SU, MU, RS):
            bank = {}
            done = [None] * len(blocks)

            def prepare():
                while "pv" not in bank:
                    yield
                for i in range(1, len(blocks)):
                    k0, n, _ = blocks[i]
                    r3 = RES[:, k0:k0 + n, :]
                    t1 = DV(lambda e: e.scalar_tensor_tensor(
                        out=r3, in0=AH[:, k0:k0 + n, :].bitcast(F), scalar=ALPHA, in1=brc(PV[:, :], n),
                        op0=ALU.mult, op1=ALU.subtract), bank["pv"])
                    yield
                    bank["pre", i] = DV(lambda e: e.scalar_tensor_tensor(
                        out=r3, in0=AL[:, k0:k0 + n, :].bitcast(F), scalar=ALPHA, in1=r3, op0=ALU.mult,
                        op1=ALU.add), t1)
                    yield 2

            def evac(i, par, g, tok):
                k0, n, _ = blocks[i]
                while i > 0 and done[i - 1] is None:
                    yield
                r3 = RES[:, k0:k0 + n, :]
                r, gv = flat(r3), g[:, 0:n * T]
                if i == 0:
                    xh, xl = flat(AH[:, k0:k0 + n, :]).bitcast(F), flat(AL[:, k0:k0 + n, :]).bitcast(F)
                    t1 = DV(lambda e: e.scalar_tensor_tensor(out=r, in0=xh, scalar=ALPHA, in1=gv, op0=ALU.mult,
                                                             op1=ALU.add), tok)
                    release(par, t1)
                    t1 = DV(lambda e: e.scalar_tensor_tensor(out=r, in0=xl, scalar=ALPHA, in1=r, op0=ALU.mult,
                                                             op1=ALU.add), t1)
                    yield 2
                    b, rel = mb.get()
                    PE.wait(rel, t1)
                    for f in range(4):
                        last = ones_sum(M[:, b, 0:T], RES[:, f, :], f == 0, f == 3)
                    tp = pe_end(last)
                    bank["pv"] = AC(lambda e: e.activation(PV[:, :], M[:, b, 0:T], ACT.Copy, scale=1.0 / 512),
                                    tp)
                    mb.put(b, [bank["pv"]])
                    (bank[1], rel1), (bank[2], rel2) = mb.get(), mb.get()
                    PE.wait(rel1, rel2)
                    yield
                    t2 = DV(lambda e: e.tensor_tensor(r3, r3, brc(PV[:, :], n), ALU.subtract), t1, bank["pv"])
                else:
                    t2 = DV(lambda e: e.tensor_tensor(r, r, gv, ALU.add), tok, bank["pre", i])
                    release(par, t2)
                if i == len(blocks) - 1:
                    AC(lambda e: e.activation(TB[:, :], eps6[:, :], ACT.Sqrt), t_eps, bank.get("tb"))
                t3 = AC(lambda e: e.activation(flat(SQ[:, 0:n, :]), r, ACT.Square), t2, bank.get("sq"))
                first, last_ = i == 0, i == len(blocks) - 1
                if n == 4:
                    t4 = DV(lambda e: e.tensor_tensor(SU[:, :, :], r3[:, 0:2, :], r3[:, 2:4, :], ALU.add),
                            t2, bank.get("sq"))
                    t4 = fold(SU, 2, t4)
                    yield
                    t5 = fold(SQ, n, t3)
                    srcs, sqs = [SU[:, 0, :]], [SQ[:, 0, :]]
                else:
                    t4, t5 = t2, t3
                    srcs, sqs = [r3[:, f, :] for f in range(n)], [SQ[:, f, :] for f in range(n)]
                yield 2
                PE.wait(t4)
                for f, v in enumerate(srcs):
                    ones_sum(M[:, bank[1], 0:T], v, first and f == 0, last_ and f == len(srcs) - 1)
                PE.wait(t5)
                for f, v in enumerate(sqs):
                    last = ones_sum(M[:, bank[2], 0:T], v, first and f == 0, last_ and f == len(sqs) - 1)
                bank["sq"] = pe_end(last)
                done[i] = bank["sq"]

            now(evac(0, *res0))
            task(prepare())
            for i in range(1, len(blocks)):
                job = job1 if i == 1 and job1 else gemm_open(blocks[i][2])
                now(evac(i, *gemm_run(job, (YH, YL), yt)))
            drain()
            b1, b2, tp = bank[1], bank[2], bank["sq"]
            t2 = AC(lambda e: e.activation(PV[:, :], M[:, b1, 0:T], ACT.Square, scale=1.0 / DM), tp, bank["pv"])
            t3 = DV(lambda e: e.scalar_tensor_tensor(out=RS[:, :], in0=M[:, b2, 0:T], scalar=1.0 / DM,
                                                     in1=PV[:, :], op0=ALU.mult, op1=ALU.subtract), t2)
            t4 = AC(lambda e: e.activation(RS[:, :], RS[:, :], ACT.Sqrt, bias=eps6[:, 1:2]), t3, t_eps)
            t1 = DV(lambda e: e.tensor_scalar(MU[:, :], M[:, b1, 0:T], 1.0 / DM, None, ALU.mult), t2)
            mb.put(b1, [t1])
            mb.put(b2, [t3])
            less = {}
            less[0] = DV(lambda e: e.tensor_tensor(RES[:, 0, :], RES[:, 0, :], MU[:, :], ALU.subtract), t1)
            tr = DV(lambda e: e.reciprocal(RS[:, :], RS[:, :]), t4)
            less[1] = PL(lambda e: e.tensor_tensor(RES[:, 1, :], RES[:, 1, :], MU[:, :], ALU.subtract), t1)
            for k in range(2, 16):
                less[k] = PL(lambda e: e.tensor_tensor(RES[:, k, :], RES[:, k, :], MU[:, :], ALU.subtract), t1)

            def normal(k, n):
                r3 = RES[:, k:k + n, :]
                return DV(lambda e: e.tensor_tensor(r3, r3, brc(RS[:, :], n), ALU.mult),
                          [less[i] for i in range(k, k + n)], tr)
            return normal

        def norm_in(at, normal, gain, bias, RES, GHO, frees, t_g):
            n_, g_, h_ = {}, {}, {}

            def st_n(c):
                if c < len(CHUNKS):
                    n_[c] = normal(*CHUNKS[c])

            def st_g(c):
                k, n = CHUNKS[c]
                d = GHO(c)
                if c == 0:
                    g_[c] = DV(lambda e: e.tensor_scalar(d[:, 0, :], RES[:, 0, :], gain(0), bias(0), ALU.mult,
                                                         ALU.add), n_[c], t_g)
                    return
                g_[c] = [AC(lambda e: e.activation(d[:, i, :], RES[:, k + i, :], ACT.Identity,
                                                   scale=gain(k + i), bias=bias(k + i)),
                            n_[c], t_g, frees(c, h_)) for i in range(n)]

            def st_h(c):
                k, n = CHUNKS[c]
                h_[c] = split_act(flat(AH[:, k:k + n, :]), flat(AL[:, k:k + n, :]), flat(GHO(c)), g_[c])
                for i in range(k, k + n):
                    at[i] = h_[c]

            st_n(0)
            st_g(0)
            st_n(1)
            st_h(0)
            st_n(2)
            st_g(1)
            st_h(1)
            yield
            for c in range(2, len(CHUNKS)):
                st_n(c + 1)
                st_g(c)
                st_h(c)
                yield

        CHUNKS = ((0, 1), (1, 1)) + tuple((k, 2) for k in range(2, 16, 2))

        jobs = []
        for i in range(2):
            jobs.append(gemm_open(B_o1[i][2]))
            gemm_run(jobs[i], (YH, YL), yt, n=14)
        res0 = gemm_run(jobs[0], (YH, YL), yt)
        drain()
        c1.close()
        c2 = ExitStack()
        RES = sb("RES2", [P, 16, T], F, c2)
        PV = sb("PV2", [P, T], F, c2)
        SQ = sb("SQ2", [P, 4, T], F, c2)
        SU = sb("SU2", [P, 2, T], F, c2)
        MU = sb("MU2", [P, T], F, c2)
        RS = sb("RS2", [P, T], F, c2)
        f2 = fence()
        for l in (AC, DV):
            l.wait(f2)
        normal = ln_blocks(res0, jobs[1], B_o1, yt, RES, PV, SQ, SU, MU, RS)
        at = {}
        task(norm_in(at, normal, lambda k: vc("lg", k), lambda k: vc("lb", k), RES,
                     lambda c, R=RES: R[:, CHUNKS[c][0]:sum(CHUNKS[c]), :], lambda c, h: None, None))
        cq0 = gemm(B_cq, (AH, AL), at)
        drain()
        f3 = fence() + [(PL.sem, PL.n)]
        c2.close()

        c3 = ExitStack()
        QKB = sb("QKB", [P, 2, 2, 4, T], F, c3)
        VVB = sb("VVB", [P, 2, 2, 512], F, c3)
        SG = sb("SG", [P, 3, 4, T], F, c3)
        OT = sb("OT", [P, 4, T], F, c3)
        CQH = sb("CQH", [P, 4, T], R, c3)
        CQL = sb("CQL", [P, 4, T], R, c3)
        CKH = sb("CKH", [P, 2, T], R, c3)
        CKL = sb("CKL", [P, 2, T], R, c3)
        KI = sb("KI", [P, T], F, c3)
        WT = sb("WT", [P, 2, 16], F, c3)
        SC = sb("SC", [P, 384], F, c3)
        MA = sb("MA", [P, 384], F, c3)
        TRL = sb("TRL", [P, 384], F, c3)
        PXB = sb("PXB", [P, 2, 384], F, c3)
        PT = sb("PT", [P, 384], F, c3)
        M8 = sb("M8", [P, 2, 8], F, c3)
        MXB = sb("MXB", [P, 2, 8], F, c3)
        RQ = sb("RQ", [P, 2, T], F, c3)
        A3 = (AH, AL)
        add_slot("y3", (flat(YH[:, 28:32, :]), flat(YL[:, 28:32, :])), f3)
        QI = QKB[:, 1]
        tl = PL(lambda e: e.memset(TRL[:, :], 1.0), f3)
        for o in (0, 256):
            t_trl = PL(lambda e: e.affine_select(out=TRL[:, o:o + P], in_=TRL[:, o:o + P],
                                                 compare_op=ALU.is_ge, fill=0.0, base=0,
                                                 pattern=[[-1, P]], channel_multiplier=1), tl)

        def small_rms(src, n, tsrc, tmp, gname, H, L, ttmp, rq, name):
            t1 = AC(lambda e: e.activation(flat(tmp), flat(src), ACT.Square), tsrc, ttmp)
            yield
            t1 = fold(tmp, n, t1)
            yield 2
            b, rel = mb.get()
            PE.wait(rel, t1)
            tp = pe_end(ones_sum(M[:, b, 0:T], tmp[:, 0, :]))
            yield
            t2 = AC(lambda e: e.activation(rq, M[:, b, 0:T], ACT.Sqrt, scale=1.0 / (n * P),
                                           bias=eps6[:, 0:1]), tp, f3)
            mb.put(b, [t2])
            t3 = DV(lambda e: e.reciprocal(rq, rq), t2)
            for f in range(n):
                t4 = DV(lambda e: e.scalar_tensor_tensor(out=src[:, f, :], in0=src[:, f, :],
                                                         scalar=vc(gname, f), in1=rq,
                                                         op0=ALU.mult, op1=ALU.mult), t3, tsrc)
            yield
            tk[name] = split_act(flat(H[:, :, :]), flat(L[:, :, :]), flat(src), t4)

        class At(dict):

            def __init__(self, name):
                self.name = name

            def __contains__(self, k):
                return self.name in tk

            def __missing__(self, k):
                return tk[self.name]

        def ev_cq(par, g, tok):
            t1 = DV(lambda e: e.tensor_copy(flat(QKB[:, 0, 0]), g), tok, f3)
            release(par, t1)
            yield
            yield from small_rms(QKB[:, 0, 0], 4, t1, QKB[:, 0, 1], "qg", CQH, CQL, f3, RQ[:, 0, :], "cq")

        KW = VVB[:, 0, 0, 0:T]

        def ev_ms(par, g, tok):
            t2 = DV(lambda e: e.tensor_copy(flat(OT[:, 0:2, :]), g[:, 0:512]), tok, f3)
            t_w = DV(lambda e: e.tensor_copy(KW[0:96, :], g[0:96, 512:768]), tok)
            release(par, t_w)
            d_ki = new_ds()
            dma(d_ki, KI[0:64, :], KW[0:64, :], t_w, f3)
            tk["ki"] = dma(d_ki, KI[64:128, :], KW[0:64, :], t_w, f3)
            yield
            yield from small_rms(OT[:, 0:2, :], 2, t2, OT[:, 2:4, :], "kg", CKH, CKL, f3, RQ[:, 1, :], "ck")
            b, rel = mb.get()
            PE.wait(rel, t_w)
            for t in range(2):
                last = nc.tensor.transpose(M[:, b, 16 * t:16 * t + 16], KW[64:80, t * P:(t + 1) * P],
                                           ident[64:80, 64:80])
            tk["wt"] = DV(lambda e: e.tensor_scalar(WT[:, :, :].rearrange("p a n -> p (a n)"), M[:, b, 0:32],
                                                    0.25, 0.125, ALU.mult, ALU.mult), pe_end(last), f3)
            mb.put(b, [tk["wt"]])

        def ev_gate(j, par, g, tok):
            while j > 2 and ("og", j - 3) not in tk:
                yield
            tk[("sg", j)] = AC(lambda e: e.activation(flat(SG[:, j % 3]), g, ACT.Silu), tok,
                               tk.get(("og", j - 3)), f3)
            release(par, tk[("sg", j)])

        def ev_qi(i, par, g, tok):
            tk[("qi", i)] = DV(lambda e: e.tensor_copy(flat(QI[:, i]), g), tok, f3)
            release(par, tk[("qi", i)])
            yield

        now(ev_cq(*cq0))
        now(ev_ms(*gemm(B_ms, A3, at)))
        now(ev_gate(0, *gemm(B_gate[0], A3, at)))
        for i in range(2):
            now(ev_qi(i, *gemm(B_qi[i], (CQH, CQL), At("cq"))))

        def index_scores():
            acc = [None, None]
            RLS, rl_free = (PT, PXB[:, 0, :]), [None, None]
            while not (("qi", 1) in tk and "wt" in tk):
                yield
            for h0 in range(0, 16, 2):
                made = []
                for h in (h0, h0 + 1):
                    f, o = h // 2, 64 * (h % 2)
                    b, rel = mb.get()
                    PE.wait(rel, tk[("qi", 0)], tk[("qi", 1)], tk["ki"])
                    qh = QI[o:o + 64, f // 4, f % 4, :]
                    mm(M[:, b, 0:P], qh[:, 0:P], KI[o:o + 64, 0:P], True, True)
                    tp = PE(lambda e: mm(M[:, b, P:P + T], qh[:, P:T], KI[o:o + 64, :], False, True))
                    made.append((b, tp))
                tk["qi_read"] = tp
                yield
                for i, (b, tp) in enumerate(made):
                    h, RL = h0 + i, RLS[i]
                    ta = AC(lambda e: e.activation(RL[:, :], M[:, b, 0:384], ACT.Relu), tp, rl_free[i], f3)
                    mb.put(b, [ta])
                    for t, (a, z) in enumerate(((0, P), (P, 384))):
                        w = WT[:, t, h:h + 1]
                        if h == 0:
                            acc[t] = DV(lambda e: e.tensor_scalar(SC[:, a:z], RL[:, a:z], w, None, ALU.mult),
                                        ta, tk["wt"], f3)
                        else:
                            acc[t] = DV(lambda e: e.scalar_tensor_tensor(
                                out=SC[:, a:z], in0=RL[:, a:z], scalar=w, in1=SC[:, a:z], op0=ALU.mult,
                                op1=ALU.add), ta, acc[t])
                    rl_free[i] = acc[1]
            tk["qi_done"] = tk["qi_read"]
            t1 = DV(lambda e: e.tensor_scalar(MA[:, :], TRL[:, :], -NEG * 1e8, NEG * 1e8, ALU.mult, ALU.add),
                    t_trl, f3)
            t2 = DV(lambda e: e.tensor_tensor(SC[:, :], SC[:, :], TRL[:, :], ALU.mult), acc)
            t3 = DV(lambda e: e.tensor_tensor(SC[:, :], SC[:, :], MA[:, :], ALU.add), t2, t1)
            yield
            tr = [t3, t3]
            for i in range(8):
                tm = [None, None]
                for t, (a, z) in enumerate(((0, P), (P, 384))):
                    tm[t] = DV(lambda e: e.max(M8[:, t, :], SC[:, a:z]), tr[t], f3)
                for t, (a, z) in enumerate(((0, P), (P, 384))):
                    tr[t] = DV(lambda e: e.match_replace(SC[:, a:z], M8[:, t, :], SC[:, a:z], -3.0e38), tm[t])
                yield
            t4 = DV(lambda e: e.tensor_scalar(SC[:, :], SC[:, :], -2.0e38, None, ALU.is_lt), tr)
            t5 = DV(lambda e: e.tensor_tensor(SC[:, :], SC[:, :], TRL[:, :], ALU.mult), t4)
            tk["rl"] = rl_free
            tk["mask"] = DV(lambda e: e.tensor_scalar(MA[:, :], SC[:, :], -NEG, NEG, ALU.mult, ALU.add), t5)

        yt = {}
        PTB = (PT, SC)
        s3 = [{"px": None, "pt": None, "mx": None} for _ in range(2)]
        SCALE = 128.0 ** -0.5

        def attend(j, c):
            while not ("mask" in tk and ("v", j) in tk and (j == 0 or ("pv", j - 1, c) in tk)):
                yield
            QK, VV = QKB[:, j % 2], VVB[:, j % 2]
            PX, PT_, MX, s = PXB[:, c, :], PTB[c], MXB[:, c, :], s3[c]
            spans = ((0, P), (P, 384))
            ot = []
            for h in (c, c + 2):
                b, rel = mb.get()
                PE.wait(rel, tk[("q", j)], tk[("k", j)])
                q, k = QK[:, 0, h, :], QK[:, 1, h, :]
                mm(M[:, b, 0:P], q[:, 0:P], k[:, 0:P], True, True)
                tp = PE(lambda e: mm(M[:, b, P:384], q[:, P:T], k[:, :], False, True))
                tmx = []
                for t, (a, z) in enumerate(spans):
                    tmx.append(DV(lambda e: e.tensor_tensor_reduce(
                        out=PX[:, a:z], in0=M[:, b, a:z], in1=MA[:, a:z], scale=SCALE, scalar=-3.0e38,
                        op0=ALU.add, op1=ALU.max, accum_out=MX[:, t:t + 1]), tp, tk["mask"], s["px"],
                        s["mx"], f3))
                mb.put(b, [tmx[-1]])
                tn = DV(lambda e: e.tensor_scalar(MX[:, 2:4], MX[:, 0:2], -1.0, None, ALU.mult), tmx)
                te = []
                for t, (a, z) in enumerate(spans):
                    te.append(AC(lambda e: e.activation(PX[:, a:z], PX[:, a:z], ACT.Exp, bias=MX[:, 2 + t:3 + t],
                                                        accum_out=MX[:, 4 + t:5 + t]), tn))
                yield
                tr = DV(lambda e: e.reciprocal(MX[:, 6:8], MX[:, 4:6]), te)
                for t, (a, z) in enumerate(spans):
                    ts = DV(lambda e: e.tensor_scalar(PX[:, a:z], PX[:, a:z], MX[:, 6 + t:7 + t], None,
                                                      ALU.mult), tr)
                s["mx"] = ts
                yield 2
                b, rel = mb.get()
                PE.wait(rel, ts)
                nc.tensor.transpose(M[:, b, 0:P], PX[:, 0:P], ident[:, :])
                nc.tensor.transpose(M[:, b, P:T], PX[:, P:T], ident[:, :])
                tp = PE(lambda e: e.transpose(M[:, b, T:384], PX[:, T:384], ident[:, :]))
                s["px"] = tp
                tc = AC(lambda e: e.copy(PT_[:, :], M[:, b, 0:384]), tp, s["pt"], tk["rl"], tk["mask"])
                mb.put(b, [tc])
                yield
                b, rel = mb.get()
                PE.wait(rel, tc, tk[("v", j)])
                mm(M[:, b, 0:T], VV[:, 0, h * P:(h + 1) * P], PT_[:, 0:T], True, False)
                tp = PE(lambda e: mm(M[:, b, P:T], VV[:, 1, h * P:(h + 1) * P], PT_[:, T:384], False, True))
                s["pt"] = tp
                while j > 0 and ("ot", j - 1) not in tk:
                    yield
                ot.append(DV(lambda e: e.tensor_copy(OT[:, h, :], M[:, b, 0:T]), tp, tk.get(("ot", j - 1)),
                             tk["ck"]))
                mb.put(b, [ot[-1]])
            tk[("pv", j, c)] = [tp, ot]

        def gated(j):
            while not (("pv", j, 0) in tk and ("pv", j, 1) in tk and ("sg", j) in tk):
                yield
            pv = [tk[("pv", j, 0)], tk[("pv", j, 1)]]
            tk[("qkv_read", j)] = pv
            t1 = DV(lambda e: e.tensor_tensor(OT[:, :, :], OT[:, :, :], SG[:, j % 3], ALU.mult), pv,
                    tk[("sg", j)])
            tk[("og", j)] = t1
            yield
            toks = split_act(flat(YH[:, 4 * j:4 * j + 4, :]), flat(YL[:, 4 * j:4 * j + 4, :]),
                             flat(OT[:, :, :]), t1, slot_end["y3"] if j == 7 else None)
            tk[("ot", j)] = toks
            for f in range(4):
                yt[4 * j + f] = toks

        def kv_gemm(u, values):
            step()
            par = gpar[0]
            gpar[0] ^= 1
            take(par)
            split_ahead(u)
            PE.wait(w_tok[u], get("ck"))
            if values:
                wh = w_at[u][0][:, :].rearrange("p (c m) -> p c m", c=2)
                wl = w_at[u][1][:, :].rearrange("p (c m) -> p c m", c=2)
                for t in range(2):
                    o = G[:, 2 * par + t, :]
                    for c in range(2):
                        xh, xl = CKH[:, c, t * P:(t + 1) * P], CKL[:, c, t * P:(t + 1) * P]
                        mm(o, xh, wh[:, c, :], c == 0, False)
                        mm(o, xh, wl[:, c, :], False, False)
                        last = mm(o, xl, wh[:, c, :], False, c == 1)
            else:
                wh = w_at[u][0][:, :].rearrange("p (h c n) -> p h c n", h=4, c=2)
                wl = w_at[u][1][:, :].rearrange("p (h c n) -> p h c n", h=4, c=2)
                for h in range(4):
                    o = G[:, 2 * par + h // 2, (h % 2) * T:(h % 2 + 1) * T]
                    for c in range(2):
                        mm(o, wh[:, h, c, :], CKH[:, c, :], c == 0 and h % 2 == 0, False)
                        mm(o, wh[:, h, c, :], CKL[:, c, :], False, False)
                        last = mm(o, wl[:, h, c, :], CKH[:, c, :], False, c == 1)
            tok = end_unit(u, last)
            return par, flat(G[:, 2 * par:2 * par + 2, :]), tok

        def ev_qkv(name, j, dst, par, g, tok, act):
            while (j > 1 and ("qkv_read", j - 2) not in tk) or (j == 1 and "qi_done" not in tk) or "wt" not in tk:
                yield
            free = tk.get(("qkv_read", j - 2)) if j > 1 else [tk.get("qi_read"), tk["cq"], tk["wt"], tk["ki"]]
            if act:
                t = AC(lambda e: e.copy(dst, g), tok, free, f3)
            else:
                t = DV(lambda e: e.tensor_copy(dst, g), tok, free, f3)
            release(par, t)
            tk[(name, j)] = t

        task(index_scores())
        for j in range(8):
            if j == 6:
                drop_slot("y3")
            now(ev_qkv("q", j, flat(QKB[:, j % 2, 0]), *gemm(B_qkv[j][0], (CQH, CQL), At("cq")), False))
            now(ev_qkv("k", j, flat(QKB[:, j % 2, 1]), *kv_gemm(B_qkv[j][1], False), True))
            now(ev_qkv("v", j, flat(VVB[:, j % 2]), *kv_gemm(B_qkv[j][2], True), False))
            task(attend(j, 0))
            task(attend(j, 1))
            task(gated(j))
            for i in GATES[j]:
                now(ev_gate(i, *gemm(B_gate[i], A3, at)))
        res0 = gemm(B_o2[0][2], (YH, YL), yt)
        drain()
        f4 = fence()
        c3.close()

        c4 = ExitStack()
        RES = sb("RES4", [P, 16, T], F, c4)
        c5 = ExitStack()
        V = sb("V5", [P, 2, 4096], F, c5)
        U = sb("U5", [P, 4, T], F, c5)
        Z = sb("Z5", [P, 4, T], F, c5)
        WS = sb("WS5", [P, 2, P], F, c5)
        WM = sb("WM5", [P, 2, P], F, c5)
        WR = sb("WR5", [P, 2, 2, P], F, c5)
        BS = sb("BS5", [P, 2, P], F, c5)
        VS5 = sb("VS5", [P, 2, 8], F, c5)
        VR = sb("VR5", [P, 2], F, c5)
        GB = sb("GB5", [P, 2, 16], F, c5)
        SQ, GH = U, Z
        VA = V[:, 0, 0:5 * T].rearrange("p (a n) -> p a n", a=5)
        for l in (AC, DV):
            l.wait(f4)
        for q, name in enumerate(("lg", "lb")):
            (a0, b0), (a1, b1) = col[(name, 16)], col[("n2", 0)]
            t_gb = DV(lambda e: e.tensor_tensor(GB[:, q, :], VC[:, a0, b0:b0 + 16], VC[:, a1, b1:b1 + 16],
                                                ALU.mult))
        PV, MU, RS, SU = VA[:, 0, :], VA[:, 1, :], VA[:, 2, :], VA[:, 3:5, :]
        normal = ln_blocks(res0, None, B_o2, yt, RES, PV, SQ, SU, MU, RS)

        def rms_sum(i, n, toks, SQ, bank, first, last, line=None):
            r, q = flat(RES[:, i:i + n, :]), flat(SQ[:, 0:n, :])
            if line:
                t1 = line(lambda e: e.tensor_tensor(q, r, r, ALU.mult), toks, bank.get("sq"))
            else:
                t1 = AC(lambda e: e.activation(q, r, ACT.Square), toks, bank.get("sq"))
            t1 = fold(SQ, n, t1, line=line or DV)
            yield 2
            if first:
                bank["b"], rel = mb.get()
                PE.wait(rel)
            PE.wait(t1)
            bank["sq"] = pe_end(ones_sum(M[:, bank["b"], 0:T], SQ[:, 0, :], first, last))

        def rms_scale(RSX, CS, bank, *toks):
            yield
            t2 = AC(lambda e: e.activation(RSX, M[:, bank["b"], 0:T], ACT.Sqrt, scale=1.0 / DM,
                                           bias=eps6[:, 0:1]), bank["sq"], *toks)
            mb.put(bank["b"], [t2])
            t3 = DV(lambda e: e.reciprocal(RSX, RSX), t2)
            yield 2
            b, rel = mb.get()
            PE.wait(rel, t3)
            for t in range(2):
                last = nc.tensor.transpose(M[:, b, t * P:(t + 1) * P], RSX[:, t * P:(t + 1) * P], ident[:, :])
            t4 = DV(lambda e: e.tensor_copy(CS, M[:, b, 0:T].rearrange("p (t n) -> p t n", t=2)[:, :, 0]),
                    pe_end(last), *toks)
            mb.put(b, [t4])
            return t3, t4

        def scaled(src, gname, g0, k, n, GH, toks, free):
            for i in range(n):
                t = DV(lambda e: e.tensor_scalar(GH[:, i, :], src[:, i, :], vc(gname, g0 + k + i), None,
                                                 ALU.mult), toks, free)
            return split_act(flat(AH[:, k:k + n, :]), flat(AL[:, k:k + n, :]), flat(GH[:, 0:n, :]), t)

        at = {}
        bank = {}

        def rms4():
            for k in range(0, 16, 4):
                while k + 3 not in at:
                    yield
                ta = [DV(lambda e: e.tensor_scalar(RES[:, i, :], RES[:, i, :], vc("lg", 16 + i),
                                                   vc("lb", 16 + i), ALU.mult, ALU.add), at[i])
                      for i in range(k, k + 4)]
                yield
                yield from rms_sum(k, 4, ta, SQ, bank, k == 0, k == 12, line=PL)
            tk["r5"], tk["c5"] = yield from rms_scale(RSK[:, :], CC[:, 0:2], bank)

        task(norm_in(at, normal, lambda k: GB[:, 0, k:k + 1], lambda k: GB[:, 1, k:k + 1], RES,
                     lambda c: GH[:, 2 * (c % 2):2 * (c % 2) + CHUNKS[c][1], :],
                     lambda c, h: h.get(c - 2), t_gb))
        task(rms4())
        tvb = []
        add_slot("y5", (flat(YH[:, 28:32, :]), flat(YL[:, 28:32, :])), (PE.sem, PE.n))
        s5 = {"vs0": None, "vs1": None, "ws": f4, "wr": None, "bs": f4, "z": None, "u": None}
        C5, R5 = CC[:, 0:2], RSK

        def ev_v(j, par, g, tok):
            while "c5" not in tk:
                yield
            for t in range(2):
                tv = AC(lambda e: e.activation(V[:, t, 512 * j:512 * j + 512], g[:, 512 * t:512 * t + 512],
                                               ACT.Gelu_apprx_tanh, scale=C5[:, t:t + 1]), tok, tk["c5"])
                tvb.append(tv)
                ts = DV(lambda e: e.tensor_tensor_reduce(
                    out=flat(U[:, 2 * t:2 * t + 2, :]),
                    in0=V[:, t, 512 * j:512 * j + 512], in1=V[:, t, 512 * j:512 * j + 512], scale=1.0,
                    scalar=0.0, op0=ALU.mult, op1=ALU.add, accum_out=VS5[:, t, j:j + 1]), tv, tk["c5"],
                    s5[f"vs{t}"])
                s5[f"vs{t}"] = ts
            release(par, tv)
            if j == 7:
                t1 = DV(lambda e: e.tensor_reduce(VR[:, :], VS5[:, :, :], AX.X, ALU.add), s5["vs0"], s5["vs1"])
                t2 = AC(lambda e: e.activation(VR[:, :], VR[:, :], ACT.Sqrt, scale=1.0 / 4096,
                                               bias=eps6[:, 0:1]), t1)
                tk["vr"] = DV(lambda e: e.reciprocal(VR[:, :], VR[:, :]), t2)
                s5["u"] = t1
            yield

        for j in range(8):
            now(ev_v(j, *gemm(B_v[j], (AH, AL), at, token_major=True)))
        yt = {}
        d_ws, d_bs = new_ds(), new_ds()

        def mix_w(j):
            while j > 0 and ("mixed", j - 1) not in tk:
                yield
            tw = dma(d_ws, WS[:, :, :], A["a_w_s_2"][0, 2 * j:2 * j + 2].rearrange("g t s -> t g s"), s5["ws"])
            tk[("bs", j)] = dma(d_bs, BS[:, :, :].rearrange("p g t -> p (g t)"),
                                A["a_b_s_2"][0, 2 * j:2 * j + 2].rearrange("g t -> (g t)")
                                .partition_broadcast(P), s5["bs"])
            yield
            yield
            b, rel = mb.get()
            PE.wait(rel, tw)
            for q in range(2):
                last = nc.tensor.transpose(M[:, b, q * P:(q + 1) * P], WS[:, q, :], ident[:, :])
            tp = pe_end(last)
            s5["ws"] = tp
            tm = DV(lambda e: e.tensor_tensor(WM[:, :, :], M[:, b, 0:T].rearrange("p (g t) -> p g t", g=2),
                                              brc(triu[:, 0:P], 2), ALU.mult), tp)
            mb.put(b, [tm])
            yield
            while "vr" not in tk:
                yield
            for n in range(2):
                tk[("wr", j)] = DV(lambda e: e.tensor_scalar(WR[:, n], WM[:, :, :], VR[:, n:n + 1], None,
                                                             ALU.mult), tm, tk["vr"], s5["wr"])

        def ev_u(j, par, g, tok):
            while not (("wr", j) in tk and "vr" in tk and (j == 0 or ("yt5", j - 1) in tk)):
                yield
            t0 = DV(lambda e: e.tensor_tensor(U[:, :, :], g.rearrange("p (a n) -> p a n", a=4),
                                              brc(R5[:, :], 4), ALU.mult), tok, s5["u"], tk["r5"])
            release(par, t0)
            yield
            tu = AC(lambda e: e.activation(flat(U[:, :, :]), flat(U[:, :, :]), ACT.Gelu_apprx_tanh), t0)
            yield
            uz = []
            for f in range(4):
                b, rel = mb.get()
                PE.wait(rel, tk[("wr", j)], tvb)
                c = 4 * j + f
                for n in range(2):
                    last = mm(M[:, b, n * P:(n + 1) * P], V[:, n, c * P:(c + 1) * P], WR[:, n, f // 2, :],
                              n == 0, True)
                tp = pe_end(last)
                s5["wr"] = tp
                m3 = M[:, b, 0:T].rearrange("p (n t) -> p n t", n=2)
                z3 = Z[:, f, :].rearrange("p (n t) -> p n t", n=2)
                tmx = DV(lambda e: e.scalar_tensor_tensor(out=z3, in0=m3, scalar=vc("vg", c),
                                                          in1=brc(BS[:, f // 2, :], 2), op0=ALU.mult,
                                                          op1=ALU.add), tp, tk[("bs", j)], s5["z"])
                mb.put(b, [tmx])
                uz.append(tmx)
                yield
            s5["bs"] = tmx
            t1 = DV(lambda e: e.tensor_tensor(Z[:, :, :], Z[:, :, :], U[:, :, :], ALU.mult), uz, tu)
            s5["u"] = t1
            tk[("mixed", j)] = t1

        def ev_z(j, par, g, tok):
            while ("mixed", j) not in tk:
                yield
            t0 = DV(lambda e: e.tensor_tensor(U[:, :, :], g.rearrange("p (a n) -> p a n", a=4),
                                              brc(R5[:, :], 4), ALU.mult), tok, s5["u"])
            release(par, t0)
            yield
            tz = AC(lambda e: e.activation(flat(U[:, :, :]), flat(U[:, :, :]), ACT.Silu), t0)
            yield
            ty = DV(lambda e: e.tensor_tensor(Z[:, :, :], Z[:, :, :], U[:, :, :], ALU.mult), tz,
                    tk[("mixed", j)])
            s5["u"] = ty
            yield
            toks = split_act(flat(YH[:, 4 * j:4 * j + 4, :]), flat(YL[:, 4 * j:4 * j + 4, :]),
                             flat(Z[:, :, :]), ty, slot_end["y5"] if j == 7 else None)
            s5["z"] = toks
            for f in range(4):
                yt[4 * j + f] = toks
            tk[("yt5", j)] = toks

        for j in range(8):
            task(mix_w(j))
            if j == 7:
                drop_slot("y5")
            now(ev_u(j, *gemm(B_uz[j][0], (AH, AL), at)))
            now(ev_z(j, *gemm(B_uz[j][1], (AH, AL), at)))
        res0 = gemm(B_o3[0][2], (YH, YL), yt)
        drain()
        f6 = fence()
        c5.close()

        c6 = ExitStack()
        RS7 = RSK
        c6b = ExitStack()
        SQ6 = sb("SQ6", [P, 4, T], F, c6b)
        GH6 = sb("GH6", [P, 4, T], F, c6b)
        for l in (AC, DV):
            l.wait(f6)
        at = {}
        s6 = {"gh": None}
        bank = {}

        def ev_o3(i, par, g, tok):
            k, n, _ = B_o3[i]
            while i > 0 and ("o3", i - 1) not in tk:
                yield
            r = flat(RES[:, k:k + n, :])
            t1 = DV(lambda e: e.tensor_tensor(r, r, g[:, 0:n * T], ALU.add), tok)
            release(par, t1)
            yield
            s6["gh"] = scaled(RES[:, k:k + n, :], "n2", 16, k, n, GH6, t1, s6["gh"])
            for f in range(n):
                at[k + f] = s6["gh"]
            tk[("o3", i)] = t1
            yield
            if i > 0:
                while ("sum", i - 1) not in tk:
                    yield
            yield from rms_sum(k, n, t1, SQ6, bank, i == 0, i == len(B_o3) - 1)
            tk[("sum", i)] = True
            if i == len(B_o3) - 1:
                tk["r7"], tk["c7"] = yield from rms_scale(RS7[:, :], CC[:, 2:4], bank)

        now(ev_o3(0, *res0))
        for i in range(1, len(B_o3)):
            now(ev_o3(i, *gemm(B_o3[i][2], (YH, YL), yt)))

        q0 = gemm(B_at[0][0], (AH, AL), at)
        drain()
        f7 = fence()
        c6b.close()
        c7 = ExitStack()
        Q7 = sb("Q7", [P, 4, T], F, c7)
        K7 = sb("K7", [P, 4, T], F, c7)
        V7 = sb("V7", [P, 2, 512], F, c7)
        Z7 = sb("Z7", [P, 4, T], F, c7)
        O7 = sb("O7", [P, 4, T], F, c7)
        ZMB = sb("ZMB", [P, 2, 384], F, c7)
        LSB = sb("LSB", [P, 2, 384], F, c7)
        SPB = sb("SPB", [P, 2, 384], F, c7)
        NM = sb("NM", [P, 384], F, c7)
        add_slot("x7", w_pair("x7", c7), f7)
        TG = sb("TG", [P, P], F, c7)
        HT = sb("HT", [P, 2, 512], F, c7)
        tn = PL(lambda e: e.memset(NM[:, :], 0.0), f7)
        for o in (0, 256):
            t_nm = PL(lambda e: e.affine_select(out=NM[:, o:o + P], in_=NM[:, o:o + P],
                                                compare_op=ALU.is_gt, fill=NEG, base=0,
                                                pattern=[[1, P]], channel_multiplier=-1), tn)
        tg = PL(lambda e: e.memset(TG[:, :], 1.0), f7)
        t_tg = PL(lambda e: e.affine_select(out=TG[:, :], in_=TG[:, :], compare_op=ALU.is_ge, fill=0.0,
                                            base=0, pattern=[[-1, P]], channel_multiplier=1), tg)
        yt = {}
        s7 = {"z": None, "ht": None}
        s7c = {"zm": None, "sp": None, "ls": None}

        def stick(j):
            while not (("v7", j) in tk and (j == 0 or ("s7", j - 1) in tk)):
                yield
            ZM, LS, SPX, s = flat(ZMB[:, :, :]), flat(LSB[:, :, :]), flat(SPB[:, :, :]), s7c
            ot = []
            for h0 in (0, 2):
                tz = []
                for c in range(2):
                    q, k = Q7[:, h0 + c, :], K7[:, h0 + c, :]
                    b, rel = mb.get()
                    PE.wait(rel, tk[("q7", j)], tk[("k7", j)])
                    mm(M[:, b, 0:T], k[:, 0:P], q[:, :], True, True)
                    tp = PE(lambda e: mm(M[:, b, T:384], k[:, P:T], q[:, P:T], False, True))
                    tz.append(DV(lambda e: e.scalar_tensor_tensor(
                        out=ZMB[:, c, :], in0=M[:, b, 0:384], scalar=SCALE, in1=NM[:, :], op0=ALU.mult,
                        op1=ALU.add), tp, t_nm, s["zm"], f7))
                    mb.put(b, [tz[-1]])
                t2 = DV(lambda e: e.scalar_tensor_tensor(out=LS, in0=ZM, scalar=-1.0, in1=ZM, op0=ALU.mult,
                                                         op1=ALU.max), tz, s["ls"], f7)
                yield
                t3 = AC(lambda e: e.activation(LS, LS, ACT.Exp, scale=-1.0), t2)
                yield
                t4 = AC(lambda e: e.activation(LS, LS, ACT.Ln, bias=1.0), t3)
                yield
                t5 = DV(lambda e: e.scalar_tensor_tensor(out=SPX, in0=ZM, scalar=0.0, in1=LS, op0=ALU.max,
                                                         op1=ALU.add), t4, s["sp"], f7)
                yield 2
                t6 = []
                for c in range(2):
                    b, rel = mb.get()
                    PE.wait(rel, t5, t_tg)
                    mm(M[:, b, 0:T], TG[:, :], SPB[:, c, 0:T], True, False)
                    mm(M[:, b, P:T], ones[:, :], SPB[:, c, T:384], False, True)
                    tp = PE(lambda e: mm(M[:, b, T:384], TG[:, :], SPB[:, c, T:384], False, True))
                    t6.append(DV(lambda e: e.tensor_tensor(ZMB[:, c, :], ZMB[:, c, :], M[:, b, 0:384],
                                                           ALU.subtract), tp))
                    mb.put(b, [t6[-1]])
                s["sp"] = tp
                yield
                t7 = AC(lambda e: e.activation(LS, ZM, ACT.Exp), t6, t5)
                s["zm"] = t7
                yield 2
                for c in range(2):
                    h = h0 + c
                    b, rel = mb.get()
                    PE.wait(rel, t7, tk[("v7", j)])
                    mm(M[:, b, 0:T], V7[:, 0, h * P:(h + 1) * P], LSB[:, c, 0:T], True, False)
                    tp = PE(lambda e: mm(M[:, b, P:T], V7[:, 1, h * P:(h + 1) * P], LSB[:, c, T:384],
                                         False, True))
                    while j > 0 and ("o7", j - 1) not in tk:
                        yield
                    ot.append(AC(lambda e: e.copy(O7[:, h, :], M[:, b, 0:T]), tp, tk.get(("o7", j - 1)), f7))
                    mb.put(b, [ot[-1]])
                s["ls"] = tp
                yield
            tk[("s7", j)] = [tp, ot]

        def gated7(j):
            while not (("s7", j) in tk and ("z7", j) in tk):
                yield
            t1 = DV(lambda e: e.tensor_tensor(O7[:, :, :], O7[:, :, :], Z7[:, :, :], ALU.mult),
                    tk[("z7", j)], tk[("s7", j)])
            s7["z"] = t1
            yield
            toks = split_act(flat(YH[:, 4 * j:4 * j + 4, :]), flat(YL[:, 4 * j:4 * j + 4, :]),
                             flat(O7[:, :, :]), t1)
            for f in range(4):
                yt[4 * j + f] = toks
            tk[("o7", j)] = toks

        def ev7(name, j, dst, par, g, tok):
            while j > 0 and ("s7", j - 1) not in tk:
                yield
            free = tk.get(("s7", j - 1))
            if name == "v7":
                for t in range(2):
                    t1 = DV(lambda e: e.tensor_scalar(dst[:, t, :], g[:, 512 * t:512 * t + 512],
                                                      CC[:, 2 + t:3 + t], None, ALU.mult), tok, free, f7,
                            tk["c7"])
            else:
                t1 = DV(lambda e: e.tensor_tensor(dst, g.rearrange("p (a n) -> p a n", a=4),
                                                  brc(RS7[:, :], 4), ALU.mult), tok, free, f7, tk["r7"])
            release(par, t1)
            tk[(name, j)] = t1

        def ev7z(j, par, g, tok):
            while j > 0 and ("o7", j - 1) not in tk:
                yield
            t1 = DV(lambda e: e.tensor_tensor(Z7[:, :, :], g.rearrange("p (a n) -> p a n", a=4),
                                              brc(RS7[:, :], 4), ALU.mult), tok, f7, tk["r7"], s7["z"])
            release(par, t1)
            yield
            tk[("z7", j)] = AC(lambda e: e.activation(flat(Z7[:, :, :]), flat(Z7[:, :, :]), ACT.Silu), t1)

        d_ht = new_ds()

        OUT = flat(RES[:, :, :]).rearrange("p (t n) -> p t n", t=2)

        def turn_h():
            for j in range(4):
                for t in range(2):
                    b, rel = mb.get()
                    PE.wait(rel)
                    for f in range(4):
                        last = nc.tensor.transpose(M[:, b, f * P:(f + 1) * P],
                                                   RES[:, 4 * j + f, t * P:(t + 1) * P], ident[:, :])
                    tc = DV(lambda e: e.tensor_copy(HT[:, t, :], M[:, b, :]), pe_end(last), s7["ht"], f7)
                    mb.put(b, [tc])
                    yield
                s7["ht"] = dma(d_ht, h2_d[:, j, :, :].rearrange("t p n -> p t n"), HT[:, :, :], tc)
            tk["out"] = dma(new_ds(), OUT.rearrange("p t (j n) -> p t j n", j=4),
                            h2_d[:, :, :, :].rearrange("t j p n -> p t j n"), (PE.sem, PE.n), s7["ht"])

        for j in range(4):
            if j == 0:
                now(ev7("q7", 0, Q7[:, :, :], *q0))
            else:
                now(ev7("q7", j, Q7[:, :, :], *gemm(B_at[j][0], (AH, AL), at)))
            now(ev7("k7", j, K7[:, :, :], *gemm(B_at[j][1], (AH, AL), at)))
            now(ev7("v7", j, V7[:, :, :], *gemm(B_at[j][2], (AH, AL), at, token_major=True)))
            task(stick(j))
            task(gated7(j))
            if j == 0:
                task(turn_h())
            now(ev7z(j, *gemm(B_at[j][3], (AH, AL), at)))
        drop_slot("x7")
        jobs = []
        for i in range(2):
            jobs.append(gemm_open(B_o4[i]))
            gemm_run(jobs[i], (YH, YL), yt, token_major=True, n=6)
        res0 = gemm_run(jobs[0], (YH, YL), yt, token_major=True)
        drain()
        f8 = fence()
        c7.close()

        c8 = ExitStack()
        FG = sb("FG8", [P, DM], F, c8)
        TT = sb("TT8", [P, 512], F, c8)
        SS = sb("SS8", [P, 2, 5], F, c8)
        RR = sb("RR8", [P, 2], F, c8)
        t_fg = dma(new_ds(), FG[:, :], A["final_g_2"].partition_broadcast(P), f8)
        t_o = tk["out"]
        tsq = [None, None]

        t_sq = AC(lambda e: e.activation(RR[:, :], eps6[:, :], ACT.Sqrt), f8)
        tf = [None, None]

        def ev_o(j, par, g, tok):
            c, w = OUTS[j]
            for t in range(2):
                o = OUT[:, t, c:c + w]
                tc = DV(lambda e: e.tensor_tensor(o, o, g[:, 512 * t:512 * t + w], ALU.add), tok, t_o)
                tsq[t] = DV(lambda e: e.tensor_tensor_reduce(
                    out=TT[:, 0:w], in0=o, in1=o, scale=1.0, scalar=0.0, op0=ALU.mult, op1=ALU.add,
                    accum_out=SS[:, t, j:j + 1]), tc, tsq, f8)
            release(par, tc)
            for t in range(2):
                o = OUT[:, t, c:c + w]
                tf[t] = PL(lambda e: e.tensor_tensor(o, o, FG[:, c:c + w], ALU.mult), tsq[t], t_fg)
            yield

        now(ev_o(0, *res0))
        now(ev_o(1, *gemm_run(jobs[1], (YH, YL), yt, token_major=True)))
        for j in range(2, 5):
            now(ev_o(j, *gemm(B_o4[j], (YH, YL), yt, token_major=True)))
        drain()
        d_o = new_ds()
        t1 = DV(lambda e: e.tensor_reduce(RR[:, :], SS[:, :, :], AX.X, ALU.add), tsq, t_sq)
        t2 = AC(lambda e: e.activation(RR[:, :], RR[:, :], ACT.Sqrt, scale=1.0 / DM, bias=eps6[:, 0:1]), t1)
        t3 = DV(lambda e: e.reciprocal(RR[:, :], RR[:, :]), t2)
        for q in range(2):
            o = [OUT[:, t, 1024 * q:1024 * q + 1024] for t in range(2)]
            t4 = [DV(lambda e: e.tensor_scalar(o[0], o[0], RR[:, 0:1], None, ALU.mult), t3, tf),
                  AC(lambda e: e.activation(o[1], o[1], ACT.Copy, scale=RR[:, 1:2]), t3, tf)]
            for t in range(2):
                t5 = dma(d_o, out[0, t * P:(t + 1) * P, 1024 * q:1024 * q + 1024], o[t], t4[t])
        SP.wait(t5)
        SP.wait(tk["csd"], s7["ht"])
        c8.close()
        c6.close()
        c4.close()
        cy.close()


_INS = ['x', 'ssd_w_in', 'ssd_conv_w', 'ssd_conv_b', 'ssd_dt_bias', 'ssd_a_log', 'ssd_d_skip',
        'ssd_norm_g', 'ssd_w_out', 'dsa_w_in', 'dsa_q_norm_g', 'dsa_kv_norm_g', 'dsa_w_uq', 'dsa_w_uk',
        'dsa_w_uv', 'dsa_w_idx_q', 'dsa_w_out', 'ln_g', 'ln_b', 'norm_g_2', 'a_w_in_2', 'a_v_norm_g_2',
        'a_w_s_2', 'a_b_s_2', 'a_w_out_2', 'b_w_in_2', 'b_w_out_2', 'final_g_2']


def kernel(**inputs):
    import numpy as _np
    import concourse.bacc as _bacc
    from concourse import mybir as _mybir
    from concourse.bass_utils import run_bass_kernel_spmd as _run

    nc = _bacc.Bacc("TRN2", target_bir_lowering=False, num_devices=1)
    arrays, args = {}, {}
    for name in _INS:
        a = _np.ascontiguousarray(inputs[name])
        arrays[f"in_{name}"] = a
        args[name] = nc.dram_tensor(f"in_{name}", a.shape, _mybir.dt.from_np(a.dtype), kind="ExternalInput").ap()
    out = nc.dram_tensor("out_0", (1, 256, 2048), _mybir.dt.float32, kind="ExternalOutput").ap()
    build(nc, args, out)
    r = _run(nc, [arrays], core_ids=[0])
    return r.results[0]["out_0"]
```
